# Optimizing a Trainium2 kernel written in Bass

```python
import jax, jax.numpy as jnp
from jax import lax
import numpy as np

D_MODEL = 1024
BATCH = 1
SEQ = 512
DEPTH = 2
DEC_BATCH = 8
DEC_SEQ = 1
PAST_LEN = 4096
PAGE_SIZE = 128

N_MIXERS = 2
N_RET_LAYERS = (DEPTH + 1) // 2
N_SSM_LAYERS = DEPTH // 2

RET_HEADS = 4
RET_DK = D_MODEL // RET_HEADS
RET_DV = 2 * RET_DK
RET_CHUNK = 128
RET_IN = RET_HEADS * (2 * RET_DK + 2 * RET_DV)
ROPE_BASE = 10000.0

SSM_GROUP = 16
SSM_GROUPS = D_MODEL // SSM_GROUP
SSM_STATE = 64
DT_MIN = 1e-3
DT_MAX = 1e-1

PEER_HEADS = 8
PEER_NKEYS = 128
PEER_EXPERTS = PEER_NKEYS * PEER_NKEYS
PEER_DQ = 256
PEER_TOPK = 16
PEER_BLOCK = 128

EPS = 1e-6

kernel_name = "retention_s5_peer_hybrid_step"

def rmsnorm(x, g):
    xf = x.astype(jnp.float32)
    y = xf * lax.rsqrt(jnp.mean(xf * xf, axis=-1, keepdims=True) + EPS)
    return (y * g.astype(jnp.float32)).astype(x.dtype)

def modulate(h, shift, scale):
    return h * (1 + scale[:, None, :]) + shift[:, None, :]

def rotary(x, pos):
    half = x.shape[-1] // 2
    inv = ROPE_BASE ** (-jnp.arange(half, dtype=jnp.float32) / half)
    ang = pos.astype(jnp.float32)[:, None] * inv[None, :]
    cos = jnp.cos(ang)[None, :, None, :]
    sin = jnp.sin(ang)[None, :, None, :]
    x1 = x[..., :half].astype(jnp.float32)
    x2 = x[..., half:].astype(jnp.float32)
    return jnp.concatenate([x1 * cos - x2 * sin, x2 * cos + x1 * sin], axis=-1).astype(x.dtype)

def retention_scan(q, k, v, s0):
    B, S, H, _ = q.shape
    L = RET_CHUNK if S % RET_CHUNK == 0 else S
    nc = S // L
    lg = jnp.log1p(-jnp.exp2(-5.0 - jnp.arange(H, dtype=jnp.float32)))
    i = jnp.arange(L, dtype=jnp.float32)
    diff = i[:, None] - i[None, :]
    dmask = jnp.where(diff >= 0, jnp.exp(lg[:, None, None] * jnp.maximum(diff, 0.0)), 0.0)
    cross = jnp.exp(lg[:, None] * (i[None, :] + 1.0))[None, :, :, None]
    tail = jnp.exp(lg[:, None] * (L - 1.0 - i[None, :]))[None, :, :, None]
    chunk_decay = jnp.exp(lg * L)[None, :, None, None]

    def to_chunks(t):
        return t.reshape(B, nc, L, H, t.shape[-1]).transpose(1, 0, 3, 2, 4).astype(jnp.float32)

    def step(s, qkv):
        qc, kc, vc = qkv
        att = jnp.einsum('bhid,bhjd->bhij', qc, kc) * dmask
        o = jnp.einsum('bhij,bhjv->bhiv', att, vc) + jnp.einsum('bhid,bhdv->bhiv', qc, s) * cross
        s = s * chunk_decay + jnp.einsum('bhjd,bhjv->bhdv', kc * tail, vc)
        return s, o

    s, o = lax.scan(step, s0.astype(jnp.float32), (to_chunks(q), to_chunks(k), to_chunks(v)))
    o = o.transpose(1, 0, 3, 2, 4).reshape(B, S, H, -1)
    return o, s

def retention_mixer(h, pos, s0, w_in, w_out):
    B, S, _ = h.shape
    proj = h @ w_in
    nq = RET_HEADS * RET_DK
    nv = RET_HEADS * RET_DV
    q, k, v, g = jnp.split(proj, [nq, 2 * nq, 2 * nq + nv], axis=-1)
    q = rotary(q.reshape(B, S, RET_HEADS, RET_DK), pos)
    k = rotary(k.reshape(B, S, RET_HEADS, RET_DK), pos) * (RET_DK ** -0.5)
    v = v.reshape(B, S, RET_HEADS, RET_DV)
    o, s = retention_scan(q, k, v, s0)
    mu = jnp.mean(o, axis=-1, keepdims=True)
    var = jnp.mean(jnp.square(o - mu), axis=-1, keepdims=True)
    o = ((o - mu) * lax.rsqrt(var + EPS)).reshape(B, S, RET_HEADS * RET_DV).astype(h.dtype)
    return (jax.nn.silu(g) * o) @ w_out, s

def ssm_discretize(lam_re, lam_im, log_dt, b_re, b_im):
    dt = jnp.exp(log_dt.astype(jnp.float32))[:, None]
    lr = lam_re.astype(jnp.float32)
    li = lam_im.astype(jnp.float32)
    mag = jnp.exp(lr * dt)
    a_re = mag * jnp.cos(li * dt)
    a_im = mag * jnp.sin(li * dt)
    den = lr * lr + li * li
    nr = a_re - 1.0
    c_re = ((nr * lr + a_im * li) / den)[..., None]
    c_im = ((a_im * lr - nr * li) / den)[..., None]
    br = b_re.astype(jnp.float32)
    bi = b_im.astype(jnp.float32)
    return a_re, a_im, c_re * br - c_im * bi, c_re * bi + c_im * br

def ssm_scan(u, h0_re, h0_im, a_re, a_im, bb_re, bb_im):
    bu_re = jnp.einsum('bsgp,gnp->bsgn', u, bb_re)
    bu_im = jnp.einsum('bsgp,gnp->bsgn', u, bb_im)
    h0r = h0_re.astype(jnp.float32)
    h0i = h0_im.astype(jnp.float32)
    bu_re = bu_re.at[:, 0].add(a_re * h0r - a_im * h0i)
    bu_im = bu_im.at[:, 0].add(a_re * h0i + a_im * h0r)
    A_re = jnp.broadcast_to(a_re, bu_re.shape)
    A_im = jnp.broadcast_to(a_im, bu_im.shape)

    def combine(e1, e2):
        ar1, ai1, br1, bi1 = e1
        ar2, ai2, br2, bi2 = e2
        return (ar2 * ar1 - ai2 * ai1, ar2 * ai1 + ai2 * ar1,
                ar2 * br1 - ai2 * bi1 + br2, ar2 * bi1 + ai2 * br1 + bi2)

    _, _, h_re, h_im = lax.associative_scan(combine, (A_re, A_im, bu_re, bu_im), axis=1)
    return h_re, h_im

def ssm_mixer(h, h0_re, h0_im, w_in, lam_re, lam_im, log_dt, b_re, b_im, c_re, c_im, d_skip, w_glu):
    B, S, D = h.shape
    u = (h @ w_in).astype(jnp.float32).reshape(B, S, SSM_GROUPS, SSM_GROUP)
    a_re, a_im, bb_re, bb_im = ssm_discretize(lam_re, lam_im, log_dt, b_re, b_im)
    hs_re, hs_im = ssm_scan(u, h0_re, h0_im, a_re, a_im, bb_re, bb_im)
    y = (jnp.einsum('bsgn,gpn->bsgp', hs_re, c_re.astype(jnp.float32))
         - jnp.einsum('bsgn,gpn->bsgp', hs_im, c_im.astype(jnp.float32))
         + d_skip.astype(jnp.float32) * u)
    z = jax.nn.gelu(y.reshape(B, S, D)).astype(h.dtype)
    a, gt = jnp.split(z @ w_glu, 2, axis=-1)
    return a * jax.nn.sigmoid(gt), hs_re[:, -1], hs_im[:, -1]

def peer_block(xb, w_q, key1, key2, u_tab, v_tab):
    T = xb.shape[0]
    q = (xb @ w_q).astype(jnp.float32).reshape(T, PEER_HEADS, 2, PEER_DQ // 2)
    s1 = jnp.einsum('thd,hkd->thk', q[:, :, 0], key1.astype(jnp.float32))
    s2 = jnp.einsum('thd,hkd->thk', q[:, :, 1], key2.astype(jnp.float32))
    v1, i1 = lax.top_k(s1, PEER_TOPK)
    v2, i2 = lax.top_k(s2, PEER_TOPK)
    cand = (v1[..., :, None] + v2[..., None, :]).reshape(T, PEER_HEADS, PEER_TOPK * PEER_TOPK)
    cidx = (i1[..., :, None] * PEER_NKEYS + i2[..., None, :]).reshape(T, PEER_HEADS, PEER_TOPK * PEER_TOPK)
    top, sel = lax.top_k(cand, PEER_TOPK)
    eidx = jnp.take_along_axis(cidx, sel, axis=-1)
    gate = jax.nn.softmax(top, axis=-1)
    u = jnp.take(u_tab, eidx, axis=0)
    act = jax.nn.gelu(jnp.einsum('thkd,td->thk', u, xb).astype(jnp.float32))
    w = (gate * act).astype(xb.dtype)
    v = jnp.take(v_tab, eidx, axis=0)
    return jnp.einsum('thk,thkd->td', w, v)

def peer(x, w_q, key1, key2, u_tab, v_tab):
    B, S, D = x.shape
    T = B * S
    nb = -(-T // PEER_BLOCK)
    xf = jnp.pad(x.reshape(T, D), ((0, nb * PEER_BLOCK - T), (0, 0)))
    out = lax.map(lambda xb: peer_block(xb, w_q, key1, key2, u_tab, v_tab), xf.reshape(nb, PEER_BLOCK, D))
    return out.reshape(nb * PEER_BLOCK, D)[:T].reshape(B, S, D)

def setup_inputs(seed: int = 0) -> dict:
    key = jax.random.key(seed)
    ks = jax.random.split(key, 32)
    f32 = jnp.float32
    D = D_MODEL
    nrm = lambda k, shape, s: jax.random.normal(k, shape, f32) * s
    n_idx = jnp.arange(SSM_STATE, dtype=f32)
    return {
        "x_prompt": nrm(ks[0], (BATCH, SEQ, D), 1.0),
        "x_sample": nrm(ks[1], (DEC_BATCH, DEC_SEQ, D), 1.0),
        "c_prompt": nrm(ks[2], (BATCH, D), 1.0),
        "c_sample": nrm(ks[3], (DEC_BATCH, D), 1.0),
        "state_ret": nrm(ks[4], (N_RET_LAYERS, DEC_BATCH, RET_HEADS, RET_DK, RET_DV), 0.3),
        "state_ssm_re": nrm(ks[5], (N_SSM_LAYERS, DEC_BATCH, SSM_GROUPS, SSM_STATE), 0.5),
        "state_ssm_im": nrm(ks[6], (N_SSM_LAYERS, DEC_BATCH, SSM_GROUPS, SSM_STATE), 0.5),
        "norm_g": 1.0 + nrm(ks[7], (DEPTH, 2, D), 0.01),
        "final_g": 1.0 + nrm(ks[8], (D,), 0.01),
        "w_ada": nrm(ks[9], (DEPTH, D, 6 * D), 0.5 * D ** -0.5),
        "b_ada": nrm(ks[10], (DEPTH, 6 * D), 0.02),
        "ret_w_in": nrm(ks[11], (N_RET_LAYERS, D, RET_IN), D ** -0.5),
        "ret_w_out": nrm(ks[12], (N_RET_LAYERS, RET_HEADS * RET_DV, D), (RET_HEADS * RET_DV) ** -0.5),
        "ssm_w_in": nrm(ks[13], (N_SSM_LAYERS, D, D), D ** -0.5),
        "ssm_lam_re": -0.5 + nrm(ks[14], (N_SSM_LAYERS, SSM_GROUPS, SSM_STATE), 0.01),
        "ssm_lam_im": jnp.pi * n_idx + nrm(ks[15], (N_SSM_LAYERS, SSM_GROUPS, SSM_STATE), 0.01),
        "ssm_log_dt": jax.random.uniform(ks[16], (N_SSM_LAYERS, SSM_GROUPS), f32, float(np.log(DT_MIN)), float(np.log(DT_MAX))),
        "ssm_b_re": nrm(ks[17], (N_SSM_LAYERS, SSM_GROUPS, SSM_STATE, SSM_GROUP), (2 * SSM_GROUP) ** -0.5),
        "ssm_b_im": nrm(ks[18], (N_SSM_LAYERS, SSM_GROUPS, SSM_STATE, SSM_GROUP), (2 * SSM_GROUP) ** -0.5),
        "ssm_c_re": nrm(ks[19], (N_SSM_LAYERS, SSM_GROUPS, SSM_GROUP, SSM_STATE), (2 * SSM_STATE) ** -0.5),
        "ssm_c_im": nrm(ks[20], (N_SSM_LAYERS, SSM_GROUPS, SSM_GROUP, SSM_STATE), (2 * SSM_STATE) ** -0.5),
        "ssm_d": nrm(ks[21], (N_SSM_LAYERS, SSM_GROUPS, SSM_GROUP), 1.0),
        "ssm_w_glu": nrm(ks[22], (N_SSM_LAYERS, D, 2 * D), D ** -0.5),
        "peer_w_q": nrm(ks[23], (DEPTH, D, PEER_HEADS * PEER_DQ), D ** -0.5),
        "peer_key1": nrm(ks[24], (DEPTH, PEER_HEADS, PEER_NKEYS, PEER_DQ // 2), (PEER_DQ // 2) ** -0.5),
        "peer_key2": nrm(ks[25], (DEPTH, PEER_HEADS, PEER_NKEYS, PEER_DQ // 2), (PEER_DQ // 2) ** -0.5),
        "peer_u": nrm(ks[26], (DEPTH, PEER_EXPERTS, D), D ** -0.5),
        "peer_v": nrm(ks[27], (DEPTH, PEER_EXPERTS, D), PEER_HEADS ** -0.5),
    }

def reference(x_prompt, x_sample, c_prompt, c_sample, state_ret, state_ssm_re, state_ssm_im,
              norm_g, final_g, w_ada, b_ada, ret_w_in, ret_w_out,
              ssm_w_in, ssm_lam_re, ssm_lam_im, ssm_log_dt, ssm_b_re, ssm_b_im, ssm_c_re, ssm_c_im, ssm_d, ssm_w_glu,
              peer_w_q, peer_key1, peer_key2, peer_u, peer_v):

    def run(x, c, pos, ret_s0, ssm_re0, ssm_im0):
        new_ret, new_re, new_im = [], [], []
        for i in range(DEPTH):
            mod = jax.nn.silu(c) @ w_ada[i] + b_ada[i]
            sh1, sc1, g1, sh2, sc2, g2 = jnp.split(mod, 6, axis=-1)
            h = modulate(rmsnorm(x, norm_g[i, 0]), sh1, sc1)
            j = i // N_MIXERS
            if i % N_MIXERS == 0:
                y, s = retention_mixer(h, pos, ret_s0[j], ret_w_in[j], ret_w_out[j])
                new_ret.append(s.astype(x.dtype))
            else:
                y, hr, hi = ssm_mixer(h, ssm_re0[j], ssm_im0[j], ssm_w_in[j], ssm_lam_re[j], ssm_lam_im[j],
                                      ssm_log_dt[j], ssm_b_re[j], ssm_b_im[j], ssm_c_re[j], ssm_c_im[j],
                                      ssm_d[j], ssm_w_glu[j])
                new_re.append(hr.astype(x.dtype))
                new_im.append(hi.astype(x.dtype))
            x = x + g1[:, None, :] * y
            h = modulate(rmsnorm(x, norm_g[i, 1]), sh2, sc2)
            x = x + g2[:, None, :] * peer(h, peer_w_q[i], peer_key1[i], peer_key2[i], peer_u[i], peer_v[i])
        return rmsnorm(x, final_g), jnp.stack(new_ret), jnp.stack(new_re), jnp.stack(new_im)

    B = x_prompt.shape[0]
    dt = x_prompt.dtype
    pos_p = jnp.arange(x_prompt.shape[1], dtype=jnp.int32)
    pos_s = PAST_LEN + jnp.arange(x_sample.shape[1], dtype=jnp.int32)
    ret0_p = jnp.zeros((N_RET_LAYERS, B, RET_HEADS, RET_DK, RET_DV), dt)
    ssm0_p = jnp.zeros((N_SSM_LAYERS, B, SSM_GROUPS, SSM_STATE), dt)
    y_prompt, ret_prompt, ssm_re_prompt, ssm_im_prompt = run(x_prompt, c_prompt, pos_p, ret0_p, ssm0_p, ssm0_p)
    y_sample, ret_sample, ssm_re_sample, ssm_im_sample = run(x_sample, c_sample, pos_s, state_ret, state_ssm_re, state_ssm_im)
    return (y_prompt, y_sample, ret_prompt, ret_sample, ssm_re_prompt, ssm_im_prompt, ssm_re_sample, ssm_im_sample)


_drawn_inputs = setup_inputs


def setup_inputs(seed=0):
    import zlib

    import numpy as np

    out = dict(_drawn_inputs(seed))
    spreads = {}
    factors = {'norm_g': 5.55, 'final_g': 5.936, 'ssm_lam_re': 3.15}
    for name, (base, spread) in spreads.items():
        noise = np.random.default_rng([zlib.crc32(name.encode()), seed]).standard_normal(out[name].shape)
        drawn = base * np.exp(spread * noise) if base else spread * noise
        out[name] = __import__('jax').numpy.asarray(drawn.astype(out[name].dtype))
    for name, factor in factors.items():
        out[name] = (out[name] * factor).astype(out[name].dtype)
    return out
```

```python
from contextlib import ExitStack

import concourse.bass as bass
from concourse import mybir

F32 = mybir.dt.float32
U32 = mybir.dt.uint32
I32 = mybir.dt.int32
ALU = mybir.AluOpType
ACT = mybir.ActivationFunctionType
AX = mybir.AxisListType

D = 1024
P = 128
KC = D // P
TP = 4
NS = 8
TILES = TP + 1
NTOK = TP * P + NS
ROWS = [P] * TP + [NS]
NC = NS + 1
LAYERS = 2
BW = 512
HEADS, DK, DV = 4, 256, 512
PH, NK, TOPK = 8, 128, 16
NE = PH * TOPK
EXPERTS = NK * NK
RING = 8
BATCH = 2 * RING
G, GP, NST = 64, 16, 64
BL = 8
NB = TP * P // BL
PAIRS = G // 2
EPS = 1e-6
LOWEST = -3.0e38
ADA_BLOCKS = LAYERS * 6 * D // BW
HEAD_BLOCKS = 4
W_HEADS = ADA_BLOCKS
W_PEER = [W_HEADS + HEADS * HEAD_BLOCKS, W_HEADS + HEADS * HEAD_BLOCKS + 4 + 2 + 4]
W_SSM = W_PEER[0] + 4
W_GLU = W_SSM + 2
GELU_A, GELU_C = 0.044715, 0.7978845608028654


class Steps:

    def __init__(self, eng, sem):
        self.eng, self.sem, self.n, self.i, self.per = eng, sem, 0, None, 0

    def link(self, ins):
        ins.then_inc(self.sem, 1)
        self.n += 1
        self.eng.wait_ge(self.sem, self.value())

    def value(self):
        return self.n if self.i is None else self.i * self.per + self.n

    def loop(self, i, per):
        self.i, self.per, self.start = i, per, self.n

    def end(self, times):
        assert self.n - self.start == self.per, (self.n - self.start, self.per)
        self.n, self.i = self.start + times * self.per, None
HEAD_LINKS = 12
FINAL = 2 * LAYERS
NORMS = FINAL + 1 + HEADS
PEER_ROOT = [2 + HEADS, NORMS - 1]
TURN = [0, 1, 2, 4, 5]


class Cut:

    def __init__(self, whole, at=0):
        self.whole, self.at = whole, at

    def __call__(self, *shape, dtype=F32):
        n = 1
        for s in shape:
            n *= s
        view = self.whole[:, self.at:self.at + n]
        self.at += n
        assert self.at <= self.whole.shape[1], self.at
        if dtype != F32:
            view = view.bitcast(dtype)
        names = "abcd"[:len(shape)]
        if len(shape) > 1:
            view = view.rearrange(f"p ({' '.join(names)}) -> p {' '.join(names)}", **dict(zip(names, shape)))
        return view


def spread(ap, axis, n):
    shape = list(ap.shape)
    shape.insert(axis, n)
    return ap.unsqueeze(axis).to_broadcast(shape)


def build(nc, x_prompt, x_sample, c_prompt, c_sample, state_ret, state_ssm_re, state_ssm_im,
          norm_g, final_g, w_ada, b_ada, ret_w_in, ret_w_out, ssm_w_in, ssm_lam_re, ssm_lam_im, ssm_log_dt,
          ssm_b_re, ssm_b_im, ssm_c_re, ssm_c_im, ssm_d, ssm_w_glu, peer_w_q, peer_key1, peer_key2, peer_u, peer_v,
          rot_tab, decay_tab, decay_cols, lane_tab,
          y_prompt, y_sample, ret_prompt, ret_sample, re_prompt, im_prompt, re_sample, im_sample):
    with ExitStack() as ctx:
        def sb(name, shape, dtype=F32):
            return ctx.enter_context(nc.sbuf_tensor(name, shape, dtype))

        def sem(name):
            return ctx.enter_context(nc.semaphore(name))

        mod_d = nc.dram_tensor("mod_d", (NC, LAYERS * 6 * D), F32).ap()
        hs_d = nc.dram_tensor("hs_d", (LAYERS, NS, D), F32).ap()
        u_d = nc.dram_tensor("u_d", (TP * P + NS, D), F32).ap()
        z_d = nc.dram_tensor("z_d", (TP * P + NS, D), F32).ap()
        k_d = nc.dram_tensor("k_d", (G, GP, 2 * BL - 1, GP), F32).ap()

        x = sb("x", [P, TILES, D])
        h = sb("h", [P, TILES, D])
        hT = sb("hT", [P, KC, NTOK])
        modp = sb("modp", [P, 3, D])
        mods = sb("mods", [P, 3, D])
        w = sb("w", [P, 2, KC * BW])
        ident = sb("ident", [P, P])
        zeros = sb("zeros", [P, P])
        sq = sb("sq", [P, TILES])
        var = sb("var", [P, TILES])
        rstd = sb("rstd", [P, TILES])
        mhalf = sb("mhalf", [P, TILES])
        lane = sb("lane", [P, TOPK])
        arena = sb("arena", [P, 24064])
        ps = ctx.enter_context(nc.psum_tensor("ps", [P, 8, BW], F32))

        gain = arena[:, 0:D]

        cut = Cut(arena)
        bias = cut(LAYERS * 6 * D)[0:NC]
        cut = Cut(arena, LAYERS * 6 * D)
        cond, cond_t = cut(D)[0:NC], cut(D)[0:NC]
        condT = cut(KC, NC)
        cut = Cut(arena)
        proj = cut(TILES, 3 * BW)
        qkr = cut(TILES, 2, DK)
        qkT = cut(TP, 4, P)
        cut.at -= TP * 4 * P
        oT = cut(4, NTOK)
        qz = cut(2, NS * NS)
        state = cut(2, DV)
        kt = cut(TP, DK)
        kz = cut(NS, DK)[0:NS]
        sring = cut(2, 2, DV)
        att = cut(2, P)
        cross = cut(2, DV)
        mask = cut(P)
        cols = cut(4)
        stats = cut(TILES, 6)
        meanv = cut(TILES, 2)
        masks = cut(HEADS, P)
        colss = cut(HEADS, 4)
        rots = cut(TILES, 2, 2, P)
        cut = Cut(h[:, :, :].rearrange("p t n -> p (t n)"))
        o = cut(TILES, DV)
        sil = cut(TILES, DV)
        rot1 = o[:, 0:4, :].rearrange("p t (a n) -> p t a n", a=4)
        rot2 = sil[:, 0:4, :].rearrange("p t (a n) -> p t a n", a=4)
        cut = Cut(arena)
        u_ring = cut(RING, D)
        cut.at = 0
        qT = cut(2 * PH, NTOK)
        v_ring = cut(RING, D)
        cut.at -= RING * D
        keys = cut(2 * PH, P)
        keyT = cut(2 * PH, P)
        score = cut(2 * PH, NK)
        score2 = cut(2 * PH, NK)
        cand = cut(PH, TOPK * TOPK)
        cand2 = cut(PH, TOPK * TOPK)
        cut.at -= 2 * PH * TOPK * TOPK
        hb = cut(2, D)
        gated = cut(2, BW)
        acts = cut(NE)
        acts2 = cut(NE)
        wgt = cut(2, NE)
        diag = cut(4, P)
        best = cut(2 * PH, TOPK)
        besti = cut(2 * PH, TOPK, dtype=U32)
        bestf = cut(2 * PH, TOPK)
        topv = cut(PH, TOPK)
        topi = cut(PH, TOPK, dtype=U32)
        place = cut(NE)
        place_s = cut(NE)
        side1 = cut(NE)
        side2 = cut(NE)
        total = cut(PH)
        rtotal = cut(PH)
        eidx = cut(TILES, NE, dtype=U32)
        gate = cut(TILES, NE)
        eidx_s = cut(NS, dtype=U32)
        gate_s = cut(NS)
        stage_u = cut(2, RING, dtype=U32)
        stage_v = cut(2, RING, dtype=U32)
        dots = cut(BATCH)
        acts_s = cut(NS)
        acts_s2 = cut(NS)
        wgt_s = cut(NS * NS)

        x_ld, c_ld, tab_ld, mod_ld, fin_ld = sem("x_ld"), sem("c_ld"), sem("tab_ld"), sem("mod_ld"), sem("fin_ld")
        w_ld = [sem("w_ld0"), sem("w_ld1")]
        w_used = sem("w_used")
        consts, constv = sem("consts"), sem("constv")
        x_ready, sq_done, var_done, rstd_done = sem("x_ready"), sem("sq_done"), sem("var_done"), sem("rstd_done")
        h_done, hT_ps, hT_done = sem("h_done"), sem("hT_ps"), sem("hT_done")
        c_tanh, c_silu, cT_ps, cT_done = sem("c_tanh"), sem("c_silu"), sem("cT_ps"), sem("cT_done")
        mod_done, mod_st = sem("mod_done"), sem("mod_st")
        proj_ps, proj_done, rot_done, kt_done = sem("proj_ps"), sem("proj_done"), sem("rot_done"), sem("kt_done")
        kz_done, qk_ps, qk_done, qz_zero = sem("kz_done"), sem("qk_ps"), sem("qk_done"), sem("qz_zero")
        att_ps, att_done, cross_ps, cross_done = sem("att_ps"), sem("att_done"), sem("cross_ps"), sem("cross_done")
        o_ps, o_done, ds_ps, state_done = sem("o_ps"), sem("o_done"), sem("ds_ps"), sem("state_done")
        state_st, state_free = sem("state_st"), sem("state_free")
        s0_ld = [sem("s0_ld0"), sem("s0_ld1")]
        s1_st = [sem("s1_st0"), sem("s1_st1")]
        outer_ps, s1_done, os_ps, os_done = sem("outer_ps"), sem("s1_done"), sem("os_ps"), sem("os_done")
        g_tanh, og_done, oT_ps, oT_done = sem("g_tanh"), sem("og_done"), sem("oT_ps"), sem("oT_done")
        y_ps, y_done = sem("y_ps"), sem("y_done")
        key_ld, key_ps, key_done = sem("key_ld"), sem("key_ps"), sem("key_done")
        q_ps, q_done, score_ps, score_done, top_done = (
            sem("q_ps"), sem("q_done"), sem("score_ps"), sem("score_done"), sem("top_done"))
        e_exp, e_sub = sem("e_exp"), sem("e_sub")
        es_ps, es_done = sem("es_ps"), sem("es_done")
        hs_st, hb_ld = sem("hs_st"), [sem("hb_ld0"), sem("hb_ld1")]
        u_ld = [sem(f"u_ld{s}") for s in range(RING)]
        v_ld = [sem(f"v_ld{s}") for s in range(RING)]
        u_used, v_used = sem("u_used"), sem("v_used")
        mix_free = sem("mix_free")
        issued, issued_pe, issued_act, issued_v = sem("issued"), sem("issued_pe"), sem("issued_act"), sem("issued_v")
        gelu_in, gelu_tanh, wgt_done, diag_done = sem("gelu_in"), sem("gelu_tanh"), sem("wgt_done"), sem("diag_done")
        mix_ps, wz_zero = sem("mix_ps"), sem("wz_zero")
        out_st = sem("out_st")
        steps_v, steps_a, steps_p = sem("steps_v"), sem("steps_a"), sem("steps_p")
        def slot_free(n):
            return n + BATCH - RING + 1

        def gather_of(layer, tile):
            return layer * (NS + TP * NE) + NS + tile * NE

        def landed(layer, tile, batch):
            return 16 * (layer * (1 + TP * NE // RING) + 1 + tile * NE // RING + batch + 1)

        cut = Cut(arena, D)
        region = cut(8 * D)
        uT = cut(G, NB + 2 * NS)
        hh = cut(2, PAIRS, NB + NS)
        braw = cut(2, PAIRS, GP)
        bb = cut(2, PAIRS, GP)
        cT = cut(2, PAIRS, GP)
        pw = cut(2, BL + 1, PAIRS)
        rpw = cut(2, BL, PAIRS)
        disc = cut(4, PAIRS)
        stepA = cut(2, 2, PAIRS)
        oneA = cut(2, 2, PAIRS)
        part = cut(2, 2, PAIRS)
        cut = Cut(region)
        ublk = cut(BL, G, GP)[0:NB + 2 * NS]
        ublk_rows = region[0:NB + 2 * NS, :]
        cut.at = 0
        wb = cut(2, 8, BL, GP)
        wbT = cut(8, 2, P)
        wtmp = cut(4, 8, BL, GP)
        cut.at = 0
        toep = cut(2, 16, P)
        ca = cut(2, 8, BL, GP)
        yc = cut(BL, 16, GP)
        ktmp = region[:, 4 * D:5 * D].rearrange("p (q s n) -> p s q n", s=2, n=GP)
        cut = Cut(hh.rearrange("p c q n -> p (c q n)"))
        craw = cut(2, 8, 2, NST)
        tiny = [cut(P)[0:PAIRS] for _ in range(18)]
        cut = Cut(hT[:, :, :].rearrange("p c n -> p (c n)"))
        hs = cut(NB + 1, 2, PAIRS)
        cut.at = 0
        ugroup = cut(2, 16, BL * GP)
        cut.at = 0
        catmp = cut(2, 8, BL, GP)
        yc2 = cut(BL, 16, GP)
        cut = Cut(h[:, :, :].rearrange("p t n -> p (t n)"))
        dskip = cut(G, GP)
        kk = cut(G, GP)
        s0l = cut(2, NS, P)[0:PAIRS]
        s0t = cut(NS, 2, PAIRS)
        snew = cut(NS, 2, PAIRS)
        slast = kk.rearrange("p g n -> p (g n)")[0:PAIRS, 0:2 * P].rearrange("p (c n) -> p c n", c=2)
        p1_ld, p2_ld, p3_ld, h2_ld = sem("p1_ld"), sem("p2_ld"), sem("p3_ld"), sem("h2_ld")
        kzero_st, ud_st, ub_ld, ub_zero = sem("kzero_st"), sem("ud_st"), sem("ub_ld"), sem("ub_zero")
        u_ps, u_done, kd_st, k_done = sem("u_ps"), sem("u_done"), sem("kd_st"), sem("k_done")
        k_ps, disc_read, ug_done = sem("k_ps"), sem("disc_read"), sem("ug_done")
        t_ld = [sem("t_ld0"), sem("t_ld1")]
        zd_st, z_done, z_ld, so_st, so_done = sem("zd_st"), sem("z_done"), sem("z_ld"), sem("so_st"), sem("so_done")
        sin_in, sin_done, disc_done, disc_ps = sem("sin_in"), sem("sin_done"), sem("disc_done"), sem("disc_ps")
        cT_ps2, cT_done2, s0_ps, s0_done = sem("cT_ps2"), sem("cT_done2"), sem("s0_ps"), sem("s0_done")
        uT_ps, uT_done, wb_done, wb_ps, wb_T = sem("uT_ps"), sem("uT_done"), sem("wb_done"), sem("wb_ps"), sem("wb_T")
        b_ps, b_done, scan_done, hh_done, ca_done = sem("b_ps"), sem("b_done"), sem("scan_done"), sem("hh_done"), sem("ca_done")
        yb_ps, yb_done, zg_in, zg_tanh = sem("yb_ps"), sem("yb_done"), sem("zg_in"), sem("zg_tanh")
        fin_ps, snew_done, glu_ps, glu_tanh, glu_done = (
            sem("fin_ps"), sem("snew_done"), sem("glu_ps"), sem("glu_tanh"), sem("glu_done"))
        GLU_USED = [2 * TILES, 2 * TILES]
        PROMPT = TP * P

        def ssm_sync(sp, load_block, columns, modulation):
            for b in range(2):
                sp.wait_ge(q_ps, 4 * (3 + b))
                load_block(b, columns(b, ssm_w_in[0], b * BW))
            modulation(2)
            pairs = "(q s) n -> q (s n)"
            sp.dma_start(tiny[0], ssm_lam_re[0].rearrange(pairs, s=2)).then_inc(p1_ld, 16)
            sp.dma_start(tiny[1], ssm_lam_im[0].rearrange(pairs, s=2)).then_inc(p1_ld, 16)
            sp.dma_start(tiny[2][:, 0:2], ssm_log_dt[0].rearrange("(q s) -> q s", s=2)).then_inc(p1_ld, 16)
            for c, src in enumerate((ssm_c_re, ssm_c_im)):
                for twice in range(2):
                    sp.dma_start(craw[:, c, :, twice], src[0].rearrange("(a g) o n -> (g o) a n", a=8)).then_inc(p2_ld, 16)
            for c, src in enumerate((ssm_b_re, ssm_b_im)):
                sp.dma_start(braw[:, c], src[0].rearrange("(q s) n i -> (s n) q i", s=2)).then_inc(p3_ld, 16)
            rows = k_d.rearrange("g i j o -> (g i) (j o)")[:, 0:(BL - 1) * GP].rearrange("(a b) n -> b a n", b=P)
            sp.dma_start(rows, spread(zeros[:, 0:(BL - 1) * GP], 1, G * GP // P)).then_inc(kzero_st, 16)
            sp.wait_ge(u_done, 2 * TILES)
            sp.dma_start(u_d[0:PROMPT].rearrange("(t p) n -> p t n", p=P), h[:, 0:TP, :]).then_inc(ud_st, 16)
            sp.dma_start(u_d[PROMPT:NTOK], h[0:NS, TP, :]).then_inc(ud_st, 16)
            sp.wait_ge(ud_st, 32)
            sp.wait_ge(ub_zero, 1)
            sp.dma_start(ublk_rows[0:NB], u_d[0:PROMPT].rearrange("(m t) n -> m (t n)", t=BL)).then_inc(ub_ld, 16)
            sp.dma_start(ublk_rows[NB:NB + NS, 0:D], u_d[PROMPT:NTOK]).then_inc(ub_ld, 16)
            sp.dma_start(ublk_rows[NB + NS:NB + 2 * NS, (BL - 1) * D:BL * D], u_d[PROMPT:NTOK]).then_inc(ub_ld, 16)
            sp.dma_start(dskip.rearrange("p g n -> p (g n)"),
                         ssm_d[0].rearrange("(a g) n -> a (g n)", a=1).to_broadcast([P, D])).then_inc(h2_ld, 16)
            for c, src in enumerate((state_ssm_re, state_ssm_im)):
                sp.dma_start(s0l[:, c], src[0].rearrange("b (q s) n -> q b (s n)", s=2)).then_inc(h2_ld, 16)
            for b, col in ((0, 0), (1, D)):
                load_block(b, columns(b, ssm_w_glu[0], col))
            sp.wait_ge(k_done, 1)
            sp.wait_ge(kzero_st, 16)
            for t in range(BL):
                sp.dma_start(k_d.rearrange("g i j o -> i g j o")[:, :, 2 * BL - 2 - t, :],
                             kk[t * GP:(t + 1) * GP]).then_inc(kd_st, 16)
            sp.wait_ge(kd_st, 16 * BL)
            sp.wait_ge(b_done, 16)
            for c in range(4):
                if c >= 2:
                    sp.wait_ge(yb_ps, c - 1)
                for t in range(BL):
                    src = k_d[16 * c:16 * (c + 1)].rearrange("g i j o -> i g (j o)")
                    sp.dma_start(toep[t * GP:(t + 1) * GP, c % 2], src[:, :, (BL - 1 - t) * GP:(2 * BL - 1 - t) * GP])\
                      .then_inc(t_ld[c % 2], 16)
            sp.wait_ge(so_done, 5)
            for c, (prompt, sample) in enumerate(((re_prompt, re_sample), (im_prompt, im_sample))):
                sp.dma_start(prompt[0, 0].rearrange(pairs, s=2), slast[:, c]).then_inc(so_st, 16)
                sp.dma_start(sample[0].rearrange("b (q s) n -> q b (s n)", s=2), s0l[:, c]).then_inc(so_st, 16)
            for c in range(4):
                sp.wait_ge(z_done, c + 1)
                cols_z = slice(256 * c, 256 * (c + 1))
                sp.dma_start(z_d[0:PROMPT, cols_z].rearrange("(m t) n -> m t n", t=BL),
                             yc[0:NB].rearrange("m t g n -> m t (g n)")).then_inc(zd_st, 16)
                sp.dma_start(z_d[PROMPT:NTOK, cols_z], yc[NB:NB + NS, 0].rearrange("m g n -> m (g n)")).then_inc(zd_st, 16)
            sp.wait_ge(zd_st, 128)
            sp.wait_ge(so_st, 64)
            sp.dma_start(h[:, 0:TP, :], z_d[0:PROMPT].rearrange("(t p) n -> p t n", p=P)).then_inc(z_ld, 16)
            sp.dma_start(h[0:NS, TP, :], z_d[PROMPT:NTOK]).then_inc(z_ld, 16)
            sp.wait_ge(glu_ps, TILES)
            for b, col in ((0, BW), (1, D + BW)):
                load_block(b, columns(b, ssm_w_glu[0], col))

        def ssm_pool(pool, link, root):
            root(HEADS + 3)

        def ssm_act(act, link, norm, transposed):
            norm(2)
            transposed(2)
            for n in range(2 * TILES):
                t, rows = n % TILES, ROWS[n % TILES]
                act.wait_ge(u_ps, n + 1)
                b = n // TILES
                act.activation(h[0:rows, t, b * BW:(b + 1) * BW], ps[0:rows, n % 8, :], ACT.Copy).then_inc(u_done, 1)
            act.wait_ge(sin_in, 1)
            act.activation(tiny[8], tiny[7], ACT.Sin).then_inc(sin_done, 1)
            act.activation(tiny[9], tiny[7], ACT.Sin, scale=0.5).then_inc(sin_done, 1)
            for b in range(4):
                act.wait_ge(cT_ps2, b + 1)
                src = ps[:, b, :].rearrange("p (q s o) -> p q s o", s=2, o=GP)
                for s in range(2):
                    part_ = slice(NST * s, NST * (s + 1))
                    act.activation(cT[part_, b // 2, 16 * (b % 2):16 * (b % 2) + 16], src[part_, :, s], ACT.Copy,
                                   scale=1.0 if b < 2 else -1.0).then_inc(cT_done2, 1)
            act.wait_ge(s0_ps, 1)
            act.activation(s0t, ps[:, 5, :].rearrange("p (b c q) -> p b c q", b=NS, c=2), ACT.Copy).then_inc(s0_done, 1)
            m = NB + 2 * NS

            def regroup(k):
                dst = ugroup[0:m, k % 2].rearrange("m g (t i) -> m t g i", t=BL)
                act.activation(dst, ublk[:, :, 16 * k:16 * k + 16, :], ACT.Copy).then_inc(ug_done, 1)

            act.wait_ge(ub_ld, 48)
            regroup(0)
            regroup(1)
            for n in range(G // 4):
                act.wait_ge(uT_ps, n + 1)
                if n % 4 == 0 and 4 <= n < 12:
                    regroup(n // 4 + 1)
                act.activation(uT[:, 4 * n:4 * n + 4], ps[:, 6 + n % 2, :].rearrange("p (g m) -> p g m", g=4)[:, :, 0:NB + 2 * NS],
                               ACT.Copy).then_inc(uT_done, 1)
            for c in range(4):
                for n in range(4):
                    act.wait_ge(wb_ps, 4 * c + n + 1)
                    act.activation(wbT[:, 2 * n:2 * n + 2], ps[:, n, :].rearrange("p (q c n) -> p q c n", q=2, c=2),
                                   ACT.Copy).then_inc(wb_T, 1)
                for n in range(4):
                    act.wait_ge(b_ps, 4 * c + n + 1)
                    q = 8 * c + 2 * n
                    src = ps[:, 6 + n % 2, :].rearrange("p (q c m) -> p q c m", q=2, c=2)
                    for k in range(2):
                        act.activation(hs[:, 1:NB + 1, k, q:q + 2].rearrange("p m q -> p q m"), src[:, :, k, 0:NB], ACT.Copy)
                        ins = act.activation(snew[:, :, k, q:q + 2].rearrange("p b q -> p q b"),
                                             src[:, :, k, NB + NS:NB + 2 * NS], ACT.Copy)
                    ins.then_inc(b_done, 1)
            act.wait_ge(fin_ps, 1)
            for n in range(4):
                act.activation(s0l[:, n // 2, 4 * (n % 2):4 * (n % 2) + 4], ps[0:PAIRS, n, :].rearrange("p (b n) -> p b n", b=4),
                               ACT.Copy).then_inc(so_done, 1)
            act.wait_ge(kd_st, 16 * BL)
            act.activation(slast, ps[0:PAIRS, 4, 0:2 * P].rearrange("p (c n) -> p c n", c=2), ACT.Copy).then_inc(so_done, 1)
            for c in range(4):
                act.wait_ge(yb_ps, c + 1)
                if c:
                    act.wait_ge(zd_st, 32 * c)
                for n in range(4):
                    src = ps[0:NB + NS, 4 * (c % 2) + n, :].rearrange("m (q t o) -> m q t o", q=4, o=GP)
                    dst = yc[0:NB + NS].rearrange("m t (q s) o -> m s q t o", s=2)[:, n // 2, 4 * (n % 2):4 * (n % 2) + 4]
                    act.activation(dst, src, ACT.Copy).then_inc(yb_done, 1)
                act.wait_ge(zg_in, c + 1)
                act.activation(yc2[0:NB + NS], yc2[0:NB + NS], ACT.Tanh, scale=GELU_C).then_inc(zg_tanh, 1)
            transposed(3)
            for n in range(2 * TILES):
                rows = ROWS[n % TILES]
                act.wait_ge(glu_ps, n + 1)
                if n >= 2:
                    act.wait_ge(glu_done, n - 1)
                act.activation(arena[0:rows, D + n % 2 * BW:D + (n % 2 + 1) * BW], ps[0:rows, 2 * (n % 4) + 1, :], ACT.Tanh,
                               scale=0.5).then_inc(glu_tanh, 1)

        def ssm_pe(pe, norm, block_rows):
            norm(2)
            for n in range(2 * TILES):
                b, t, rows = n // TILES, n % TILES, ROWS[n % TILES]
                if t == 0:
                    pe.wait_ge(w_ld[b], 32 * ((W_SSM + b) // 2 + 1))
                if n == 0:
                    pe.wait_ge(hT_done, 2 * TILES * 3)
                if n >= 8:
                    pe.wait_ge(u_done, n - 7)
                for c in range(KC):
                    mm = pe.matmul(ps[0:rows, n % 8, :], hT[:, c, t * P:t * P + rows], block_rows(b)[:, c, :],
                                   start=(c == 0), stop=(c == KC - 1))
                mm.then_inc(u_ps, 1)
            pe.wait_ge(u_done, 2 * TILES)
            pe.wait_ge(p2_ld, 64)
            for n in range(16):
                mm = pe.transpose(ps[:, n // 4, n % 4 * P:(n % 4 + 1) * P],
                                  craw[:, n // 8, n % 8].rearrange("p a n -> p (a n)"), ident[:, :])
                if n % 4 == 3:
                    mm.then_inc(cT_ps2, 1)
            pe.wait_ge(disc_done, 1)
            for n in range(4):
                mm = pe.transpose(ps[:, 4, n * PAIRS:(n + 1) * PAIRS], tiny[14 + n], ident[0:PAIRS, 0:PAIRS])
            mm.then_inc(disc_ps, 1)
            pe.wait_ge(h2_ld, 48)
            for b in range(NS):
                for c in range(2):
                    at = (2 * b + c) * PAIRS
                    mm = pe.transpose(ps[:, 5, at:at + PAIRS], s0l[:, c, b], ident[0:PAIRS, 0:PAIRS])
            mm.then_inc(s0_ps, 1)
            m = NB + 2 * NS
            for n in range(G // 4):
                if n >= 2:
                    pe.wait_ge(uT_done, n - 1)
                if n % 4 == 0:
                    pe.wait_ge(ug_done, n // 4 + 1)
                for i in range(4):
                    mm = pe.transpose(ps[:, 6 + n % 2, i * P:i * P + m], ugroup[0:m, n // 4 % 2, 4 * (n % 4) + i],
                                      ident[0:m, 0:m])
                mm.then_inc(uT_ps, 1)
            pe.wait_ge(cT_done2, 8)
            pe.wait_ge(s0_done, 1)
            pe.wait_ge(disc_read, 1)
            pe.wait_ge(uT_done, G // 4)
            for c in range(4):
                pe.wait_ge(wb_done, c + 1)
                for n in range(4):
                    if c:
                        pe.wait_ge(wb_T, 4 * (c - 1) + n + 1)
                    for i in range(4):
                        mm = pe.transpose(ps[:, n, i * P:(i + 1) * P],
                                          wb[:, i % 2, 2 * n + i // 2].rearrange("p t n -> p (t n)"), ident[:, :])
                    mm.then_inc(wb_ps, 1)
                for q in range(8):
                    for s in range(2):
                        half = slice(NST * s, NST * (s + 1))
                        at = (8 * c + q) * GP
                        for k in range(2):
                            mm = pe.matmul(ps[:, 4 + s, at:at + GP], wb[half, k, q].rearrange("p t n -> p (t n)"),
                                           cT[half, k, 8 * c + q], start=(k == 0), stop=(k == 1))
                mm.then_inc(k_ps, 1)
                for n in range(4):
                    pe.wait_ge(wb_T, 4 * c + n + 1)
                    if 4 * c + n >= 2:
                        pe.wait_ge(b_done, 4 * c + n - 1)
                    for i in range(2):
                        for k in range(2):
                            for s in range(2):
                                at = (2 * i + k) * P
                                q = 2 * n + i
                                mm = pe.matmul(ps[NST * s:NST * (s + 1), 6 + n % 2, at:at + m],
                                               wbT[:, q, k, NST * s:NST * (s + 1)], uT[:, 2 * (8 * c + q) + s, :],
                                               start=True, stop=True)
                    mm.then_inc(b_ps, 1)
            pe.wait_ge(scan_done, 1)
            pe.wait_ge(snew_done, 1)
            pe.wait_ge(k_done, 1)
            for c in range(2):
                for b in range(NS):
                    mm = pe.transpose(ps[0:PAIRS, 2 * c + b // 4, b % 4 * P:(b % 4 + 1) * P], snew[:, b, c], ident[:, :])
            for c in range(2):
                mm = pe.transpose(ps[0:PAIRS, 4, c * P:(c + 1) * P], hs[:, NB, c], ident[:, :])
            mm.then_inc(fin_ps, 1)
            pe.wait_ge(so_done, 5)
            pe.wait_ge(hh_done, 1)
            pe.wait_ge(b_done, 16)
            m = NB + NS
            for c in range(4):
                pe.wait_ge(ca_done, c + 1)
                pe.wait_ge(t_ld[c % 2], 128 * (c // 2 + 1))
                if c >= 2:
                    pe.wait_ge(yb_done, 4 * (c - 1))
                for s in range(2):
                    half = slice(NST * s, NST * (s + 1))
                    for q in range(8):
                        g, at = 2 * (8 * c + q) + s, q % 4 * P
                        out = ps[0:m, 4 * (c % 2) + 2 * s + q // 4, at:at + P]
                        pe.matmul(out, uT[:, g, 0:m], toep[:, c % 2, 2 * q + s, :], start=True, stop=False)
                        for k in range(2):
                            mm = pe.matmul(out, hh[half, k, 8 * c + q], ca[half, k, q].rearrange("p t n -> p (t n)"),
                                           start=False, stop=(k == 1))
                mm.then_inc(yb_ps, 1)
            pe.wait_ge(yb_done, 16)
            norm(3)
            pe.wait_ge(hT_done, 2 * TILES * 4)
            for j in range(2):
                for t, rows in enumerate(ROWS):
                    n = j * TILES + t
                    if t == 0:
                        for b in range(2):
                            pe.wait_ge(w_ld[b], 32 * ((W_GLU + 2 * j) // 2 + 1))
                    if n >= 4:
                        pe.wait_ge(glu_done, n - 3)
                    for b in range(2):
                        for c in range(KC):
                            mm = pe.matmul(ps[0:rows, 2 * (n % 4) + b, :], hT[:, c, t * P:t * P + rows],
                                           block_rows(b)[:, c, :], start=(c == 0), stop=(c == KC - 1))
                    mm.then_inc(glu_ps, 1)

        def ssm_dve(dve, link, norm):
            norm(2, HEADS + 3)
            lr, li, ldt, dt, t1, t2, t3, ang, sn, sh, mag = tiny[0:11]
            bits = tiny[11].bitcast(I32)
            are, aim, fre, fim = tiny[14:18]
            MAGIC = 12582912.0

            def tt(out, a, b, op):
                link.link(dve.tensor_tensor(out, a, b, op))

            def ts(out, a, s1, s2, op0, op1):
                link.link(dve.tensor_scalar(out, a, s1, s2, op0, op1))

            def exp(out, z):
                ts(t1, z, 1.4426950408889634, MAGIC, ALU.mult, ALU.add)
                ts(t1, t1, MAGIC, -126.0, ALU.subtract, ALU.max)
                ts(t1, t1, 127.0, None, ALU.min, ALU.bypass)
                link.link(dve.scalar_tensor_tensor(t2, t1, -0.693359375, z, ALU.mult, ALU.add))
                link.link(dve.scalar_tensor_tensor(t2, t1, 2.12194440e-4, t2, ALU.mult, ALU.add))
                ts(t3, t2, 1.0 / 5040, None, ALU.mult, ALU.bypass)
                for coefficient in (1.0 / 720, 1.0 / 120, 1.0 / 24, 1.0 / 6, 0.5, 1.0):
                    link.link(dve.scalar_tensor_tensor(t3, t3, coefficient, t2, ALU.add, ALU.mult))
                ts(t1, t1, 127.0, 8388608.0, ALU.add, ALU.mult)
                link.link(dve.tensor_copy(bits, t1))
                link.link(dve.scalar_tensor_tensor(out, t3, 1.0, bits.bitcast(F32), ALU.add, ALU.mult))

            dve.wait_ge(p1_ld, 48)
            link.link(dve.tensor_copy(mag.rearrange("q (s n) -> q s n", s=2), spread(ldt[:, 0:2], 2, NST)))
            exp(dt, mag)
            tt(ang, li, dt, ALU.mult)
            ts(t1, ang, 0.15915494309189535, MAGIC, ALU.mult, ALU.add)
            ts(t1, t1, MAGIC, None, ALU.subtract, ALU.bypass)
            for piece in (-6.28125, -0.0019350051879882812, -3.0199159819e-07):
                link.link(dve.scalar_tensor_tensor(ang, t1, piece, ang, ALU.mult, ALU.add))
            dve.tensor_scalar(ang, ang, 3.1415925, -3.1415925, ALU.min, ALU.max).then_inc(sin_in, 1)
            tt(tiny[12], lr, dt, ALU.mult)
            exp(mag, tiny[12])
            dve.wait_ge(sin_done, 2)
            tt(aim, mag, sn, ALU.mult)
            tt(sh, sh, sh, ALU.mult)
            ts(sh, sh, -2.0, 1.0, ALU.mult, ALU.add)
            tt(are, mag, sh, ALU.mult)
            tt(t1, lr, lr, ALU.mult)
            tt(t2, li, li, ALU.mult)
            tt(t1, t1, t2, ALU.add)
            link.link(dve.reciprocal(t3, t1))
            ts(tiny[12], are, -1.0, None, ALU.add, ALU.bypass)
            tt(t1, tiny[12], lr, ALU.mult)
            tt(t2, aim, li, ALU.mult)
            tt(t1, t1, t2, ALU.add)
            tt(fre, t1, t3, ALU.mult)
            tt(t1, aim, lr, ALU.mult)
            tt(t2, tiny[12], li, ALU.mult)
            tt(t1, t1, t2, ALU.subtract)
            dve.tensor_tensor(fim, t1, t3, ALU.mult).then_inc(disc_done, 1)
            dve.memset(ublk_rows[NB:NB + 2 * NS, :], 0.0).then_inc(ub_zero, 1)
            dve.wait_ge(disc_ps, 1)
            link.link(dve.tensor_copy(disc, ps[:, 4, 0:4 * PAIRS].rearrange("p (c q) -> p c q", c=4)))
            dve.sem_inc(disc_read, 1)

            tmp = part.rearrange("p a b q -> p (a b) q")

            def power(out, a, b, n):
                for m in range(n):
                    x0, x1, z0, z1 = pw[:, 0, a], pw[:, 1, a], pw[:, 0, b + m], pw[:, 1, b + m]
                    dve.tensor_tensor(tmp[:, 0], x0, z0, ALU.mult)
                    dve.tensor_tensor(tmp[:, 1], x1, z1, ALU.mult)
                    dve.tensor_tensor(tmp[:, 2], x0, z1, ALU.mult)
                    tt(tmp[:, 3], x1, z0, ALU.mult)
                    dve.tensor_tensor(pw[:, 0, out + m], tmp[:, 0], tmp[:, 1], ALU.subtract)
                    tt(pw[:, 1, out + m], tmp[:, 2], tmp[:, 3], ALU.add)

            dve.memset(pw[:, 0, 0], 1.0)
            dve.memset(pw[:, 1, 0], 0.0)
            dve.tensor_copy(pw[:, 0, 1], disc[:, 0])
            link.link(dve.tensor_copy(pw[:, 1, 1], disc[:, 1]))
            power(2, 1, 1, 1)
            power(3, 2, 1, 2)
            power(5, 4, 1, 4)
            for t in range(BL):
                ins = dve.tensor_copy(rpw[:, :, t], pw[:, :, BL - 1 - t])
            for mat, n in ((stepA, BL), (oneA, 1)):
                dve.tensor_copy(mat[:, 0, 0], pw[:, 0, n])
                dve.tensor_copy(mat[:, 1, 1], pw[:, 0, n])
                dve.tensor_copy(mat[:, 1, 0], pw[:, 1, n])
                ins = dve.tensor_scalar(mat[:, 0, 1], pw[:, 1, n], -1.0, None, ALU.mult)
            link.link(ins)
            dve.wait_ge(p3_ld, 32)
            dve.wait_ge(uT_done, G // 4)
            q4 = wtmp.rearrange("p k q t n -> p k (q t n)")
            f = [q4[:, k, 0:PAIRS * GP].rearrange("p (q n) -> p q n", q=PAIRS) for k in range(4)]
            cre, cim = spread(disc[:, 2], 2, GP), spread(disc[:, 3], 2, GP)
            dve.tensor_tensor(f[0], cre, braw[:, 0], ALU.mult)
            dve.tensor_tensor(f[1], cim, braw[:, 1], ALU.mult)
            dve.tensor_tensor(f[2], cre, braw[:, 1], ALU.mult)
            tt(f[3], cim, braw[:, 0], ALU.mult)
            dve.tensor_tensor(bb[:, 0], f[0], f[1], ALU.subtract)
            tt(bb[:, 1], f[2], f[3], ALU.add)
            for c in range(4):
                qs = slice(8 * c, 8 * c + 8)
                pr, pi = (spread(rpw[:, k, :, qs].rearrange("p t q -> p q t"), 3, GP) for k in range(2))
                br, bi = (spread(bb[:, k, qs], 2, BL) for k in range(2))
                dve.tensor_tensor(wtmp[:, 0], pr, br, ALU.mult)
                dve.tensor_tensor(wtmp[:, 1], pi, bi, ALU.mult)
                dve.tensor_tensor(wtmp[:, 2], pr, bi, ALU.mult)
                tt(wtmp[:, 3], pi, br, ALU.mult)
                if c:
                    dve.wait_ge(k_ps, c)
                dve.tensor_tensor(wb[:, 0], wtmp[:, 0], wtmp[:, 1], ALU.subtract)
                dve.tensor_tensor(wb[:, 1], wtmp[:, 2], wtmp[:, 3], ALU.add).then_inc(wb_done, 1)
                dve.wait_ge(wb_done, c + 1)
            dve.wait_ge(h2_ld, 48)
            tt(ktmp, spread(spread(ident[:, P - GP:P], 1, PAIRS), 1, 2),
               dskip.rearrange("p (q s) n -> p s q n", s=2), ALU.mult)
            dve.wait_ge(k_ps, 4)
            kv = kk.rearrange("p (q s) n -> p s q n", s=2)
            dve.tensor_tensor(kv[:, 0], ps[:, 4, :].rearrange("p (q n) -> p q n", q=PAIRS), ktmp[:, 0], ALU.add)
            dve.tensor_tensor(kv[:, 1], ps[:, 5, :].rearrange("p (q n) -> p q n", q=PAIRS), ktmp[:, 1], ALU.add)\
               .then_inc(k_done, 1)
            dve.memset(hs[:, 0], 0.0)
            dve.wait_ge(b_done, 16)
            s2 = snew.rearrange("p b c q -> p c b q")
            old = s0t.rearrange("p b c q -> p c b q")
            dve.wait_ge(s0_done, 1)
            dve.wait_ge(k_done, 1)
            stmp = [q4[:, k, 0:NS * PAIRS].rearrange("p (b q) -> p b q", b=NS) for k in range(4)]
            for o_ in range(2):
                for i_ in range(2):
                    ins = dve.tensor_tensor(stmp[2 * o_ + i_], old[:, i_], spread(oneA[:, o_, i_], 1, NS), ALU.mult)
            link.link(ins)
            for i_ in range(2):
                for o_ in range(2):
                    ins = dve.tensor_tensor(s2[:, o_], s2[:, o_], stmp[2 * o_ + i_], ALU.add)
                link.link(ins)
            dve.sem_inc(snew_done, 1)
            with dve.Fori(0, NB // 4) as i:
                link.loop(i, 12)
                for s in range(4):
                    before = hs[:, bass.ds(4 * i + s, 1)].rearrange("p a c q -> p (a c) q")
                    after = hs[:, bass.ds(4 * i + s + 1, 1)].rearrange("p a c q -> p (a c) q")
                    link.link(dve.tensor_tensor(part, stepA, spread(before, 1, 2), ALU.mult))
                    link.link(dve.tensor_tensor(after, after, part[:, :, 0], ALU.add))
                    link.link(dve.tensor_tensor(after, after, part[:, :, 1], ALU.add))
            link.end(NB // 4)
            dve.sem_inc(scan_done, 1)
            for k in range(2):
                dve.tensor_copy(hh[:, k, :, 0:NB], hs[:, 0:NB, k].rearrange("p m q -> p q m"))
                ins = dve.tensor_copy(hh[:, k, :, NB:], s0t[:, :, k].rearrange("p b q -> p q b"))
            link.link(ins)
            dve.sem_inc(hh_done, 1)
            dve.wait_ge(fin_ps, 1)
            for c in range(4):
                qs = slice(8 * c, 8 * c + 8)
                ar, ai = (spread(pw[:, k, 1:BL + 1, qs].rearrange("p t q -> p q t"), 3, GP) for k in range(2))
                cr, ci = (spread(cT[:, k, qs], 2, BL) for k in range(2))
                if c:
                    dve.wait_ge(yb_ps, c)
                for k, op in enumerate((ALU.add, ALU.subtract)):
                    a_, b_ = catmp[:, 0], catmp[:, 1]
                    dve.tensor_tensor(a_, cr if k == 0 else ci, ar, ALU.mult)
                    tt(b_, ci if k == 0 else cr, ai, ALU.mult)
                    ins = dve.tensor_tensor(ca[:, k], a_, b_, op)
                    if k == 0:
                        link.link(ins)
                    else:
                        ins.then_inc(ca_done, 1)
                dve.wait_ge(ca_done, c + 1)
                dve.wait_ge(yb_done, 4 * (c + 1))
                y_, y2 = yc[0:NB + NS], yc2[0:NB + NS]
                y_, y2 = (v.rearrange("m t g o -> m (t g o)") for v in (y_, y2))
                tt(y2, y_, y_, ALU.mult)
                ts(y2, y2, GELU_A, 1.0, ALU.mult, ALU.add)
                dve.tensor_tensor(y2, y2, y_, ALU.mult).then_inc(zg_in, 1)
                dve.wait_ge(zg_tanh, c + 1)
                link.link(dve.scalar_tensor_tensor(y2, y2, 1.0, y_, ALU.add, ALU.mult))
                dve.tensor_scalar(y_, y2, 0.5, None, ALU.mult).then_inc(z_done, 1)
                dve.wait_ge(z_done, c + 1)
            dve.wait_ge(z_ld, 32)
            dve.sem_inc(h_done, TILES)
            gt = arena[:, 2 * D:4 * D].rearrange("p (a n) -> p a n", a=4)
            for n in range(2 * TILES):
                j, t, rows = n // TILES, n % TILES, ROWS[n % TILES]
                mod = (modp if t < TP else mods)[0:rows, 2, j * BW:(j + 1) * BW]
                dve.wait_ge(glu_tanh, n + 1)
                th = arena[0:rows, D + n % 2 * BW:D + (n % 2 + 1) * BW]
                v1, v2 = gt[0:rows, n % 2], gt[0:rows, 2 + n % 2]
                dve.scalar_tensor_tensor(v1, th, 1.0, ps[0:rows, 2 * (n % 4), :], ALU.add, ALU.mult).then_inc(glu_done, 1)
                dve.wait_ge(glu_done, n + 1)
                link.link(dve.scalar_tensor_tensor(v2, v1, 0.5, mod, ALU.mult, ALU.mult))
                xt = x[0:rows, t, j * BW:(j + 1) * BW]
                link.link(dve.tensor_tensor(xt, xt, v2, ALU.add))
            dve.sem_inc(x_ready, 1)

        block = ctx.enter_context(nc.Block())

        @block.sync
        def _(sp):
            def load_block(slot, halves):
                for dst, src in halves:
                    sp.dma_start(dst, src).then_inc(w_ld[slot], 16)

            def columns(slot, wm, col):
                dst = w[:, slot, :].rearrange("p (c n) -> p c n", c=KC)
                src = wm.rearrange("(c p) n -> p c n", p=P)
                return [(dst[:, c:c + KC // 2], src[:, c:c + KC // 2, bass.ds(col, BW)]) for c in (0, KC // 2)]

            def qk_columns(slot, head):
                dst = w[:, slot, :].rearrange("p (c s n) -> p c s n", c=KC, s=2)
                src = ret_w_in[0].rearrange("(c p) n -> p c n", p=P)
                return [(dst[:, :, s], src[:, :, bass.ds(head * DK + s * HEADS * DK, DK)]) for s in range(2)]

            def out_rows(slot, head):
                dst = w[:, slot, :].rearrange("p (k n) -> p k n", k=4)
                src = ret_w_out[0].rearrange("(k p) n -> p k n", p=P)
                return [(dst[:, k:k + 2], src[:, bass.ds(head * 4 + k, 2), :]) for k in (0, 2)]

            def modulation(k):
                if k == 0:
                    sp.wait_ge(mod_st, 16 * LAYERS)
                if k:
                    sp.wait_ge(x_ready, k)
                at = k * 3 * D
                sp.dma_start(modp[:, :, :].rearrange("p s n -> p (s n)"),
                             mod_d[NS:NC, at:at + 3 * D].to_broadcast([P, 3 * D])).then_inc(mod_ld, 16)
                sp.dma_start(mods[0:NS, :, :].rearrange("p s n -> p (s n)"),
                             mod_d[0:NS, at:at + 3 * D]).then_inc(mod_ld, 16)
                sp.dma_start(gain, norm_g[k // 2, k % 2:k % 2 + 1, :].to_broadcast([P, D])).then_inc(mod_ld, 16)

            sp.dma_start(cond[0:NS, :], c_sample).then_inc(c_ld, 16)
            sp.dma_start(cond[NS:NC, :], c_prompt).then_inc(c_ld, 16)
            for b in range(2):
                load_block(b, columns(b, w_ada[0], b * BW))
            sp.dma_start(bias, b_ada.rearrange("l (a n) -> a (l n)", a=1).to_broadcast([NC, LAYERS * 6 * D]))\
              .then_inc(tab_ld, 16)
            sp.dma_start(x[:, 0:TP, :], x_prompt[0].rearrange("(t p) n -> p t n", p=P)).then_inc(x_ld, 16)
            sp.dma_start(x[0:NS, TP, :], x_sample[:, 0, :]).then_inc(x_ld, 16)
            sp.dma_start(rots, rot_tab).then_inc(tab_ld, 16)
            sp.dma_start(masks, decay_tab).then_inc(tab_ld, 16)
            sp.dma_start(colss, decay_cols).then_inc(tab_ld, 16)

            per_layer = ADA_BLOCKS // LAYERS
            for layer in range(LAYERS):
                with sp.Fori(1 if layer == 0 else 0, per_layer // 2) as i:
                    for s in range(2):
                        sp.wait_ge(w_used, 2 * i + (layer * per_layer + s - 1))
                        load_block(s, columns(s, w_ada[layer], (2 * i + s) * BW))
            def head_blocks(head, last):
                sp.wait_ge(y_done, head * 2 * TILES + 1)
                load_block(1, columns(1, ret_w_in[0], head * DV + 2 * HEADS * DK))
                sp.wait_ge(proj_ps, head * 3 * TILES + TILES)
                load_block(0, columns(0, ret_w_in[0], head * DV + 2 * HEADS * DK + HEADS * DV))
                sp.wait_ge(proj_ps, head * 3 * TILES + 2 * TILES)
                load_block(1, out_rows(1, head))
                if not last:
                    sp.wait_ge(proj_ps, head * 3 * TILES + 3 * TILES)
                    load_block(0, qk_columns(0, head + 1))

            sp.wait_ge(w_used, ADA_BLOCKS - 1)
            load_block(0, qk_columns(0, 0))
            sp.wait_ge(w_used, ADA_BLOCKS)
            modulation(0)
            with sp.Fori(0, HEADS - 1) as head:
                head_blocks(head, False)
            head_blocks(HEADS - 1, True)

            def peer(layer):
                def query(b):
                    n = W_PEER[layer] + b
                    if b >= 2:
                        sp.wait_ge(q_ps, 2 * PH * layer + 4 * (b - 1))
                    elif layer == 0:
                        sp.wait_ge(*((proj_ps, HEADS * 3 * TILES), (y_ps, HEADS * 2 * TILES))[b])
                    else:
                        sp.wait_ge(glu_ps, GLU_USED[b])
                    load_block(n % 2, columns(n % 2, peer_w_q[layer], b * BW))

                query(0)
                query(1)
                modulation(2 * layer + 1)
                for side, key in enumerate((peer_key1, peer_key2)):
                    sp.dma_start(keys.rearrange("p (e s) d -> p e s d", s=2)[:, :, side],
                                 key[layer].rearrange("e k d -> k e d")).then_inc(key_ld, 16)
                if layer == 0:
                    sp.dma_start(lane[:, :], lane_tab).then_inc(key_ld, 16)
                query(2)
                query(3)
                sp.wait_ge(h_done, TILES * (TURN[2 * layer + 1] + 1))
                sp.dma_start(hs_d[layer], h[0:NS, TP, :]).then_inc(hs_st, 16)
                sp.wait_ge(hs_st, 16 * (layer + 1))
                sp.wait_ge(top_done, TILES * (layer + 1))
                for b in range(NS):
                    if b >= 2:
                        sp.wait_ge(u_used, BATCH + gather_of(layer, 0) - NS + b - 1)
                    sp.dma_start(hb[:, b % 2], hs_d[layer, b:b + 1, :].to_broadcast([P, D])).then_inc(hb_ld[b % 2], 16)

            peer(0)
            ssm_sync(sp, load_block, columns, modulation)
            peer(1)
            sp.wait_ge(x_ready, FINAL)
            sp.dma_start(gain, final_g.rearrange("(a n) -> a n", a=1).to_broadcast([P, D])).then_inc(fin_ld, 16)
            sp.wait_ge(h_done, TILES * (TURN[FINAL] + 1))
            sp.dma_start(y_prompt[0].rearrange("(t p) n -> p t n", p=P), h[:, 0:TP, :]).then_inc(out_st, 16)
            sp.dma_start(y_sample[:, 0, :], h[0:NS, TP, :]).then_inc(out_st, 16)
            sp.wait_ge(out_st, 32)

        @block.gpsimd
        def _(pool):
            link = Steps(pool, steps_p)
            pool.memset(ident[:, :], 0.0).then_inc(consts, 1)
            pool.memset(zeros[:, :], 0.0).then_inc(consts, 1)
            pool.memset(mhalf[:, :], -0.5).then_inc(consts, 1)
            pool.wait_ge(consts, 3)
            pool.affine_select(out=ident[:, :], in_=ident[:, :], compare_op=ALU.not_equal, fill=1.0, base=0,
                               pattern=[[-1, P]], channel_multiplier=1).then_inc(consts, 1)
            pool.wait_ge(consts, 4)

            def root(n):
                pool.wait_ge(var_done, n)
                pool.tensor_tensor(rstd[:, :], var[:, :], mhalf[:, :], ALU.pow).then_inc(rstd_done, 1)

            root(1)

            def s0(head, b):
                return state_ret[0, b].rearrange("e (c p) v -> p e c v", p=P)[:, bass.ds(head, 1)]

            def s1(head, b):
                return ret_sample[0, b].rearrange("e (c p) v -> p e c v", p=P)[:, bass.ds(head, 1)]

            def load_state(head, b):
                pool.dma_start(sring[:, b % 2].unsqueeze(1), s0(head, b)).then_inc(s0_ld[b % 2], 16)

            def head_states(head, last):
                for b in range(NS):
                    pool.wait_ge(s1_done, head * NS + (b + 1))
                    pool.sem_inc(issued, 1)
                    pool.dma_start(s1(head, b), sring[:, b % 2].unsqueeze(1)).then_inc(s1_st[b % 2], 16)
                    if b >= 1 and (b < NS - 1 or not last):
                        slot = (b - 1) % 2
                        pool.wait_ge(s1_st[slot], head * (NS // 2) * 16 + 16 * ((b - 1) // 2 + 1))
                        pool.wait_ge(os_ps, head * NS + b)
                        pool.sem_inc(issued, 1)
                        if b + 1 < NS:
                            load_state(head, b + 1)
                        else:
                            load_state(head + 1, 0)
                if not last:
                    pool.wait_ge(s1_st[1], head * (NS // 2) * 16 + 16 * (NS // 2))
                    pool.wait_ge(os_ps, head * NS + NS)
                    pool.sem_inc(issued, 1)
                    load_state(head + 1, 1)
                pool.wait_ge(state_done, head * TP + TP)
                pool.sem_inc(issued, 1)
                pool.dma_start(ret_prompt[0, 0].rearrange("e (c p) v -> p e c v", p=P)[:, bass.ds(head, 1)],
                               state.unsqueeze(1)).then_inc(state_st, 16)
                pool.wait_ge(var_done, head + 2)
                pool.tensor_tensor(rstd[:, :], var[:, :], mhalf[:, :], ALU.pow).then_inc(rstd_done, 1)
                pool.wait_ge(state_st, head * 16 + 16)
                pool.sem_inc(state_free, 1)

            pool.wait_ge(h_done, TILES)
            pool.sem_inc(state_free, 1)
            load_state(0, 0)
            load_state(0, 1)
            with pool.Fori(0, HEADS - 1) as head:
                head_states(head, False)
            head_states(HEADS - 1, True)
            for s in range(2):
                pool.wait_ge(s1_st[s], 16 * HEADS * NS // 2)

            def gather(ring, slot, table, index, landed_sem):
                pool.indirect_dma_start(ring[:, slot, :], None, table,
                                        bass.IndirectOffsetOnAxis(ap=index, axis=0)).then_inc(landed_sem[slot], 16)

            def peer(layer):
                root(1 + HEADS + 1 if layer == 0 else NORMS - 1)
                ut = peer_u.rearrange("l e n -> (l e) n")
                vt = peer_v.rearrange("l e n -> (l e) n")
                pool.wait_ge(es_done, 2 * (layer + 1))
                for b in range(NS):
                    n = gather_of(layer, 0) - NS + b
                    pool.wait_ge(u_used, slot_free(n))
                    gather(u_ring, b, ut, eidx_s[:, b:b + 1], u_ld)
                    pool.wait_ge(v_used, slot_free(n))
                    gather(v_ring, b, vt, eidx_s[:, b:b + 1], v_ld)
                for turn in range(TP + 1):
                    lanes = [(ring, table, stage, used, ld, tile)
                             for ring, table, stage, used, ld, tile in (
                                 (u_ring, ut, stage_u, u_used, u_ld, turn), (v_ring, vt, stage_v, v_used, v_ld, turn - 1))
                             if 0 <= tile < TP]
                    with pool.Fori(0, NE // BATCH) as i:
                        link.loop(i, 2 * len(lanes))
                        for half in range(2):
                            for ring, table, stage, used, ld, tile in lanes:
                                n = gather_of(layer, tile) + half * RING
                                pool.wait_ge(used, i * BATCH + (n + BATCH - RING))
                                pool.sem_inc(issued, 1)
                                link.link(pool.tensor_copy(stage[:, half],
                                                           eidx[:, tile, bass.ds(i * BATCH + half * RING, RING)]))
                                pool.sem_inc(issued, 1)
                            for s in range(RING):
                                for ring, table, stage, used, ld, tile in lanes:
                                    pool.wait_ge(used, i * BATCH + slot_free(gather_of(layer, tile) + half * RING + s))
                                    pool.sem_inc(issued, 1)
                                    gather(ring, s, table, stage[:, half, s:s + 1], ld)
                    link.end(NE // BATCH)

            peer(0)
            ssm_pool(pool, link, root)
            peer(1)
            root(NORMS)

        @block.scalar
        def _(act):
            link = Steps(act, steps_a)

            def norm(k):
                if k:
                    act.wait_ge(x_ready, k)
                else:
                    act.wait_ge(x_ld, 32)
                    act.wait_ge(constv, 1)
                for t, rows in enumerate(ROWS):
                    act.activation(h[0:rows, t, :], x[0:rows, t, :], ACT.Square, accum_out=sq[0:rows, t:t + 1])\
                       .then_inc(sq_done, 1)

            def transposed(k):
                for t, rows in enumerate(ROWS):
                    for half in range(2):
                        n = 2 * t + half
                        act.wait_ge(hT_ps, 2 * TILES * k + n + 1)
                        src = ps[:, n % 8, :].rearrange("p (c r) -> p c r", c=4)
                        act.activation(hT[:, 4 * half:4 * half + 4, t * P:t * P + rows], src[:, :, 0:rows], ACT.Copy)\
                           .then_inc(hT_done, 1)

            act.wait_ge(c_ld, 32)
            act.activation(cond_t, cond, ACT.Tanh, scale=0.5).then_inc(c_tanh, 1)
            for layer in range(LAYERS):
                act.wait_ge(mod_done, 2 + (layer + 1) * ADA_BLOCKS // LAYERS)
                at = layer * 6 * D
                act.dma_start(mod_d[:, at:at + 6 * D], bias[:, at:at + 6 * D]).then_inc(mod_st, 16)
            norm(0)
            transposed(TURN[0])

            with act.Fori(0, HEADS) as head:
                act.wait_ge(y_done, head * 2 * TILES + 1)
                for j in range(3):
                    for t, rows in enumerate(ROWS):
                        act.wait_ge(proj_ps, head * 3 * TILES + (j * TILES + t + 1))
                        act.activation(proj[0:rows, t, j * BW:(j + 1) * BW], ps[0:rows, t, :], ACT.Copy)\
                           .then_inc(proj_done, 1)
                for t in range(TP):
                    act.wait_ge(qk_ps, head * TILES + (t + 1))
                    act.activation(qkT[:, t], ps[:, 5 + t % 2, :].rearrange("p (c r) -> p c r", c=4), ACT.Copy)\
                       .then_inc(qk_done, 1)
                act.wait_ge(qk_ps, head * TILES + TILES)
                act.wait_ge(qz_zero, 1)
                act.activation(qz[:, :, ::NS + 1], ps[:, 7, 0:2 * NS].rearrange("p (c r) -> p c r", c=2), ACT.Copy)\
                   .then_inc(qk_done, 1)
                act.wait_ge(rot_done, head * 2 + 2)
                act.wait_ge(proj_done, head * 3 * TILES + 3 * TILES)
                for t, rows in enumerate(ROWS):
                    act.activation(sil[0:rows, t], proj[0:rows, t, 2 * BW:3 * BW], ACT.Tanh, scale=0.5)\
                       .then_inc(g_tanh, 1)
                for t in range(1, TP):
                    act.wait_ge(cross_ps, head * (TP - 1) + t)
                    if t >= 3:
                        act.wait_ge(o_done, head * TP + (t - 1))
                    act.activation(cross[:, t % 2], ps[:, 6, :], ACT.Copy, scale=cols[:, 0:1]).then_inc(cross_done, 1)
                for t, rows in enumerate(ROWS):
                    act.wait_ge(oT_ps, head * TILES + (t + 1))
                    src = ps[:, 5 + t % 2, :].rearrange("p (c r) -> p c r", c=4)
                    act.activation(oT[:, :, t * P:t * P + rows], src[:, :, 0:rows], ACT.Copy).then_inc(oT_done, 1)

            def peer(layer):
                k = 2 * layer + 1
                norm(k)
                transposed(TURN[k])
                for b in range(4):
                    act.wait_ge(key_ps, 4 * layer + b + 1)
                    act.activation(keyT[:, 4 * b:4 * b + 4], ps[:, 4 + b, :].rearrange("p (c r) -> p c r", c=4),
                                   ACT.Copy).then_inc(key_done, 1)
                for n in range(2 * PH):
                    act.wait_ge(q_ps, 2 * PH * layer + n + 1)
                    act.activation(qT[:, n, 0:TP * P], ps[:, n % 2, :], ACT.Copy).then_inc(q_done, 1)
                    act.activation(qT[:, n, TP * P:NTOK], ps[:, 2 + n % 2, 0:NS], ACT.Copy).then_inc(q_done, 1)
                for m in range(TILES):
                    t = (TP + m) % TILES
                    rows = ROWS[t]
                    act.wait_ge(score_ps, TILES * layer + m + 1)
                    if m:
                        act.wait_ge(top_done, TILES * layer + m)
                    for b in range(4):
                        act.activation(score[0:rows, 4 * b:4 * b + 4],
                                       ps[0:rows, 4 * (m % 2) + b, :].rearrange("p (c r) -> p c r", c=4), ACT.Copy)\
                           .then_inc(score_done, 1)
                    act.wait_ge(e_sub, TILES * layer + m + 1)
                    act.activation(topv[0:rows], topv[0:rows], ACT.Exp).then_inc(e_exp, 1)
                act.wait_ge(gelu_in, TILES * layer + 1)
                act.activation(acts_s2, acts_s2, ACT.Tanh, scale=GELU_C).then_inc(gelu_tanh, 1)
                for t in range(TP):
                    act.wait_ge(gelu_in, TILES * layer + t + 2)
                    act.activation(acts2, acts2, ACT.Tanh, scale=GELU_C).then_inc(gelu_tanh, 1)
                    act.wait_ge(wgt_done, TILES * layer + t + 2)
                    with act.Fori(0, NE // 4) as i:
                        for s in range(4):
                            act.wait_ge(v_used, 4 * i + (gather_of(layer, t) + s + BATCH - 4 + 1))
                            act.sem_inc(issued_act, 1)
                            act.activation(diag[:, s], ident[:, :], ACT.Copy,
                                           scale=wgt[:, t % 2, bass.ds(4 * i + s, 1)]).then_inc(diag_done, 1)

            peer(0)
            ssm_act(act, link, norm, transposed)
            peer(1)
            norm(FINAL)

        @block.tensor
        def _(pe):
            def norm(k):
                for t, rows in enumerate(ROWS):
                    pe.wait_ge(h_done, TILES * k + t + 1)
                    for half in range(2):
                        n = 2 * t + half
                        if n >= 8:
                            pe.wait_ge(hT_done, 2 * TILES * k + n - 8 + 1)
                        for c in range(4):
                            mm = pe.transpose(ps[:, n % 8, c * P:c * P + rows],
                                              h[0:rows, t, (4 * half + c) * P:(4 * half + c + 1) * P],
                                              ident[0:rows, 0:rows])
                        mm.then_inc(hT_ps, 1)

            def block_rows(slot):
                return w[:, slot, :].rearrange("p (c n) -> p c n", c=KC)

            pe.wait_ge(consts, 4)
            pe.wait_ge(c_silu, 1)
            for c in range(KC):
                mm = pe.transpose(ps[:, 0, c * NC:(c + 1) * NC], cond[:, c * P:(c + 1) * P], ident[0:NC, 0:NC])
            mm.then_inc(cT_ps, 1)
            pe.wait_ge(cT_done, 1)
            with pe.Fori(0, ADA_BLOCKS // 2) as i:
                for s in range(2):
                    pe.wait_ge(w_ld[s], i * 32 + 32)
                    pe.wait_ge(mod_done, 2 * i + (s + 1))
                    for c in range(KC):
                        mm = pe.matmul(ps[0:NC, 1 + s, :], condT[:, c, :], block_rows(s)[:, c, :],
                                       start=(c == 0), stop=(c == KC - 1))
                    mm.then_inc(w_used, 1)
            norm(0)

            with pe.Fori(0, HEADS) as head:
                pe.wait_ge(y_done, head * 2 * TILES + 1)
                for j in range(3):
                    slot = j % 2
                    pe.wait_ge(w_ld[slot], head * 64 + 32 * (W_HEADS // 2 + j // 2 + 1))
                    for t, rows in enumerate(ROWS):
                        if j:
                            pe.wait_ge(proj_done, head * 3 * TILES + ((j - 1) * TILES + t + 1))
                        elif t == 0:
                            pe.wait_ge(hT_done, 2 * TILES)
                        for c in range(KC):
                            mm = pe.matmul(ps[0:rows, t, :], hT[:, c, t * P:t * P + rows], block_rows(slot)[:, c, :],
                                           start=(c == 0), stop=(c == KC - 1))
                        mm.then_inc(proj_ps, 1)
                pe.wait_ge(rot_done, head * 2 + 2)
                pe.sem_inc(issued_pe, 1)
                for t in range(TP):
                    if t >= 2:
                        pe.wait_ge(qk_done, head * TILES + (t - 1))
                    for c in range(4):
                        mm = pe.transpose(ps[:, 5 + t % 2, c * P:(c + 1) * P],
                                          qkr[:, t, c // 2, c % 2 * P:(c % 2 + 1) * P], ident[:, :])
                    mm.then_inc(qk_ps, 1)
                for c in range(2):
                    mm = pe.transpose(ps[:, 7, c * NS:(c + 1) * NS], qkr[0:NS, TP, 0, c * P:(c + 1) * P],
                                      ident[0:NS, 0:NS])
                mm.then_inc(qk_ps, 1)
                pe.wait_ge(qk_done, head * TILES + TILES)
                pe.wait_ge(kt_done, head + 1)
                pe.wait_ge(proj_done, head * 3 * TILES + 3 * TILES)
                for t in range(TP):
                    if t:
                        pe.wait_ge(att_done, head * TP + t)
                    for c in range(2):
                        mm = pe.matmul(ps[:, 7, 0:P], qkT[:, t, 2 + c], qkT[:, t, c], start=(c == 0), stop=(c == 1))
                    mm.then_inc(att_ps, 1)
                    if t:
                        pe.wait_ge(state_done, head * TP + t)
                        if t >= 2:
                            pe.wait_ge(cross_done, head * (TP - 1) + (t - 1))
                        for c in range(2):
                            mm = pe.matmul(ps[:, 6, :], qkT[:, t, c], state[:, c], start=(c == 0), stop=(c == 1))
                        mm.then_inc(cross_ps, 1)
                        pe.wait_ge(o_done, head * TP + t)
                    for c in range(2):
                        mm = pe.matmul(ps[:, c, :], kt[:, t, c * P:(c + 1) * P], proj[:, t, BW:2 * BW],
                                       start=True, stop=True)
                    mm.then_inc(ds_ps, 1)
                    pe.wait_ge(att_done, head * TP + (t + 1))
                    pe.matmul(ps[:, 5, :], att[:, t % 2], proj[:, t, BW:2 * BW], start=True, stop=True)\
                      .then_inc(o_ps, 1)
                pe.wait_ge(kz_done, head + 1)
                for b in range(NS):
                    for c in range(2):
                        mm = pe.matmul(ps[:, 2 + c, :], kz[:, b, c * P:(c + 1) * P], proj[0:NS, TP, BW:2 * BW],
                                       start=True, stop=True)
                    mm.then_inc(outer_ps, 1)
                    pe.wait_ge(s1_done, head * NS + (b + 1))
                    for c in range(2):
                        mm = pe.matmul(ps[0:NS, 4, :], qz[:, c, b * NS:(b + 1) * NS], sring[:, b % 2, c],
                                       start=(b == 0 and c == 0), stop=(b == NS - 1 and c == 1))
                    mm.then_inc(os_ps, 1)
                for t, rows in enumerate(ROWS):
                    pe.wait_ge(og_done, head * TILES + (t + 1))
                    if t >= 2:
                        pe.wait_ge(oT_done, head * TILES + (t - 1))
                    pe.sem_inc(issued_pe, 1)
                    for c in range(4):
                        mm = pe.transpose(ps[:, 5 + t % 2, c * P:c * P + rows], o[0:rows, t, c * P:(c + 1) * P],
                                          ident[0:rows, 0:rows])
                    mm.then_inc(oT_ps, 1)
                pe.wait_ge(w_ld[1], head * 64 + 32 * (W_HEADS // 2 + 2))
                rows_out = w[:, 1, :].rearrange("p (k n) -> p k n", k=4)
                for t, rows in enumerate(ROWS):
                    pe.wait_ge(oT_done, head * TILES + (t + 1))
                    for half in range(2):
                        n = 2 * t + half
                        if n >= 4:
                            pe.wait_ge(y_done, head * 2 * TILES + (n - 4 + 1 + 1))
                        for c in range(4):
                            mm = pe.matmul(ps[0:rows, n % 4, :], oT[:, c, t * P:t * P + rows],
                                           rows_out[:, c, half * BW:(half + 1) * BW], start=(c == 0), stop=(c == 3))
                        mm.then_inc(y_ps, 1)

            def peer(layer):
                norm(TURN[2 * layer + 1])
                pe.wait_ge(key_ld, 16 * (2 * (layer + 1) + 1))
                pe.wait_ge(hT_done, 2 * TILES * (TURN[2 * layer + 1] + 1))
                for b in range(4):
                    for c in range(4):
                        mm = pe.transpose(ps[:, 4 + b, c * P:(c + 1) * P], keys[:, 4 * b + c], ident[:, :])
                    mm.then_inc(key_ps, 1)
                for n in range(2 * PH):
                    g = W_PEER[layer] + n // 4
                    pe.wait_ge(w_ld[g % 2], 32 * (g // 2 + 1))
                    if n >= 2:
                        pe.wait_ge(q_done, 4 * PH * layer + 2 * (n - 1))
                    for c in range(KC):
                        wq = block_rows(g % 2)[:, c, n % 4 * P:(n % 4 + 1) * P]
                        pe.matmul(ps[:, n % 2, :], wq, hT[:, c, 0:TP * P], start=(c == 0), stop=(c == KC - 1))
                        mm = pe.matmul(ps[:, 2 + n % 2, 0:NS], wq, hT[:, c, TP * P:NTOK],
                                       start=(c == 0), stop=(c == KC - 1))
                    mm.then_inc(q_ps, 1)
                pe.wait_ge(q_done, 4 * PH * (layer + 1))
                pe.wait_ge(key_done, 4 * (layer + 1))
                for m in range(TILES):
                    t = (TP + m) % TILES
                    rows = ROWS[t]
                    if m >= 2:
                        pe.wait_ge(score_done, 4 * (TILES * layer + m - 1))
                    for n in range(2 * PH):
                        mm = pe.matmul(ps[0:rows, 4 * (m % 2) + n // 4, n % 4 * P:(n % 4 + 1) * P],
                                       qT[:, n, t * P:t * P + rows], keyT[:, n], start=True, stop=True)
                    mm.then_inc(score_ps, 1)
                pe.wait_ge(top_done, TILES * layer + 1)
                pe.wait_ge(score_done, 4 * (TILES * layer + 4))
                pe.transpose(ps[:, 6, 0:NS], place_s[0:NS], ident[0:NS, 0:NS])
                pe.transpose(ps[:, 6, NS:2 * NS], gate[0:NS, TP], ident[0:NS, 0:NS]).then_inc(es_ps, 1)
                pe.wait_ge(score_done, 4 * TILES * (layer + 1))
                pe.wait_ge(wgt_done, TILES * layer + 1)
                for b in range(NS):
                    pe.wait_ge(v_ld[b], landed(layer, 0, -1))
                    for half in range(2):
                        mm = pe.matmul(ps[0:NS, 4 + half, :], wgt_s[:, b * NS:(b + 1) * NS],
                                       v_ring[:, b, half * BW:(half + 1) * BW], start=(b == 0), stop=(b == NS - 1))
                    mm.then_inc(v_used, 1)
                for t in range(TP):
                    bank = 2 * (t % 2)
                    if t >= 2:
                        pe.wait_ge(mix_free, TILES * layer + t)
                    for half in range(2):
                        pe.matmul(ps[:, bank + half, :], zeros[:, :], modp[:, 0, half * BW:(half + 1) * BW],
                                  start=True, stop=False)
                    with pe.Fori(0, NE // BATCH) as i:
                        for s in range(BATCH):
                            pe.wait_ge(v_ld[s % RING], i * 32 + landed(layer, t, s // RING))
                            pe.wait_ge(diag_done, i * BATCH + ((TP * layer + t) * NE + s + 1))
                            for half in range(2):
                                mm = pe.matmul(ps[:, bank + half, :], diag[:, s % 4],
                                               v_ring[:, s % RING, half * BW:(half + 1) * BW], start=False, stop=False)
                            mm.then_inc(v_used, 1)
                    for half in range(2):
                        mm = pe.matmul(ps[:, bank + half, :], zeros[:, :], modp[:, 0, half * BW:(half + 1) * BW],
                                       start=False, stop=True)
                    mm.then_inc(mix_ps, 1)

            peer(0)
            ssm_pe(pe, norm, block_rows)
            peer(1)

        @block.vector
        def _(dve):
            link = Steps(dve, steps_v)

            def norm(k, times):
                if k < FINAL:
                    dve.wait_ge(mod_ld, 48 * (k + 1))
                    dve.scalar_tensor_tensor(modp[:, 1], modp[:, 1], 1.0, gain, ALU.add, ALU.mult)
                    link.link(dve.scalar_tensor_tensor(mods[0:NS, 1], mods[0:NS, 1], 1.0, gain[0:NS], ALU.add, ALU.mult))
                else:
                    dve.wait_ge(fin_ld, 16)
                dve.wait_ge(sq_done, TILES * (k + 1))
                dve.tensor_scalar(var[:, :], sq[:, :], 1.0 / D, EPS, ALU.mult, ALU.add).then_inc(var_done, 1)
                dve.wait_ge(rstd_done, times)
                for t, rows in enumerate(ROWS):
                    factor = gain if k == FINAL else (modp if t < TP else mods)[:, 1]
                    ins = dve.scalar_tensor_tensor(h[0:rows, t], x[0:rows, t], rstd[0:rows, t:t + 1], factor[0:rows],
                                                   ALU.mult, ALU.mult)
                    if k == FINAL:
                        ins.then_inc(h_done, 1)
                if k == FINAL:
                    return
                link.link(ins)
                for t, rows in enumerate(ROWS):
                    shift = (modp if t < TP else mods)[0:rows, 0]
                    dve.tensor_tensor(h[0:rows, t], h[0:rows, t], shift, ALU.add).then_inc(h_done, 1)

            dve.memset(sq[:, :], 1.0).then_inc(constv, 1)
            dve.sem_inc(mod_done, 2)
            dve.sem_inc(y_done, 1)
            dve.sem_inc(u_used, BATCH)
            dve.sem_inc(v_used, BATCH)
            dve.wait_ge(c_tanh, 1)
            link.link(dve.scalar_tensor_tensor(cond_t, cond_t, 1.0, cond, ALU.add, ALU.mult))
            dve.tensor_scalar(cond, cond_t, 0.5, None, ALU.mult).then_inc(c_silu, 1)
            dve.wait_ge(cT_ps, 1)
            dve.tensor_copy(condT, ps[:, 0, 0:KC * NC].rearrange("p (c n) -> p c n", c=KC)).then_inc(cT_done, 1)
            dve.wait_ge(tab_ld, 64)
            with dve.Fori(0, ADA_BLOCKS // 2) as i:
                for s in range(2):
                    dve.wait_ge(w_used, 2 * i + (s + 1))
                    part = bias[:, bass.ds((2 * i + s) * BW, BW)]
                    dve.tensor_tensor(part, part, ps[0:NC, 1 + s, :], ALU.add).then_inc(mod_done, 1)
            dve.wait_ge(x_ld, 32)
            norm(0, 1)
            dve.memset(qz, 0.0).then_inc(qz_zero, 1)

            def rotate(rows, t0, t1):
                qk = proj[0:rows, t0:t1, 0:BW].rearrange("p t (s f n) -> p t s f n", s=2, f=2)
                cos, sin = rots[0:rows, t0:t1, 0], rots[0:rows, t0:t1, 1]
                first, second = qk[:, :, :, 0], qk[:, :, :, 1]
                out = qkr[0:rows, t0:t1].rearrange("p t s (f n) -> p t s f n", f=2)
                n = t1 - t0
                a1, b1 = rot1[0:rows, 0:n, 0:2], rot2[0:rows, 0:n, 0:2]
                a2, b2 = rot1[0:rows, 0:n, 2:4], rot2[0:rows, 0:n, 2:4]
                for j in range(n):
                    dve.tensor_tensor(a1[:, j], first[:, j], cos[:, j], ALU.mult)
                    dve.tensor_tensor(b1[:, j], second[:, j], sin[:, j], ALU.mult)
                    dve.tensor_tensor(a2[:, j], second[:, j], cos[:, j], ALU.mult)
                    ins = dve.tensor_tensor(b2[:, j], first[:, j], sin[:, j], ALU.mult)
                link.link(ins)
                for j in range(n):
                    dve.tensor_tensor(out[:, j, :, 0], a1[:, j], b1[:, j], ALU.subtract)
                    ins = dve.tensor_tensor(out[:, j, :, 1], a2[:, j], b2[:, j], ALU.add)
                ins.then_inc(rot_done, 1)

            with dve.Fori(0, HEADS) as head:
                link.loop(head, HEAD_LINKS)
                dve.wait_ge(y_done, head * 2 * TILES + 1)
                dve.tensor_scalar(mask.unsqueeze(1), masks[:, bass.ds(head, 1), :], 1.0, None, ALU.mult)
                link.link(dve.tensor_scalar(cols.unsqueeze(1), colss[:, bass.ds(head, 1), :], 1.0, None, ALU.mult))
                dve.wait_ge(proj_done, head * 3 * TILES + TILES)
                rotate(P, 0, TP)
                dve.wait_ge(rot_done, head * 2 + 1)
                rotate(NS, TP, TILES)
                dve.wait_ge(rot_done, head * 2 + 2)
                dve.tensor_scalar(kt, qkr[:, 0:TP, 1], cols[:, 1:2], None, ALU.mult).then_inc(kt_done, 1)
                dve.tensor_tensor(kz, spread(qkr[0:NS, TP, 1], 1, NS), spread(ident[0:NS, 0:NS], 2, DK), ALU.mult)\
                   .then_inc(kz_done, 1)
                dve.wait_ge(state_free, head + 1)
                for t in range(TP):
                    dve.wait_ge(att_ps, head * TP + (t + 1))
                    dve.tensor_tensor(att[:, t % 2], ps[:, 7, 0:P], mask, ALU.mult).then_inc(att_done, 1)
                    dve.wait_ge(ds_ps, head * TP + (t + 1))
                    if t:
                        dve.wait_ge(cross_ps, head * (TP - 1) + t)
                        for c in range(2):
                            ins = dve.scalar_tensor_tensor(state[:, c], state[:, c], cols[:, 2:3], ps[:, c, :],
                                                           ALU.mult, ALU.add)
                    else:
                        ins = dve.tensor_copy(state, ps[:, 0:2, :])
                    ins.then_inc(state_done, 1)
                    dve.wait_ge(o_ps, head * TP + (t + 1))
                    if t:
                        dve.wait_ge(cross_done, head * (TP - 1) + t)
                        dve.tensor_tensor(o[:, t], ps[:, 5, :], cross[:, t % 2], ALU.add).then_inc(o_done, 1)
                    else:
                        dve.tensor_copy(o[:, t], ps[:, 5, :]).then_inc(o_done, 1)
                    dve.wait_ge(state_done, head * TP + (t + 1))
                for b in range(NS):
                    dve.wait_ge(s0_ld[b % 2], head * (NS // 2) * 16 + 16 * (b // 2 + 1))
                    dve.wait_ge(outer_ps, head * NS + (b + 1))
                    for c in range(2):
                        ins = dve.scalar_tensor_tensor(sring[:, b % 2, c], sring[:, b % 2, c], cols[:, 3:4],
                                                       ps[:, 2 + c, :], ALU.mult, ALU.add)
                    ins.then_inc(s1_done, 1)
                dve.wait_ge(os_ps, head * NS + NS)
                link.link(dve.tensor_copy(o[0:NS, TP], ps[0:NS, 4, :]))
                dve.wait_ge(o_done, head * TP + TP)
                for t, rows in enumerate(ROWS):
                    ins = dve.bn_stats(stats[0:rows, t], o[0:rows, t])
                link.link(ins)
                dve.sem_inc(issued_v, 1)
                for t, rows in enumerate(ROWS):
                    ins = dve.bn_aggr(meanv[0:rows, t], stats[0:rows, t])
                link.link(ins)
                for a, b, rows in ((0, TP, P), (TP, TILES, NS)):
                    ins = dve.tensor_scalar(var[0:rows, a:b], meanv[0:rows, a:b, 1], EPS, None, ALU.add)
                ins.then_inc(var_done, 1)
                dve.wait_ge(rstd_done, head + 2)
                for t, rows in enumerate(ROWS):
                    dve.tensor_scalar(o[0:rows, t], o[0:rows, t], meanv[0:rows, t, 0:1], rstd[0:rows, t:t + 1],
                                      ALU.subtract, ALU.mult)
                    if t == 0:
                        dve.wait_ge(g_tanh, head * TILES + TILES)
                    ins = dve.scalar_tensor_tensor(sil[0:rows, t], sil[0:rows, t], 1.0, proj[0:rows, t, 2 * BW:3 * BW],
                                                   ALU.add, ALU.mult)
                link.link(ins)
                for t, rows in enumerate(ROWS):
                    dve.scalar_tensor_tensor(o[0:rows, t], sil[0:rows, t], 0.5, o[0:rows, t], ALU.mult, ALU.mult)\
                       .then_inc(og_done, 1)
                for t, rows in enumerate(ROWS):
                    mod = (modp if t < TP else mods)[0:rows, 2]
                    for half in range(2):
                        dve.wait_ge(y_ps, head * 2 * TILES + (2 * t + half + 1))
                        dve.tensor_tensor(cross[0:rows, half], ps[0:rows, (2 * t + half) % 4, :],
                                          mod[:, half * BW:(half + 1) * BW], ALU.mult).then_inc(y_done, 1)
                    dve.wait_ge(y_done, head * 2 * TILES + (2 * t + 2 + 1))
                    xt = x[0:rows, t].rearrange("p (a n) -> p a n", a=2)
                    link.link(dve.tensor_tensor(xt, xt, cross[0:rows], ALU.add))
            link.end(HEADS)
            dve.sem_inc(x_ready, 1)

            def best_of(layer, m):
                t = (TP + m) % TILES
                rows = slice(0, ROWS[t])
                sides, sides2 = score[rows], score2[rows]
                dve.wait_ge(score_done, 4 * (TILES * layer + m + 1))

                def top(values, rest, found, index, n):
                    for e in range(n):
                        ins = dve.max(found[:, e, 0:8], values[:, e])
                    link.link(ins)
                    for e in range(n):
                        dve.max_index(index[:, e, 0:8], found[:, e, 0:8], values[:, e])
                        ins = dve.match_replace(rest[:, e], found[:, e, 0:8], values[:, e], LOWEST)
                    link.link(ins)
                    for e in range(n):
                        ins = dve.max(found[:, e, 8:16], rest[:, e])
                    link.link(ins)
                    for e in range(n):
                        ins = dve.max_index(index[:, e, 8:16], found[:, e, 8:16], rest[:, e])
                    link.link(ins)

                top(sides, sides2, best[rows], besti[rows], 2 * PH)
                dve.tensor_copy(bestf[rows], besti[rows])
                by_side = best[rows].rearrange("p (e s) k -> p e s k", s=2)
                link.link(dve.tensor_tensor(cand[rows].rearrange("p e (a b) -> p e a b", a=TOPK),
                                            spread(by_side[:, :, 0], 3, TOPK), spread(by_side[:, :, 1], 2, TOPK), ALU.add))
                top(cand[rows], cand2[rows], topv[rows], topi[rows], PH)
                gates = gate[rows, t].rearrange("p (e k) -> p e k", e=PH)
                link.link(dve.tensor_tensor(gates, topv[rows], spread(topv[rows, :, 0], 2, TOPK), ALU.subtract))
                dve.tensor_copy(topv[rows], gates).then_inc(e_sub, 1)
                flat = cand2[rows].rearrange("p e k -> p (e k)")
                picked = topi[rows].rearrange("p e k -> p (e k)")
                n1, n2 = flat[:, 0:NE].bitcast(U32), flat[:, NE:2 * NE].bitcast(U32)
                f1, f2 = flat[:, 2 * NE:3 * NE], flat[:, 3 * NE:4 * NE]
                dve.tensor_scalar(n1, picked, 4, None, ALU.logical_shift_right)
                link.link(dve.tensor_scalar(n2, picked, TOPK - 1, None, ALU.bitwise_and))
                dve.tensor_copy(f1, n1)
                link.link(dve.tensor_copy(f2, n2))
                keys_of = bestf[rows].rearrange("p (e s) k -> p e s k", s=2)
                hit = cand[rows].rearrange("p e (k a) -> p (e k) a", k=TOPK)
                hit4 = cand[rows].rearrange("p e (k a) -> p e k a", k=TOPK)
                for side, f, out in ((0, f1, side1), (1, f2, side2)):
                    link.link(dve.tensor_tensor(hit, spread(f, 2, TOPK), spread(lane[rows], 1, NE), ALU.is_equal))
                    link.link(dve.tensor_tensor(hit4, hit4, spread(keys_of[:, :, side], 2, TOPK), ALU.mult))
                    link.link(dve.tensor_reduce(out[rows], hit, AX.X, ALU.add))
                link.link(dve.tensor_scalar(side1[rows], side1[rows], float(NK), float(layer * EXPERTS), ALU.mult, ALU.add))
                if t == TP:
                    dve.tensor_tensor(place_s[rows], side1[rows], side2[rows], ALU.add)
                else:
                    link.link(dve.tensor_tensor(place[rows], side1[rows], side2[rows], ALU.add))
                    dve.tensor_copy(eidx[rows, t], place[rows])
                dve.wait_ge(e_exp, TILES * layer + m + 1)
                link.link(dve.tensor_reduce(total[rows], topv[rows], AX.X, ALU.add))
                link.link(dve.reciprocal(rtotal[rows], total[rows]))
                dve.tensor_tensor(gates, topv[rows], spread(rtotal[rows], 2, TOPK), ALU.mult).then_inc(top_done, 1)
                dve.wait_ge(top_done, TILES * layer + m + 1)

            def weights(layer, n, a, a2, gates, out):
                link.link(dve.tensor_tensor(a2, a, a, ALU.mult))
                link.link(dve.tensor_scalar(a2, a2, GELU_A, 1.0, ALU.mult, ALU.add))
                dve.tensor_tensor(a2, a2, a, ALU.mult).then_inc(gelu_in, 1)
                dve.wait_ge(gelu_tanh, n)
                link.link(dve.scalar_tensor_tensor(a2, a2, 1.0, a, ALU.add, ALU.mult))
                dve.scalar_tensor_tensor(out, a2, 0.5, gates, ALU.mult, ALU.mult).then_inc(wgt_done, 1)

            def mixed(layer, t):
                rows = ROWS[t]
                bank = 4 if t == TP else 2 * (t % 2)
                mod = (modp if t < TP else mods)[0:rows, 2]
                link.link(dve.tensor_tensor(gated[0:rows], ps[0:rows, bank:bank + 2, :],
                                            mod.rearrange("p (a n) -> p a n", a=2), ALU.mult))
                dve.sem_inc(mix_free, 1)
                xt = x[0:rows, t].rearrange("p (a n) -> p a n", a=2)
                link.link(dve.tensor_tensor(xt, xt, gated[0:rows], ALU.add))

            def peer(layer):
                k = 2 * layer + 1
                norm(k, PEER_ROOT[layer])
                if layer == 0:
                    dve.wait_ge(key_ld, 48)
                for m in range(TILES):
                    best_of(layer, m)
                dve.memset(wgt_s, 0.0).then_inc(wz_zero, 1)
                dve.wait_ge(es_ps, layer + 1)
                dve.tensor_copy(eidx_s, ps[:, 6, 0:NS]).then_inc(es_done, 1)
                dve.tensor_copy(gate_s, ps[:, 6, NS:2 * NS]).then_inc(es_done, 1)
                for b in range(NS):
                    dve.wait_ge(hb_ld[b % 2], 16 * (NS // 2 * layer + b // 2 + 1))
                    dve.wait_ge(u_ld[b], landed(layer, 0, -1))
                    dve.tensor_tensor_reduce(u_ring[:, b], u_ring[:, b], hb[:, b % 2], 1.0, 0.0, ALU.mult, ALU.add,
                                             acts_s[:, b:b + 1]).then_inc(u_used, 1)
                dve.wait_ge(es_done, 2 * (layer + 1))
                dve.wait_ge(wz_zero, layer + 1)
                dve.wait_ge(u_used, BATCH + gather_of(layer, 0))
                weights(layer, TILES * layer + 1, acts_s, acts_s2, gate_s, wgt_s[:, ::NS + 1])
                for t in range(TP):
                    with dve.Fori(0, NE // BATCH) as i:
                        link.loop(i, 1)
                        for s in range(BATCH):
                            dve.wait_ge(u_ld[s % RING], i * 32 + landed(layer, t, s // RING))
                            dve.tensor_tensor_reduce(u_ring[:, s % RING], u_ring[:, s % RING], h[:, t], 1.0, 0.0,
                                                     ALU.mult, ALU.add, dots[:, s:s + 1]).then_inc(u_used, 1)
                        dve.wait_ge(u_used, i * BATCH + (gather_of(layer, t) + 2 * BATCH))
                        link.link(dve.tensor_scalar(acts[:, bass.ds(i * BATCH, BATCH)], dots, 1.0, None, ALU.mult))
                    link.end(NE // BATCH)
                    if t >= 2:
                        dve.wait_ge(diag_done, (TP * layer + t - 1) * NE)
                    weights(layer, TILES * layer + t + 2, acts, acts2, gate[:, t], wgt[:, t % 2])
                    if t == 0:
                        dve.wait_ge(v_used, BATCH + gather_of(layer, 0))
                        mixed(layer, TP)
                    else:
                        dve.wait_ge(mix_ps, TP * layer + t)
                        mixed(layer, t - 1)
                dve.wait_ge(mix_ps, TP * (layer + 1))
                mixed(layer, TP - 1)
                dve.sem_inc(x_ready, 1)

            peer(0)
            ssm_dve(dve, link, norm)
            peer(1)
            norm(FINAL, NORMS)


_INS = ['x_prompt', 'x_sample', 'c_prompt', 'c_sample', 'state_ret', 'state_ssm_re', 'state_ssm_im', 'norm_g', 'final_g',
        'w_ada', 'b_ada', 'ret_w_in', 'ret_w_out', 'ssm_w_in', 'ssm_lam_re', 'ssm_lam_im', 'ssm_log_dt', 'ssm_b_re',
        'ssm_b_im', 'ssm_c_re', 'ssm_c_im', 'ssm_d', 'ssm_w_glu', 'peer_w_q', 'peer_key1', 'peer_key2', 'peer_u', 'peer_v']
_OUTS = [((1, 512, 1024), 'float32'), ((8, 1, 1024), 'float32'), ((1, 1, 4, 256, 512), 'float32'),
         ((1, 8, 4, 256, 512), 'float32'), ((1, 1, 64, 64), 'float32'), ((1, 1, 64, 64), 'float32'),
         ((1, 8, 64, 64), 'float32'), ((1, 8, 64, 64), 'float32')]


def _tables():
    import numpy as _np
    f = _np.float32
    half = DK // 2
    inv = f(10000.0) ** (-_np.arange(half, dtype=f) / f(half))
    pos = _np.zeros((TILES, P), f)
    pos[:TP] = _np.arange(TP * P, dtype=f).reshape(TP, P)
    pos[TP] = 4096
    angle = (pos[:, :, None] * inv[None, None, :]).astype(f).astype(_np.float64)
    rot = _np.zeros((P, TILES, 2, 2, half), f)
    for n, fn in enumerate((_np.cos, _np.sin)):
        value = fn(angle).astype(f).transpose(1, 0, 2)
        rot[:, :, n, 0] = value
        rot[:, :, n, 1] = value * f(DK ** -0.5)
    lg = _np.log1p(-_np.exp2(-5.0 - _np.arange(HEADS, dtype=_np.float64)))
    i = _np.arange(P, dtype=_np.float64)
    diff = i[None, :] - i[:, None]
    decay = _np.where(diff[:, None, :] >= 0, _np.exp(lg[None, :, None] * _np.maximum(diff, 0)[:, None, :]), 0.0)
    cols = _np.zeros((P, HEADS, 4), _np.float64)
    cols[:, :, 0] = _np.exp(lg[None, :] * (i[:, None] + 1))
    cols[:, :, 1] = _np.exp(lg[None, :] * (P - 1 - i[:, None]))
    cols[:, :, 2] = _np.exp(lg * P)[None, :]
    cols[:, :, 3] = _np.exp(lg)[None, :]
    lane = _np.tile(_np.arange(TOPK, dtype=f), (P, 1))
    return {"rot_tab": rot, "decay_tab": decay.astype(f),
            "decay_cols": cols.astype(f), "lane_tab": lane}


def kernel(**inputs):
    import numpy as _np
    import concourse.bacc as _bacc
    from concourse import mybir as _mybir
    from concourse.bass_utils import run_bass_kernel_spmd as _run

    nc = _bacc.Bacc("TRN2", target_bir_lowering=False, num_devices=1)
    arrays, args = {}, []
    given = {name: _np.ascontiguousarray(inputs[name]) for name in _INS}
    given.update(_tables())
    for name, a in given.items():
        arrays[f"in_{name}_dram"] = a
        args.append(nc.dram_tensor(f"in_{name}_dram", a.shape, _mybir.dt.from_np(a.dtype), kind="ExternalInput").ap())
    for i, (shape, dtype) in enumerate(_OUTS):
        dt = _mybir.dt.from_np(_np.dtype(dtype))
        args.append(nc.dram_tensor(f"out_{i}_dram", shape, dt, kind="ExternalOutput").ap())
    build(nc, *args)
    r = _run(nc, [arrays], core_ids=[0])
    return tuple(r.results[0][f"out_{i}_dram"] for i in range(len(_OUTS)))
```

```python
from contextlib import ExitStack

import concourse.bass as bass
from concourse import mybir

F32 = mybir.dt.float32
U32 = mybir.dt.uint32
I32 = mybir.dt.int32
ALU = mybir.AluOpType
ACT = mybir.ActivationFunctionType
AX = mybir.AxisListType

D = 1024
P = 128
KC = D // P
TP = 4
NS = 8
TILES = TP + 1
NTOK = TP * P + NS
ROWS = [P] * TP + [NS]
NC = NS + 1
LAYERS = 2
BW = 512
HEADS, DK, DV = 4, 256, 512
PH, NK, TOPK = 8, 128, 16
NE = PH * TOPK
EXPERTS = NK * NK
RING = 8
BATCH = 2 * RING
ALONE = 2 * BATCH
EARLY = 3 * BATCH
G, GP, NST = 64, 16, 64
BL = 8
NB = TP * P // BL
PAIRS = G // 2
EPS = 1e-6
LOWEST = -3.0e38
ADA_BLOCKS = LAYERS * 6 * D // BW
HEAD_BLOCKS = 4
W_HEADS = ADA_BLOCKS
W_PEER = [W_HEADS + HEADS * HEAD_BLOCKS, W_HEADS + HEADS * HEAD_BLOCKS + 4 + 2 + 4]
W_SSM = W_PEER[0] + 4
W_GLU = W_SSM + 2
GELU_A, GELU_C = 0.044715, 0.7978845608028654


class Steps:

    def __init__(self, eng, sem):
        self.eng, self.sem, self.n, self.i, self.per = eng, sem, 0, None, 0

    def link(self, ins):
        ins.then_inc(self.sem, 1)
        self.n += 1
        self.eng.wait_ge(self.sem, self.value())

    def value(self):
        return self.n if self.i is None else self.i * self.per + self.n

    def loop(self, i, per):
        self.i, self.per, self.start = i, per, self.n

    def end(self, times):
        assert self.n - self.start == self.per, (self.n - self.start, self.per)
        self.n, self.i = self.start + times * self.per, None
HEAD_LINKS = 12
FINAL = 2 * LAYERS
NORMS = FINAL + 1 + HEADS
PEER_ROOT = [2 + HEADS, NORMS - 1]
TURN = [0, 1, 2, 4, 5]


class Cut:

    def __init__(self, whole, at=0):
        self.whole, self.at = whole, at

    def __call__(self, *shape, dtype=F32):
        n = 1
        for s in shape:
            n *= s
        view = self.whole[:, self.at:self.at + n]
        self.at += n
        assert self.at <= self.whole.shape[1], self.at
        if dtype != F32:
            view = view.bitcast(dtype)
        names = "abcd"[:len(shape)]
        if len(shape) > 1:
            view = view.rearrange(f"p ({' '.join(names)}) -> p {' '.join(names)}", **dict(zip(names, shape)))
        return view


def spread(ap, axis, n):
    shape = list(ap.shape)
    shape.insert(axis, n)
    return ap.unsqueeze(axis).to_broadcast(shape)


def build(nc, x_prompt, x_sample, c_prompt, c_sample, state_ret, state_ssm_re, state_ssm_im,
          norm_g, final_g, w_ada, b_ada, ret_w_in, ret_w_out, ssm_w_in, ssm_lam_re, ssm_lam_im, ssm_log_dt,
          ssm_b_re, ssm_b_im, ssm_c_re, ssm_c_im, ssm_d, ssm_w_glu, peer_w_q, peer_key1, peer_key2, peer_u, peer_v,
          rot_tab, decay_tab, decay_cols, lane_tab,
          y_prompt, y_sample, ret_prompt, ret_sample, re_prompt, im_prompt, re_sample, im_sample):
    with ExitStack() as ctx:
        def sb(name, shape, dtype=F32):
            return ctx.enter_context(nc.sbuf_tensor(name, shape, dtype))

        def sem(name):
            return ctx.enter_context(nc.semaphore(name))

        mod_d = nc.dram_tensor("mod_d", (NC, LAYERS * 6 * D), F32).ap()
        hs_d = nc.dram_tensor("hs_d", (LAYERS, NS, D), F32).ap()
        u_d = nc.dram_tensor("u_d", (TP * P + NS, D), F32).ap()
        z_d = nc.dram_tensor("z_d", (TP * P + NS, D), F32).ap()
        k_d = nc.dram_tensor("k_d", (G, GP, 2 * BL - 1, GP), F32).ap()

        x = sb("x", [P, TILES, D])
        h = sb("h", [P, TILES, D])
        hT = sb("hT", [P, KC, NTOK])
        modp = sb("modp", [P, 3, D])
        mods = sb("mods", [P, 3, D])
        w = sb("w", [P, 2, KC * BW])
        ident = sb("ident", [P, P])
        zeros = sb("zeros", [P, P])
        sq = sb("sq", [P, TILES])
        var = sb("var", [P, TILES])
        rstd = sb("rstd", [P, TILES])
        mhalf = sb("mhalf", [P, TILES])
        u_ring = w[:, :, :].rearrange("p s (r n) -> p (s r) n", n=D)
        lane = sb("lane", [P, TOPK])
        arena = sb("arena", [P, 24064])
        ps = ctx.enter_context(nc.psum_tensor("ps", [P, 8, BW], F32))

        gain = arena[:, 0:D]

        cut = Cut(arena)
        bias = cut(LAYERS * 6 * D)[0:NC]
        cut = Cut(arena, LAYERS * 6 * D)
        cond, cond_t = cut(D)[0:NC], cut(D)[0:NC]
        condT = cut(KC, NC)
        cut = Cut(arena)
        proj = cut(TILES, 3 * BW)
        qkr = cut(TILES, 2, DK)
        qkT = cut(TP, 4, P)
        cut.at -= TP * 4 * P
        oT = cut(4, NTOK)
        qz = cut(2, NS * NS)
        state = cut(2, DV)
        kt = cut(TP, DK)
        kz = cut(NS, DK)[0:NS]
        sring = cut(2, 2, DV)
        att = cut(2, P)
        cross = cut(2, DV)
        mask = cut(P)
        cols = cut(4)
        stats = cut(TILES, 6)
        meanv = cut(TILES, 2)
        masks = cut(HEADS, P)
        colss = cut(HEADS, 4)
        rots = cut(TILES, 2, 2, P)
        cut = Cut(h[:, :, :].rearrange("p t n -> p (t n)"))
        o = cut(TILES, DV)
        sil = cut(TILES, DV)
        rot1 = o[:, 0:4, :].rearrange("p t (a n) -> p t a n", a=4)
        rot2 = sil[:, 0:4, :].rearrange("p t (a n) -> p t a n", a=4)
        cut = Cut(arena)
        hb = cut(2, D)
        cut.at = 0
        qT = cut(2 * PH, NTOK)
        v_ring = cut(RING, D)
        cut.at -= RING * D
        keys = cut(2 * PH, P)
        cut.at += RING * D - 2 * PH * P
        keyT = cut(2 * PH, P)
        gated = cut(2, BW)
        picks = cut(4, NE)
        acts = cut(NE)
        acts2 = cut(NE)
        wgt = cut(2, NE)
        diag = cut(4, P)
        best = cut(2 * PH, TOPK)
        besti = cut(2 * PH, TOPK, dtype=U32)
        bestf = cut(2 * PH, TOPK)
        topv = cut(PH, TOPK)
        topi = cut(PH, TOPK, dtype=U32)
        place = cut(NE)
        place_s = cut(NE)
        side1 = cut(NE)
        side2 = cut(NE)
        eidx = cut(TILES, NE, dtype=U32)
        gate = cut(TILES, NE)
        eidx_s = cut(NS, dtype=U32)
        gate_s = cut(NS)
        stage_u = cut(2, RING, dtype=U32)
        stage_v = cut(2, RING, dtype=U32)
        wgt_s = cut(NS * NS)

        cut = Cut(hT[:, :, :].rearrange("p c n -> p (c n)"))
        score = cut(2 * PH, NK)
        cand = cut(PH, TOPK * TOPK)
        total = cut(PH)
        rtotal = cut(PH)
        dots = cut(BATCH)
        acts_s = cut(NS)
        acts_s2 = cut(NS)

        x_ld, c_ld, tab_ld, mod_ld, fin_ld = sem("x_ld"), sem("c_ld"), sem("tab_ld"), sem("mod_ld"), sem("fin_ld")
        w_ld = [sem("w_ld0"), sem("w_ld1")]
        w_used = sem("w_used")
        consts, constv = sem("consts"), sem("constv")
        x_ready, sq_done, var_done, rstd_done = sem("x_ready"), sem("sq_done"), sem("var_done"), sem("rstd_done")
        h_done, hT_ps, hT_done = sem("h_done"), sem("hT_ps"), sem("hT_done")
        c_tanh, c_silu, cT_ps, cT_done = sem("c_tanh"), sem("c_silu"), sem("cT_ps"), sem("cT_done")
        mod_done, mod_st, bias_row = sem("mod_done"), sem("mod_st"), sem("bias_row")
        proj_ps, proj_done, rot_done, kt_done = sem("proj_ps"), sem("proj_done"), sem("rot_done"), sem("kt_done")
        kz_done, qk_ps, qk_done, qz_zero = sem("kz_done"), sem("qk_ps"), sem("qk_done"), sem("qz_zero")
        att_ps, att_done, cross_ps, cross_done = sem("att_ps"), sem("att_done"), sem("cross_ps"), sem("cross_done")
        o_ps, o_done, ds_ps, state_done = sem("o_ps"), sem("o_done"), sem("ds_ps"), sem("state_done")
        state_st, state_free = sem("state_st"), sem("state_free")
        s0_ld = [sem("s0_ld0"), sem("s0_ld1")]
        s1_st = [sem("s1_st0"), sem("s1_st1")]
        outer_ps, s1_done, os_ps = sem("outer_ps"), sem("s1_done"), sem("os_ps")
        g_tanh, og_done, oT_ps, oT_done = sem("g_tanh"), sem("og_done"), sem("oT_ps"), sem("oT_done")
        y_ps, y_done = sem("y_ps"), sem("y_done")
        key_ld, key_ps, key_done = sem("key_ld"), sem("key_ps"), sem("key_done")
        q_ps, q_done, score_ps, score_done, top_done = (
            sem("q_ps"), sem("q_done"), sem("score_ps"), sem("score_done"), sem("top_done"))
        e_exp, e_sub = sem("e_exp"), sem("e_sub")
        es_ps, es_done = sem("es_ps"), sem("es_done")
        hs_st, hb_ld = sem("hs_st"), [sem("hb_ld0"), sem("hb_ld1")]
        u_ld = [sem(f"u_ld{s}") for s in range(RING)]
        v_ld = [sem(f"v_ld{s}") for s in range(RING)]
        u_used, v_used = sem("u_used"), sem("v_used")
        mix_free = sem("mix_free")
        issued = sem("issued")
        gelu_in, gelu_tanh, wgt_done, diag_done = sem("gelu_in"), sem("gelu_tanh"), sem("wgt_done"), sem("diag_done")
        mix_ps, wz_zero = sem("mix_ps"), sem("wz_zero")
        out_st = sem("out_st")
        steps_v, steps_p = sem("steps_v"), sem("steps_p")
        def slot_free(n):
            return n + BATCH - RING + 1

        def gather_of(layer, tile):
            return layer * (NS + TP * NE) + tile * NE

        def landed(layer, tile, batch):
            return 16 * (layer * (1 + TP * NE // RING) + tile * NE // RING + batch + 1)

        def parameters(whole):
            cut = Cut(whole)
            return (cut(2, PAIRS, GP),
                    cut(2, PAIRS, GP),
                    cut(2, BL + 1, PAIRS),
                    cut(2, BL, PAIRS),
                    cut(2, 2, PAIRS),
                    cut(2, 2, PAIRS))

        PARAMS = 4 * PAIRS * GP + 2 * (2 * BL + 1) * PAIRS + 8 * PAIRS
        par_d = nc.dram_tensor("par_d", (P, PARAMS), F32).ap()
        cut = Cut(arena, LAYERS * 6 * D + 2 * D + KC * NC)
        par0 = cut(PARAMS)
        bb0, cT0, pw0, rpw0, stepA0, oneA0 = parameters(par0)
        tiny = [cut(P)[0:PAIRS] for _ in range(18)]
        craw = cut(2, 8, 2, NST)
        braw = cut(2, PAIRS, GP)
        disc = cut(4, PAIRS)
        part0 = cut(2, 2, PAIRS)
        ones = cut(NC)[0:1]
        wtmp0 = hT[:, :, :].rearrange("p c n -> p (c n)")[:, 0:4 * D].rearrange("p (k q t n) -> p k q t n", k=4, q=8, t=BL)
        cut = Cut(h[:, :, :].rearrange("p t n -> p (t n)"))
        dskip = cut(G, GP)
        kk = cut(G, GP)
        wb0 = cut(2, 8, BL, GP)
        ktmp = cut(D).rearrange("p (q s n) -> p s q n", s=2, n=GP)
        cut = Cut(arena, D)
        region = cut(8 * D)
        uT = cut(G, NB + 2 * NS)
        hh = cut(2, PAIRS, NB + NS)
        par = cut(PARAMS)
        bb, cT, pw, rpw, stepA, oneA = parameters(par)
        part = cut(2, 2, PAIRS)
        wtmp = Cut(hh.rearrange("p c q n -> p (c q n)"))(4, 8, BL, GP)
        cut = Cut(region)
        ublk = cut(BL, G, GP)[0:NB + 2 * NS]
        ublk_rows = region[0:NB + 2 * NS, :]
        cut.at = 0
        wbT = cut(4, 8, 2, P)
        cut.at = 0
        ca = cut(2, 2 * 8, BL, GP)
        ca = [ca[:, c].rearrange("p (k q) t n -> p k q t n", k=2) for c in range(2)]
        yc = cut(2, BL * 16 * GP)
        yc = [yc[:, c].rearrange("p (t g o) -> p t g o", t=BL, g=16) for c in range(2)]
        w_flat = w[:, :, :].rearrange("p s n -> p (s n)")
        wb = [Cut(w_flat, c * 2 * D)(2, 8, BL, GP) for c in range(4)]
        toep = Cut(w_flat)(4, 16, P)
        cut = Cut(hT[:, :, :].rearrange("p c n -> p (c n)"))
        hs = cut(NB + 1, 2, PAIRS)
        cut.at = 0
        ugroup = cut(2, 16, BL * GP)
        cut.at = 0
        catmp = cut(2, 8, BL, GP)
        yc2 = cut(BL, 16, GP)
        cut = Cut(h[:, :, :].rearrange("p t n -> p (t n)"))
        s0l = cut(2, NS, P)[0:PAIRS]
        s0t = cut(NS, 2, PAIRS)
        snew = cut(NS, 2, PAIRS)
        slast = cut(2, P)[0:PAIRS]
        p1_ld, p2_ld, p3_ld, h2_ld = sem("p1_ld"), sem("p2_ld"), sem("p3_ld"), sem("h2_ld")
        kzero_st, ud_st, ub_ld, ub_zero = sem("kzero_st"), sem("ud_st"), sem("ub_ld"), sem("ub_zero")
        u_ps, u_done, kd_st, k_done = sem("u_ps"), sem("u_done"), sem("kd_st"), sem("k_done")
        k_ps, ug_done = sem("k_ps"), sem("ug_done")
        t_ld = [sem(f"t_ld{c}") for c in range(4)]
        zd_st = [sem("zd_st0"), sem("zd_st1")]
        d_ld, par_done, par_st, par_ld, kwb_done = sem("d_ld"), sem("par_done"), sem("par_st"), sem("par_ld"), sem("kwb_done")
        z_done, z_ld, so_st, so_done = sem("z_done"), sem("z_ld"), sem("so_st"), sem("so_done")
        sin_in, sin_done, disc_done, disc_ps = sem("sin_in"), sem("sin_done"), sem("disc_done"), sem("disc_ps")
        cT_ps2, cT_done2, s0_ps, s0_done = sem("cT_ps2"), sem("cT_done2"), sem("s0_ps"), sem("s0_done")
        uT_ps, uT_done, wb_done, wb_ps, wb_T = sem("uT_ps"), sem("uT_done"), sem("wb_done"), sem("wb_ps"), sem("wb_T")
        b_ps, b_done, scan_done, hh_done, ca_done = sem("b_ps"), sem("b_done"), sem("scan_done"), sem("hh_done"), sem("ca_done")
        yb_ps, yb_done, zg_in, zg_tanh = sem("yb_ps"), sem("yb_done"), sem("zg_in"), sem("zg_tanh")
        fin_ps, glu_ps, glu_tanh, glu_done = (
            sem("fin_ps"), sem("glu_ps"), sem("glu_tanh"), sem("glu_done"))
        GLU_USED = [2 * TILES, 2 * TILES]
        PROMPT = TP * P

        pairs = "(q s) n -> q (s n)"

        def parameter_loads(sp):
            sp.dma_start(tiny[0], ssm_lam_re[0].rearrange(pairs, s=2)).then_inc(p1_ld, 16)
            sp.dma_start(tiny[1], ssm_lam_im[0].rearrange(pairs, s=2)).then_inc(p1_ld, 16)
            sp.dma_start(tiny[2][:, 0:2], ssm_log_dt[0].rearrange("(q s) -> q s", s=2)).then_inc(p1_ld, 16)

        def more_parameter_loads(sp):
            for c, src in enumerate((ssm_c_re, ssm_c_im)):
                for twice in range(2):
                    sp.dma_start(craw[:, c, :, twice], src[0].rearrange("(a g) o n -> (g o) a n", a=8)).then_inc(p2_ld, 16)
            for c, src in enumerate((ssm_b_re, ssm_b_im)):
                sp.dma_start(braw[:, c], src[0].rearrange("(q s) n i -> (s n) q i", s=2)).then_inc(p3_ld, 16)
            sp.wait_ge(consts, 4)
            rows = k_d.rearrange("g i j o -> (g i) (j o)")[:, 0:(BL - 1) * GP].rearrange("(a b) n -> b a n", b=P)
            sp.dma_start(rows, spread(zeros[:, 0:(BL - 1) * GP], 1, G * GP // P)).then_inc(kzero_st, 16)
            sp.dma_start(dskip.rearrange("p g n -> p (g n)"),
                         ssm_d[0].rearrange("(a g) n -> a (g n)", a=1).to_broadcast([P, D])).then_inc(d_ld, 16)

        def kernels_out(sp):
            sp.wait_ge(k_done, 1)
            sp.wait_ge(kzero_st, 16)
            for t in range(BL):
                sp.dma_start(k_d.rearrange("g i j o -> i g j o")[:, :, 2 * BL - 2 - t, :],
                             kk[t * GP:(t + 1) * GP]).then_inc(kd_st, 16)

        def ssm_sync(sp, load_block, columns, modulation):
            sp.wait_ge(u_used, BATCH + gather_of(0, TP) + NS)
            for b in range(2):
                load_block(b, columns(b, ssm_w_in[0], b * BW))
            modulation(2)
            sp.dma_start(par, par_d).then_inc(par_ld, 16)
            sp.wait_ge(u_done, 2 * TILES)
            sp.dma_start(u_d[0:PROMPT].rearrange("(t p) n -> p t n", p=P), h[:, 0:TP, :]).then_inc(ud_st, 16)
            sp.dma_start(u_d[PROMPT:NTOK], h[0:NS, TP, :]).then_inc(ud_st, 16)
            sp.wait_ge(ud_st, 32)
            sp.wait_ge(ub_zero, 1)
            sp.dma_start(ublk_rows[0:NB], u_d[0:PROMPT].rearrange("(m t) n -> m (t n)", t=BL)).then_inc(ub_ld, 16)
            sp.dma_start(ublk_rows[NB:NB + NS, 0:D], u_d[PROMPT:NTOK]).then_inc(ub_ld, 16)
            sp.dma_start(ublk_rows[NB + NS:NB + 2 * NS, (BL - 1) * D:BL * D], u_d[PROMPT:NTOK]).then_inc(ub_ld, 16)
            for c, src in enumerate((state_ssm_re, state_ssm_im)):
                sp.dma_start(s0l[:, c], src[0].rearrange("b (q s) n -> q b (s n)", s=2)).then_inc(h2_ld, 16)
            sp.wait_ge(kd_st, 16 * BL)
            sp.wait_ge(wb_ps, 16)
            for c in range(4):
                for t in range(BL):
                    src = k_d[16 * c:16 * (c + 1)].rearrange("g i j o -> i g (j o)")
                    sp.dma_start(toep[t * GP:(t + 1) * GP, c], src[:, :, (BL - 1 - t) * GP:(2 * BL - 1 - t) * GP])\
                      .then_inc(t_ld[c], 16)
            sp.wait_ge(so_done, 5)
            for c, (prompt, sample) in enumerate(((re_prompt, re_sample), (im_prompt, im_sample))):
                sp.dma_start(prompt[0, 0].rearrange(pairs, s=2), slast[:, c]).then_inc(so_st, 16)
                sp.dma_start(sample[0].rearrange("b (q s) n -> q b (s n)", s=2), s0l[:, c]).then_inc(so_st, 16)
            for c in range(4):
                if c == 3:
                    sp.wait_ge(yb_ps, 4)
                    for b, col in ((0, 0), (1, D)):
                        load_block(b, columns(b, ssm_w_glu[0], col))
                sp.wait_ge(z_done, c + 1)
                cols_z = slice(256 * c, 256 * (c + 1))
                out = yc[c % 2]
                sp.dma_start(z_d[0:PROMPT, cols_z].rearrange("(m t) n -> m t n", t=BL),
                             out[0:NB].rearrange("m t g n -> m t (g n)")).then_inc(zd_st[c % 2], 16)
                sp.dma_start(z_d[PROMPT:NTOK, cols_z], out[NB:NB + NS, 0].rearrange("m g n -> m (g n)")).then_inc(zd_st[c % 2], 16)
            sp.wait_ge(zd_st[0], 64)
            sp.wait_ge(zd_st[1], 64)
            sp.wait_ge(so_st, 64)
            sp.dma_start(h[:, 0:TP, :], z_d[0:PROMPT].rearrange("(t p) n -> p t n", p=P)).then_inc(z_ld, 16)
            sp.dma_start(h[0:NS, TP, :], z_d[PROMPT:NTOK]).then_inc(z_ld, 16)
            sp.wait_ge(glu_ps, TILES)
            for b, col in ((0, BW), (1, D + BW)):
                load_block(b, columns(b, ssm_w_glu[0], col))

        def ssm_pool(pool, link, root):
            root(HEADS + 3)

        def sines(act):
            act.wait_ge(sin_in, 1)
            act.activation(tiny[8], tiny[7], ACT.Sin).then_inc(sin_done, 1)
            act.activation(tiny[9], tiny[7], ACT.Sin, scale=0.5).then_inc(sin_done, 1)

        def c_transposed(act):
            for b in range(4):
                act.wait_ge(cT_ps2, b + 1)
                src = ps[:, 3 + b, :].rearrange("p (q s o) -> p q s o", s=2, o=GP)
                for s in range(2):
                    part_ = slice(NST * s, NST * (s + 1))
                    act.activation(cT0[part_, b // 2, 16 * (b % 2):16 * (b % 2) + 16], src[part_, :, s], ACT.Copy,
                                   scale=1.0 if b < 2 else -1.0).then_inc(cT_done2, 1)

        def ssm_act(act, norm, transposed):
            norm(2)
            transposed(2)
            for n in range(2 * TILES):
                t, rows = n % TILES, ROWS[n % TILES]
                act.wait_ge(u_ps, n + 1)
                b = n // TILES
                act.activation(h[0:rows, t, b * BW:(b + 1) * BW], ps[0:rows, n % 8, :], ACT.Copy).then_inc(u_done, 1)
            act.wait_ge(s0_ps, 1)
            act.activation(s0t, ps[:, 5, :].rearrange("p (b c q) -> p b c q", b=NS, c=2), ACT.Copy).then_inc(s0_done, 1)
            m = NB + 2 * NS

            def regroup(k):
                dst = ugroup[0:m, k % 2].rearrange("m g (t i) -> m t g i", t=BL)
                act.activation(dst, ublk[:, :, 16 * k:16 * k + 16, :], ACT.Copy).then_inc(ug_done, 1)

            act.wait_ge(ub_ld, 48)
            regroup(0)
            regroup(1)
            for n in range(G // 4):
                act.wait_ge(uT_ps, n + 1)
                if n % 4 == 0 and 4 <= n < 12:
                    regroup(n // 4 + 1)
                act.activation(uT[:, 4 * n:4 * n + 4], ps[:, 6 + n % 2, :].rearrange("p (g m) -> p g m", g=4)[:, :, 0:NB + 2 * NS],
                               ACT.Copy).then_inc(uT_done, 1)
            for c in range(4):
                for n in range(4):
                    act.wait_ge(wb_ps, 4 * c + n + 1)
                    act.activation(wbT[:, c, 2 * n:2 * n + 2], ps[:, n, :].rearrange("p (q c n) -> p q c n", q=2, c=2),
                                   ACT.Copy).then_inc(wb_T, 1)
                for n in range(4):
                    act.wait_ge(b_ps, 4 * c + n + 1)
                    q = 8 * c + 2 * n
                    src = ps[:, 6 + n % 2, :].rearrange("p (q c m) -> p q c m", q=2, c=2)
                    for k in range(2):
                        act.activation(hs[:, 1:NB + 1, k, q:q + 2].rearrange("p m q -> p q m"), src[:, :, k, 0:NB], ACT.Copy)
                        ins = act.activation(snew[:, :, k, q:q + 2].rearrange("p b q -> p q b"),
                                             src[:, :, k, NB + NS:NB + 2 * NS], ACT.Copy)
                    ins.then_inc(b_done, 1)
            act.wait_ge(fin_ps, 1)
            for n in range(4):
                act.activation(s0l[:, n // 2, 4 * (n % 2):4 * (n % 2) + 4], ps[0:PAIRS, n, :].rearrange("p (b n) -> p b n", b=4),
                               ACT.Copy).then_inc(so_done, 1)
            act.activation(slast, ps[0:PAIRS, 4, 0:2 * P].rearrange("p (c n) -> p c n", c=2), ACT.Copy).then_inc(so_done, 1)
            for c in range(4):
                act.wait_ge(yb_ps, c + 1)
                if c >= 2:
                    act.wait_ge(zd_st[c % 2], 32)
                for n in range(4):
                    src = ps[0:NB + NS, 4 * (c % 2) + n, :].rearrange("m (q t o) -> m q t o", q=4, o=GP)
                    dst = yc[c % 2][0:NB + NS].rearrange("m t (q s) o -> m s q t o", s=2)[:, n // 2, 4 * (n % 2):4 * (n % 2) + 4]
                    act.activation(dst, src, ACT.Copy).then_inc(yb_done, 1)
                act.wait_ge(zg_in, c + 1)
                act.activation(yc2[0:NB + NS], yc2[0:NB + NS], ACT.Tanh, scale=GELU_C).then_inc(zg_tanh, 1)
            transposed(3)
            for n in range(2 * TILES):
                rows = ROWS[n % TILES]
                act.wait_ge(glu_ps, n + 1)
                if n >= 2:
                    act.wait_ge(glu_done, n - 1)
                act.activation(arena[0:rows, D + n % 2 * BW:D + (n % 2 + 1) * BW], ps[0:rows, 2 * (n % 4) + 1, :], ACT.Tanh,
                               scale=0.5).then_inc(glu_tanh, 1)

        def c_transposes(pe):
            pe.wait_ge(p2_ld, 64)
            for n in range(16):
                mm = pe.transpose(ps[:, 3 + n // 4, n % 4 * P:(n % 4 + 1) * P],
                                  craw[:, n // 8, n % 8].rearrange("p a n -> p (a n)"), ident[:, :])
                if n % 4 == 3:
                    mm.then_inc(cT_ps2, 1)

        def disc_transposes(pe):
            pe.wait_ge(disc_done, 1)
            for n in range(4):
                mm = pe.transpose(ps[:, 7, n * PAIRS:(n + 1) * PAIRS], tiny[14 + n], ident[0:PAIRS, 0:PAIRS])
            mm.then_inc(disc_ps, 1)

        def kernel_products(pe):
            pe.wait_ge(cT_done2, 8)
            for c in range(4):
                pe.wait_ge(kwb_done, c + 1)
                for q in range(8):
                    for s in range(2):
                        half = slice(NST * s, NST * (s + 1))
                        at = (8 * c + q) * GP
                        for k in range(2):
                            mm = pe.matmul(ps[:, 4 + s, at:at + GP], wb0[half, k, q].rearrange("p t n -> p (t n)"),
                                           cT0[half, k, 8 * c + q], start=(k == 0), stop=(k == 1))
                mm.then_inc(k_ps, 1)

        def ssm_pe(pe, norm, block_rows):
            norm(2)
            for n in range(2 * TILES):
                b, t, rows = n // TILES, n % TILES, ROWS[n % TILES]
                if t == 0:
                    pe.wait_ge(w_ld[b], 32 * ((W_SSM + b) // 2 + 1))
                if n == 0:
                    pe.wait_ge(hT_done, 2 * TILES * 3)
                if n >= 8:
                    pe.wait_ge(u_done, n - 7)
                for c in range(KC):
                    mm = pe.matmul(ps[0:rows, n % 8, :], hT[:, c, t * P:t * P + rows], block_rows(b)[:, c, :],
                                   start=(c == 0), stop=(c == KC - 1))
                mm.then_inc(u_ps, 1)
            pe.wait_ge(u_done, 2 * TILES)
            pe.wait_ge(h2_ld, 32)
            for b in range(NS):
                for c in range(2):
                    at = (2 * b + c) * PAIRS
                    mm = pe.transpose(ps[:, 5, at:at + PAIRS], s0l[:, c, b], ident[0:PAIRS, 0:PAIRS])
            mm.then_inc(s0_ps, 1)
            m = NB + 2 * NS
            for n in range(G // 4):
                if n >= 2:
                    pe.wait_ge(uT_done, n - 1)
                if n % 4 == 0:
                    pe.wait_ge(ug_done, n // 4 + 1)
                for i in range(4):
                    mm = pe.transpose(ps[:, 6 + n % 2, i * P:i * P + m], ugroup[0:m, n // 4 % 2, 4 * (n % 4) + i],
                                      ident[0:m, 0:m])
                mm.then_inc(uT_ps, 1)
            pe.wait_ge(s0_done, 1)
            pe.wait_ge(uT_done, G // 4)
            for c in range(4):
                pe.wait_ge(wb_done, c + 1)
                for n in range(4):
                    if c:
                        pe.wait_ge(wb_T, 4 * (c - 1) + n + 1)
                    for i in range(4):
                        mm = pe.transpose(ps[:, n, i * P:(i + 1) * P],
                                          wb[c][:, i % 2, 2 * n + i // 2].rearrange("p t n -> p (t n)"), ident[:, :])
                    mm.then_inc(wb_ps, 1)
                for n in range(4):
                    pe.wait_ge(wb_T, 4 * c + n + 1)
                    if 4 * c + n >= 2:
                        pe.wait_ge(b_done, 4 * c + n - 1)
                    for i in range(2):
                        for k in range(2):
                            for s in range(2):
                                at = (2 * i + k) * P
                                q = 2 * n + i
                                mm = pe.matmul(ps[NST * s:NST * (s + 1), 6 + n % 2, at:at + m],
                                               wbT[:, c, q, k, NST * s:NST * (s + 1)], uT[:, 2 * (8 * c + q) + s, :],
                                               start=True, stop=True)
                    mm.then_inc(b_ps, 1)
            pe.wait_ge(scan_done, 1)
            for c in range(2):
                for b in range(NS):
                    mm = pe.transpose(ps[0:PAIRS, 2 * c + b // 4, b % 4 * P:(b % 4 + 1) * P], snew[:, b, c], ident[:, :])
            for c in range(2):
                mm = pe.transpose(ps[0:PAIRS, 4, c * P:(c + 1) * P], hs[:, NB, c], ident[:, :])
            mm.then_inc(fin_ps, 1)
            pe.wait_ge(so_done, 5)
            pe.wait_ge(hh_done, 1)
            pe.wait_ge(b_done, 16)
            m = NB + NS
            for c in range(4):
                pe.wait_ge(ca_done, c + 1)
                pe.wait_ge(t_ld[c], 16 * BL)
                if c >= 2:
                    pe.wait_ge(yb_done, 4 * (c - 1))
                for s in range(2):
                    half = slice(NST * s, NST * (s + 1))
                    for q in range(8):
                        g, at = 2 * (8 * c + q) + s, q % 4 * P
                        out = ps[0:m, 4 * (c % 2) + 2 * s + q // 4, at:at + P]
                        pe.matmul(out, uT[:, g, 0:m], toep[:, c, 2 * q + s, :], start=True, stop=False)
                        for k in range(2):
                            mm = pe.matmul(out, hh[half, k, 8 * c + q], ca[c % 2][half, k, q].rearrange("p t n -> p (t n)"),
                                           start=False, stop=(k == 1))
                mm.then_inc(yb_ps, 1)
            pe.wait_ge(yb_done, 16)
            norm(3)
            pe.wait_ge(hT_done, 2 * TILES * 4)
            for j in range(2):
                for t, rows in enumerate(ROWS):
                    n = j * TILES + t
                    if t == 0:
                        for b in range(2):
                            pe.wait_ge(w_ld[b], 32 * ((W_GLU + 2 * j) // 2 + 1))
                    if n >= 4:
                        pe.wait_ge(glu_done, n - 3)
                    for b in range(2):
                        for c in range(KC):
                            mm = pe.matmul(ps[0:rows, 2 * (n % 4) + b, :], hT[:, c, t * P:t * P + rows],
                                           block_rows(b)[:, c, :], start=(c == 0), stop=(c == KC - 1))
                    mm.then_inc(glu_ps, 1)

        def parameter_chain(dve, link):
            lr, li, ldt, dt, t1, t2, t3, ang, sn, sh, mag = tiny[0:11]
            bits = tiny[11].bitcast(I32)
            are, aim, fre, fim = tiny[14:18]
            MAGIC = 12582912.0

            def tt(out, a, b, op):
                link.link(dve.tensor_tensor(out, a, b, op))

            def ts(out, a, s1, s2, op0, op1):
                link.link(dve.tensor_scalar(out, a, s1, s2, op0, op1))

            def exp(out, z):
                ts(t1, z, 1.4426950408889634, MAGIC, ALU.mult, ALU.add)
                ts(t1, t1, MAGIC, -126.0, ALU.subtract, ALU.max)
                ts(t1, t1, 127.0, None, ALU.min, ALU.bypass)
                link.link(dve.scalar_tensor_tensor(t2, t1, -0.693359375, z, ALU.mult, ALU.add))
                link.link(dve.scalar_tensor_tensor(t2, t1, 2.12194440e-4, t2, ALU.mult, ALU.add))
                ts(t3, t2, 1.0 / 5040, None, ALU.mult, ALU.bypass)
                for coefficient in (1.0 / 720, 1.0 / 120, 1.0 / 24, 1.0 / 6, 0.5, 1.0):
                    link.link(dve.scalar_tensor_tensor(t3, t3, coefficient, t2, ALU.add, ALU.mult))
                ts(t1, t1, 127.0, 8388608.0, ALU.add, ALU.mult)
                link.link(dve.tensor_copy(bits, t1))
                link.link(dve.scalar_tensor_tensor(out, t3, 1.0, bits.bitcast(F32), ALU.add, ALU.mult))

            dve.wait_ge(p1_ld, 48)
            link.link(dve.tensor_copy(mag.rearrange("q (s n) -> q s n", s=2), spread(ldt[:, 0:2], 2, NST)))
            exp(dt, mag)
            tt(ang, li, dt, ALU.mult)
            ts(t1, ang, 0.15915494309189535, MAGIC, ALU.mult, ALU.add)
            ts(t1, t1, MAGIC, None, ALU.subtract, ALU.bypass)
            for piece in (-6.28125, -0.0019350051879882812, -3.0199159819e-07):
                link.link(dve.scalar_tensor_tensor(ang, t1, piece, ang, ALU.mult, ALU.add))
            dve.tensor_scalar(ang, ang, 3.1415925, -3.1415925, ALU.min, ALU.max).then_inc(sin_in, 1)
            tt(tiny[12], lr, dt, ALU.mult)
            exp(mag, tiny[12])
            dve.wait_ge(sin_done, 2)
            tt(aim, mag, sn, ALU.mult)
            tt(sh, sh, sh, ALU.mult)
            ts(sh, sh, -2.0, 1.0, ALU.mult, ALU.add)
            tt(are, mag, sh, ALU.mult)
            tt(t1, lr, lr, ALU.mult)
            tt(t2, li, li, ALU.mult)
            tt(t1, t1, t2, ALU.add)
            link.link(dve.reciprocal(t3, t1))
            ts(tiny[12], are, -1.0, None, ALU.add, ALU.bypass)
            tt(t1, tiny[12], lr, ALU.mult)
            tt(t2, aim, li, ALU.mult)
            tt(t1, t1, t2, ALU.add)
            tt(fre, t1, t3, ALU.mult)
            tt(t1, aim, lr, ALU.mult)
            tt(t2, tiny[12], li, ALU.mult)
            tt(t1, t1, t2, ALU.subtract)
            dve.tensor_tensor(fim, t1, t3, ALU.mult).then_inc(disc_done, 1)
            dve.wait_ge(disc_ps, 1)
            link.link(dve.tensor_copy(disc, ps[:, 7, 0:4 * PAIRS].rearrange("p (c q) -> p c q", c=4)))

            tmp = part0.rearrange("p a b q -> p (a b) q")

            def power(out, a, b, n):
                for m in range(n):
                    x0, x1, z0, z1 = pw0[:, 0, a], pw0[:, 1, a], pw0[:, 0, b + m], pw0[:, 1, b + m]
                    dve.tensor_tensor(tmp[:, 0], x0, z0, ALU.mult)
                    dve.tensor_tensor(tmp[:, 1], x1, z1, ALU.mult)
                    dve.tensor_tensor(tmp[:, 2], x0, z1, ALU.mult)
                    tt(tmp[:, 3], x1, z0, ALU.mult)
                    dve.tensor_tensor(pw0[:, 0, out + m], tmp[:, 0], tmp[:, 1], ALU.subtract)
                    tt(pw0[:, 1, out + m], tmp[:, 2], tmp[:, 3], ALU.add)

            dve.memset(pw0[:, 0, 0], 1.0)
            dve.memset(pw0[:, 1, 0], 0.0)
            dve.tensor_copy(pw0[:, 0, 1], disc[:, 0])
            link.link(dve.tensor_copy(pw0[:, 1, 1], disc[:, 1]))
            power(2, 1, 1, 1)
            power(3, 2, 1, 2)
            power(5, 4, 1, 4)
            for t in range(BL):
                ins = dve.tensor_copy(rpw0[:, :, t], pw0[:, :, BL - 1 - t])
            for mat, n in ((stepA0, BL), (oneA0, 1)):
                dve.tensor_copy(mat[:, 0, 0], pw0[:, 0, n])
                dve.tensor_copy(mat[:, 1, 1], pw0[:, 0, n])
                dve.tensor_copy(mat[:, 1, 0], pw0[:, 1, n])
                ins = dve.tensor_scalar(mat[:, 0, 1], pw0[:, 1, n], -1.0, None, ALU.mult)
            link.link(ins)
            dve.wait_ge(p3_ld, 32)
            q4 = wtmp0.rearrange("p k q t n -> p k (q t n)")
            f = [q4[:, k, 0:PAIRS * GP].rearrange("p (q n) -> p q n", q=PAIRS) for k in range(4)]
            cre, cim = spread(disc[:, 2], 2, GP), spread(disc[:, 3], 2, GP)
            dve.tensor_tensor(f[0], cre, braw[:, 0], ALU.mult)
            dve.tensor_tensor(f[1], cim, braw[:, 1], ALU.mult)
            dve.tensor_tensor(f[2], cre, braw[:, 1], ALU.mult)
            tt(f[3], cim, braw[:, 0], ALU.mult)
            dve.tensor_tensor(bb0[:, 0], f[0], f[1], ALU.subtract)
            tt(bb0[:, 1], f[2], f[3], ALU.add)
            dve.wait_ge(cT_done2, 8)
            dve.sem_inc(par_done, 1)
            for c in range(4):
                qs = slice(8 * c, 8 * c + 8)
                pr, pi = (spread(rpw0[:, k, :, qs].rearrange("p t q -> p q t"), 3, GP) for k in range(2))
                br, bi = (spread(bb0[:, k, qs], 2, BL) for k in range(2))
                dve.tensor_tensor(wtmp0[:, 0], pr, br, ALU.mult)
                dve.tensor_tensor(wtmp0[:, 1], pi, bi, ALU.mult)
                dve.tensor_tensor(wtmp0[:, 2], pr, bi, ALU.mult)
                tt(wtmp0[:, 3], pi, br, ALU.mult)
                if c:
                    dve.wait_ge(k_ps, c)
                dve.tensor_tensor(wb0[:, 0], wtmp0[:, 0], wtmp0[:, 1], ALU.subtract)
                dve.tensor_tensor(wb0[:, 1], wtmp0[:, 2], wtmp0[:, 3], ALU.add).then_inc(kwb_done, 1)
                dve.wait_ge(kwb_done, c + 1)
            dve.wait_ge(d_ld, 16)
            tt(ktmp, spread(spread(ident[:, P - GP:P], 1, PAIRS), 1, 2),
               dskip.rearrange("p (q s) n -> p s q n", s=2), ALU.mult)
            dve.wait_ge(k_ps, 4)
            kv = kk.rearrange("p (q s) n -> p s q n", s=2)
            dve.tensor_tensor(kv[:, 0], ps[:, 4, :].rearrange("p (q n) -> p q n", q=PAIRS), ktmp[:, 0], ALU.add)
            dve.tensor_tensor(kv[:, 1], ps[:, 5, :].rearrange("p (q n) -> p q n", q=PAIRS), ktmp[:, 1], ALU.add)\
               .then_inc(k_done, 1)
            dve.wait_ge(par_st, 16)

        def ssm_dve(dve, link, norm):
            def tt(out, a, b, op):
                link.link(dve.tensor_tensor(out, a, b, op))

            def ts(out, a, s1, s2, op0, op1):
                link.link(dve.tensor_scalar(out, a, s1, s2, op0, op1))

            norm(2, HEADS + 3)
            dve.memset(ublk_rows[NB:NB + 2 * NS, :], 0.0).then_inc(ub_zero, 1)
            dve.wait_ge(par_ld, 16)
            dve.wait_ge(u_done, 2 * TILES)
            for c in range(4):
                qs = slice(8 * c, 8 * c + 8)
                pr, pi = (spread(rpw[:, k, :, qs].rearrange("p t q -> p q t"), 3, GP) for k in range(2))
                br, bi = (spread(bb[:, k, qs], 2, BL) for k in range(2))
                dve.tensor_tensor(wtmp[:, 0], pr, br, ALU.mult)
                dve.tensor_tensor(wtmp[:, 1], pi, bi, ALU.mult)
                dve.tensor_tensor(wtmp[:, 2], pr, bi, ALU.mult)
                tt(wtmp[:, 3], pi, br, ALU.mult)
                dve.tensor_tensor(wb[c][:, 0], wtmp[:, 0], wtmp[:, 1], ALU.subtract)
                dve.tensor_tensor(wb[c][:, 1], wtmp[:, 2], wtmp[:, 3], ALU.add).then_inc(wb_done, 1)
                dve.wait_ge(wb_done, c + 1)
            q4 = wtmp.rearrange("p k q t n -> p k (q t n)")
            dve.wait_ge(b_done, 16)
            dve.memset(hs[:, 0], 0.0)
            s2 = snew.rearrange("p b c q -> p c b q")
            old = s0t.rearrange("p b c q -> p c b q")
            dve.wait_ge(s0_done, 1)
            stmp = [q4[:, k, 0:NS * PAIRS].rearrange("p (b q) -> p b q", b=NS) for k in range(4)]
            for o_ in range(2):
                for i_ in range(2):
                    ins = dve.tensor_tensor(stmp[2 * o_ + i_], old[:, i_], spread(oneA[:, o_, i_], 1, NS), ALU.mult)
            link.link(ins)
            for i_ in range(2):
                for o_ in range(2):
                    ins = dve.tensor_tensor(s2[:, o_], s2[:, o_], stmp[2 * o_ + i_], ALU.add)
                link.link(ins)
            with dve.Fori(0, NB // 4) as i:
                link.loop(i, 12)
                for s in range(4):
                    before = hs[:, bass.ds(4 * i + s, 1)].rearrange("p a c q -> p (a c) q")
                    after = hs[:, bass.ds(4 * i + s + 1, 1)].rearrange("p a c q -> p (a c) q")
                    link.link(dve.tensor_tensor(part, stepA, spread(before, 1, 2), ALU.mult))
                    link.link(dve.tensor_tensor(after, after, part[:, :, 0], ALU.add))
                    link.link(dve.tensor_tensor(after, after, part[:, :, 1], ALU.add))
            link.end(NB // 4)
            dve.sem_inc(scan_done, 1)
            for k in range(2):
                dve.tensor_copy(hh[:, k, :, 0:NB], hs[:, 0:NB, k].rearrange("p m q -> p q m"))
                ins = dve.tensor_copy(hh[:, k, :, NB:], s0t[:, :, k].rearrange("p b q -> p q b"))
            link.link(ins)
            dve.sem_inc(hh_done, 1)
            dve.wait_ge(fin_ps, 1)
            def output_factors(c):
                qs = slice(8 * c, 8 * c + 8)
                ar, ai = (spread(pw[:, k, 1:BL + 1, qs].rearrange("p t q -> p q t"), 3, GP) for k in range(2))
                cr, ci = (spread(cT[:, k, qs], 2, BL) for k in range(2))
                if c >= 2:
                    dve.wait_ge(yb_ps, c - 1)
                for k, op in enumerate((ALU.add, ALU.subtract)):
                    a_, b_ = catmp[:, 0], catmp[:, 1]
                    dve.tensor_tensor(a_, cr if k == 0 else ci, ar, ALU.mult)
                    tt(b_, ci if k == 0 else cr, ai, ALU.mult)
                    ins = dve.tensor_tensor(ca[c % 2][:, k], a_, b_, op)
                    if k == 0:
                        link.link(ins)
                    else:
                        ins.then_inc(ca_done, 1)
                dve.wait_ge(ca_done, c + 1)

            output_factors(0)
            for c in range(4):
                if c < 3:
                    output_factors(c + 1)
                dve.wait_ge(yb_done, 4 * (c + 1))
                y_, y2 = yc[c % 2][0:NB + NS], yc2[0:NB + NS]
                y_, y2 = (v.rearrange("m t g o -> m (t g o)") for v in (y_, y2))
                tt(y2, y_, y_, ALU.mult)
                ts(y2, y2, GELU_A, 1.0, ALU.mult, ALU.add)
                dve.tensor_tensor(y2, y2, y_, ALU.mult).then_inc(zg_in, 1)
                dve.wait_ge(zg_tanh, c + 1)
                link.link(dve.scalar_tensor_tensor(y2, y2, 1.0, y_, ALU.add, ALU.mult))
                dve.tensor_scalar(y_, y2, 0.5, None, ALU.mult).then_inc(z_done, 1)
                dve.wait_ge(z_done, c + 1)
            dve.wait_ge(z_ld, 32)
            dve.sem_inc(h_done, TILES)
            gt = arena[:, 2 * D:4 * D].rearrange("p (a n) -> p a n", a=4)
            for n in range(2 * TILES):
                j, t, rows = n // TILES, n % TILES, ROWS[n % TILES]
                mod = (modp if t < TP else mods)[0:rows, 2, j * BW:(j + 1) * BW]
                dve.wait_ge(glu_tanh, n + 1)
                th = arena[0:rows, D + n % 2 * BW:D + (n % 2 + 1) * BW]
                v1, v2 = gt[0:rows, n % 2], gt[0:rows, 2 + n % 2]
                dve.scalar_tensor_tensor(v1, th, 1.0, ps[0:rows, 2 * (n % 4), :], ALU.add, ALU.mult).then_inc(glu_done, 1)
                dve.wait_ge(glu_done, n + 1)
                link.link(dve.scalar_tensor_tensor(v2, v1, 0.5, mod, ALU.mult, ALU.mult))
                xt = x[0:rows, t, j * BW:(j + 1) * BW]
                link.link(dve.tensor_tensor(xt, xt, v2, ALU.add))
            dve.sem_inc(x_ready, 1)

        block = ctx.enter_context(nc.Block())

        @block.sync
        def _(sp):
            def load_block(slot, halves):
                for dst, src in halves:
                    sp.dma_start(dst, src).then_inc(w_ld[slot], 16)

            def columns(slot, wm, col):
                dst = w[:, slot, :].rearrange("p (c n) -> p c n", c=KC)
                src = wm.rearrange("(c p) n -> p c n", p=P)
                return [(dst[:, c:c + KC // 2], src[:, c:c + KC // 2, bass.ds(col, BW)]) for c in (0, KC // 2)]

            def qk_columns(slot, head):
                dst = w[:, slot, :].rearrange("p (c s n) -> p c s n", c=KC, s=2)
                src = ret_w_in[0].rearrange("(c p) n -> p c n", p=P)
                return [(dst[:, :, s], src[:, :, bass.ds(head * DK + s * HEADS * DK, DK)]) for s in range(2)]

            def out_rows(slot, head):
                dst = w[:, slot, :].rearrange("p (k n) -> p k n", k=4)
                src = ret_w_out[0].rearrange("(k p) n -> p k n", p=P)
                return [(dst[:, k:k + 2], src[:, bass.ds(head * 4 + k, 2), :]) for k in (0, 2)]

            def modulation(k):
                if k == 0:
                    sp.wait_ge(mod_st, 16 * LAYERS)
                if k:
                    sp.wait_ge(x_ready, k)
                at = k * 3 * D
                sp.dma_start(modp[:, :, :].rearrange("p s n -> p (s n)"),
                             mod_d[NS:NC, at:at + 3 * D].to_broadcast([P, 3 * D])).then_inc(mod_ld, 16)
                sp.dma_start(mods[0:NS, :, :].rearrange("p s n -> p (s n)"),
                             mod_d[0:NS, at:at + 3 * D]).then_inc(mod_ld, 16)
                sp.dma_start(gain, norm_g[k // 2, k % 2:k % 2 + 1, :].to_broadcast([P, D])).then_inc(mod_ld, 16)

            parameter_loads(sp)
            sp.dma_start(cond[0:NS, :], c_sample).then_inc(c_ld, 16)
            sp.dma_start(cond[NS:NC, :], c_prompt).then_inc(c_ld, 16)
            for b in range(2):
                load_block(b, columns(b, w_ada[0], b * BW))
            sp.dma_start(bias, b_ada.rearrange("l (a n) -> a (l n)", a=1).to_broadcast([NC, LAYERS * 6 * D]))\
              .then_inc(tab_ld, 16)
            more_parameter_loads(sp)
            sp.dma_start(x[:, 0:TP, :], x_prompt[0].rearrange("(t p) n -> p t n", p=P)).then_inc(x_ld, 16)
            sp.dma_start(x[0:NS, TP, :], x_sample[:, 0, :]).then_inc(x_ld, 16)

            per_layer = ADA_BLOCKS // LAYERS
            for layer in range(LAYERS):
                with sp.Fori(1 if layer == 0 else 0, per_layer // 2) as i:
                    for s in range(2):
                        sp.wait_ge(w_used, 2 * i + (layer * per_layer + s - 1))
                        load_block(s, columns(s, w_ada[layer], (2 * i + s) * BW))
            def head_blocks(head, last):
                sp.wait_ge(y_done, head * 2 * TILES + 1)
                load_block(1, columns(1, ret_w_in[0], head * DV + 2 * HEADS * DK))
                sp.wait_ge(proj_ps, head * 3 * TILES + TILES)
                load_block(0, columns(0, ret_w_in[0], head * DV + 2 * HEADS * DK + HEADS * DV))
                sp.wait_ge(proj_ps, head * 3 * TILES + 2 * TILES)
                load_block(1, out_rows(1, head))
                if not last:
                    sp.wait_ge(proj_ps, head * 3 * TILES + 3 * TILES)
                    load_block(0, qk_columns(0, head + 1))

            sp.wait_ge(w_used, ADA_BLOCKS - 1)
            load_block(0, qk_columns(0, 0))
            sp.wait_ge(w_used, ADA_BLOCKS)
            modulation(0)
            kernels_out(sp)
            sp.wait_ge(par_st, 16)
            sp.dma_start(rots, rot_tab).then_inc(tab_ld, 16)
            sp.dma_start(masks, decay_tab).then_inc(tab_ld, 16)
            sp.dma_start(colss, decay_cols).then_inc(tab_ld, 16)
            with sp.Fori(0, HEADS - 1) as head:
                head_blocks(head, False)
            head_blocks(HEADS - 1, True)

            def peer(layer):
                def query(b):
                    n = W_PEER[layer] + b
                    if b >= 2:
                        sp.wait_ge(q_ps, 2 * PH * layer + 4 * (b - 1))
                    elif layer == 0:
                        sp.wait_ge(*((proj_ps, HEADS * 3 * TILES), (y_ps, HEADS * 2 * TILES))[b])
                    else:
                        sp.wait_ge(glu_ps, GLU_USED[b])
                    load_block(n % 2, columns(n % 2, peer_w_q[layer], b * BW))

                query(0)
                query(1)
                modulation(2 * layer + 1)
                for side, key in enumerate((peer_key1, peer_key2)):
                    sp.dma_start(keys.rearrange("p (e s) d -> p e s d", s=2)[:, :, side],
                                 key[layer].rearrange("e k d -> k e d")).then_inc(key_ld, 16)
                if layer == 0:
                    sp.dma_start(lane[:, :], lane_tab).then_inc(key_ld, 16)
                query(2)
                query(3)
                sp.wait_ge(h_done, TILES * (TURN[2 * layer + 1] + 1))
                sp.dma_start(hs_d[layer], h[0:NS, TP, :]).then_inc(hs_st, 16)
                sp.wait_ge(hs_st, 16 * (layer + 1))
                sp.wait_ge(score_ps, TILES * (layer + 1))
                for b in range(NS):
                    if b >= 2:
                        sp.wait_ge(u_used, BATCH + gather_of(layer, TP) + b - 1)
                    sp.dma_start(hb[:, b % 2], hs_d[layer, b:b + 1, :].to_broadcast([P, D])).then_inc(hb_ld[b % 2], 16)

            peer(0)
            ssm_sync(sp, load_block, columns, modulation)
            peer(1)
            sp.wait_ge(x_ready, FINAL)
            sp.dma_start(gain, final_g.rearrange("(a n) -> a n", a=1).to_broadcast([P, D])).then_inc(fin_ld, 16)
            sp.wait_ge(h_done, TILES * (TURN[FINAL] + 1))
            sp.dma_start(y_prompt[0].rearrange("(t p) n -> p t n", p=P), h[:, 0:TP, :]).then_inc(out_st, 16)
            sp.dma_start(y_sample[:, 0, :], h[0:NS, TP, :]).then_inc(out_st, 16)
            sp.wait_ge(out_st, 32)

        @block.gpsimd
        def _(pool):
            link = Steps(pool, steps_p)
            pool.memset(ident[:, :], 0.0).then_inc(consts, 1)
            pool.memset(zeros[:, :], 0.0).then_inc(consts, 1)
            pool.memset(mhalf[:, :], -0.5).then_inc(consts, 1)
            pool.wait_ge(consts, 3)
            pool.affine_select(out=ident[:, :], in_=ident[:, :], compare_op=ALU.not_equal, fill=1.0, base=0,
                               pattern=[[-1, P]], channel_multiplier=1).then_inc(consts, 1)
            pool.wait_ge(consts, 4)

            def root(n):
                pool.wait_ge(var_done, n)
                pool.tensor_tensor(rstd[:, :], var[:, :], mhalf[:, :], ALU.pow).then_inc(rstd_done, 1)

            root(1)

            def s0(head, b):
                return state_ret[0, b].rearrange("e (c p) v -> p e c v", p=P)[:, bass.ds(head, 1)]

            def s1(head, b):
                return ret_sample[0, b].rearrange("e (c p) v -> p e c v", p=P)[:, bass.ds(head, 1)]

            def load_state(head, b):
                pool.dma_start(sring[:, b % 2].unsqueeze(1), s0(head, b)).then_inc(s0_ld[b % 2], 16)

            def head_states(head, last):
                for b in range(NS):
                    pool.wait_ge(s1_done, head * NS + (b + 1))
                    pool.sem_inc(issued, 1)
                    pool.dma_start(s1(head, b), sring[:, b % 2].unsqueeze(1)).then_inc(s1_st[b % 2], 16)
                    if b >= 1 and (b < NS - 1 or not last):
                        slot = (b - 1) % 2
                        pool.wait_ge(s1_st[slot], head * (NS // 2) * 16 + 16 * ((b - 1) // 2 + 1))
                        pool.wait_ge(os_ps, head * NS + b)
                        pool.sem_inc(issued, 1)
                        if b + 1 < NS:
                            load_state(head, b + 1)
                        else:
                            load_state(head + 1, 0)
                if not last:
                    pool.wait_ge(s1_st[1], head * (NS // 2) * 16 + 16 * (NS // 2))
                    pool.wait_ge(os_ps, head * NS + NS)
                    pool.sem_inc(issued, 1)
                    load_state(head + 1, 1)
                pool.wait_ge(state_done, head * TP + TP)
                pool.sem_inc(issued, 1)
                pool.dma_start(ret_prompt[0, 0].rearrange("e (c p) v -> p e c v", p=P)[:, bass.ds(head, 1)],
                               state.unsqueeze(1)).then_inc(state_st, 16)
                pool.wait_ge(var_done, head + 2)
                pool.tensor_tensor(rstd[:, :], var[:, :], mhalf[:, :], ALU.pow).then_inc(rstd_done, 1)
                pool.wait_ge(state_st, head * 16 + 16)
                pool.sem_inc(state_free, 1)

            pool.wait_ge(h_done, TILES)
            pool.sem_inc(state_free, 1)
            load_state(0, 0)
            load_state(0, 1)
            with pool.Fori(0, HEADS - 1) as head:
                head_states(head, False)
            head_states(HEADS - 1, True)
            for s in range(2):
                pool.wait_ge(s1_st[s], 16 * HEADS * NS // 2)

            def gather(ring, slot, table, index, landed_sem):
                pool.indirect_dma_start(ring[:, slot, :], None, table,
                                        bass.IndirectOffsetOnAxis(ap=index, axis=0)).then_inc(landed_sem[slot], 16)

            def peer(layer):
                root(1 + HEADS + 1 if layer == 0 else NORMS - 1)
                ut = peer_u.rearrange("l e n -> (l e) n")
                vt = peer_v.rearrange("l e n -> (l e) n")
                u_lane = (u_ring, ut, stage_u, u_used, u_ld)
                v_lane = (v_ring, vt, stage_v, v_used, v_ld)

                def gathers(count, lanes):
                    with pool.Fori(0, count // BATCH) as i:
                        link.loop(i, 2 * len(lanes))
                        for half in range(2):
                            for (ring, table, stage, used, ld), tile, first in lanes:
                                n = gather_of(layer, tile) + first + half * RING
                                pool.wait_ge(used, i * BATCH + (n + BATCH - RING))
                                pool.sem_inc(issued, 1)
                                link.link(pool.tensor_copy(stage[:, half],
                                                           eidx[:, tile, bass.ds(i * BATCH + (first + half * RING), RING)]))
                                pool.sem_inc(issued, 1)
                            for s in range(RING):
                                for (ring, table, stage, used, ld), tile, first in lanes:
                                    n = gather_of(layer, tile) + first + half * RING + s
                                    pool.wait_ge(used, i * BATCH + slot_free(n))
                                    pool.sem_inc(issued, 1)
                                    gather(ring, s, table, stage[:, half, s:s + 1], ld)
                    link.end(count // BATCH)

                def sample_gathers(lane_):
                    ring, table, _, used, ld = lane_
                    for b in range(NS):
                        pool.wait_ge(used, slot_free(gather_of(layer, TP) + b))
                        gather(ring, b, table, eidx_s[:, b:b + 1], ld)

                pool.wait_ge(top_done, TILES * layer + 1)
                gathers(NE, [(u_lane, 0, 0)])
                for t in range(1, TP):
                    gathers(ALONE, [(v_lane, t - 1, 0)])
                    pool.wait_ge(top_done, TILES * layer + t + 1)
                    gathers(NE - ALONE, [(u_lane, t, 0), (v_lane, t - 1, ALONE)])
                    gathers(ALONE, [(u_lane, t, NE - ALONE)])
                gathers(EARLY, [(v_lane, TP - 1, 0)])
                pool.wait_ge(es_done, 2 * (layer + 1))
                sample_gathers(u_lane)
                gathers(NE - EARLY, [(v_lane, TP - 1, EARLY)])
                sample_gathers(v_lane)

            peer(0)
            ssm_pool(pool, link, root)
            peer(1)
            root(NORMS)

        @block.scalar
        def _(act):

            def norm(k):
                if k:
                    act.wait_ge(x_ready, k)
                else:
                    act.wait_ge(x_ld, 32)
                    act.wait_ge(constv, 1)
                for t, rows in enumerate(ROWS):
                    act.activation(h[0:rows, t, :], x[0:rows, t, :], ACT.Square, accum_out=sq[0:rows, t:t + 1])\
                       .then_inc(sq_done, 1)

            def transposed(k):
                for t, rows in enumerate(ROWS):
                    for half in range(2):
                        n = 2 * t + half
                        act.wait_ge(hT_ps, 2 * TILES * k + n + 1)
                        src = ps[:, n % 8, :].rearrange("p (c r) -> p c r", c=4)
                        act.activation(hT[:, 4 * half:4 * half + 4, t * P:t * P + rows], src[:, :, 0:rows], ACT.Copy)\
                           .then_inc(hT_done, 1)

            act.wait_ge(c_ld, 32)
            act.activation(cond_t, cond, ACT.Tanh, scale=0.5).then_inc(c_tanh, 1)
            act.wait_ge(tab_ld, 16)
            for s in range(2):
                act.activation(modp[0:1, s, 0:BW], bias[0:1, s * BW:(s + 1) * BW], ACT.Copy).then_inc(bias_row, 1)
            for third in range(3):
                with act.Fori(third * ADA_BLOCKS // 6, (third + 1) * ADA_BLOCKS // 6) as i:
                    for s in range(2):
                        act.wait_ge(w_used, 2 * i + (s + 1))
                        act.activation(bias[:, bass.ds((2 * i + s) * BW, BW)], ps[0:NC, 1 + s, :], ACT.Copy)\
                           .then_inc(bias_row, 1)
                        act.wait_ge(bias_row, 2 * i + (s + 3))
                        act.activation(modp[0:1, s, 0:BW], arena[0:1, bass.ds((2 * i + s + 2) * BW, BW)], ACT.Copy)\
                           .then_inc(mod_done, 1)
                if third == 0:
                    sines(act)
                    continue
                act.wait_ge(mod_done, 2 + (third + 1) * ADA_BLOCKS // 3)
                at = (third - 1) * 6 * D
                act.dma_start(mod_d[:, at:at + 6 * D], bias[:, at:at + 6 * D]).then_inc(mod_st, 16)
                if third == 1:
                    c_transposed(act)
            act.wait_ge(par_done, 1)
            act.dma_start(par_d, par0).then_inc(par_st, 16)
            act.wait_ge(kd_st, 16 * BL)
            norm(0)
            transposed(TURN[0])

            with act.Fori(0, HEADS) as head:
                act.wait_ge(y_done, head * 2 * TILES + 1)
                for j in range(3):
                    for t, rows in enumerate(ROWS):
                        act.wait_ge(proj_ps, head * 3 * TILES + (j * TILES + t + 1))
                        act.activation(proj[0:rows, t, j * BW:(j + 1) * BW], ps[0:rows, t, :], ACT.Copy)\
                           .then_inc(proj_done, 1)
                for t in range(TP):
                    act.wait_ge(qk_ps, head * TILES + (t + 1))
                    act.activation(qkT[:, t], ps[:, 5 + t % 2, :].rearrange("p (c r) -> p c r", c=4), ACT.Copy)\
                       .then_inc(qk_done, 1)
                act.wait_ge(qk_ps, head * TILES + TILES)
                act.wait_ge(qz_zero, 1)
                act.activation(qz[:, :, ::NS + 1], ps[:, 7, 0:2 * NS].rearrange("p (c r) -> p c r", c=2), ACT.Copy)\
                   .then_inc(qk_done, 1)
                act.wait_ge(rot_done, head * 2 + 2)
                act.wait_ge(proj_done, head * 3 * TILES + 3 * TILES)
                for t, rows in enumerate(ROWS):
                    act.activation(sil[0:rows, t], proj[0:rows, t, 2 * BW:3 * BW], ACT.Tanh, scale=0.5)\
                       .then_inc(g_tanh, 1)
                for t in range(1, TP):
                    act.wait_ge(cross_ps, head * (TP - 1) + t)
                    if t >= 3:
                        act.wait_ge(o_done, head * TP + (t - 1))
                    act.activation(cross[:, t % 2], ps[:, 6, :], ACT.Copy, scale=cols[:, 0:1]).then_inc(cross_done, 1)
                for t, rows in enumerate(ROWS):
                    act.wait_ge(oT_ps, head * TILES + (t + 1))
                    src = ps[:, 5 + t % 2, :].rearrange("p (c r) -> p c r", c=4)
                    act.activation(oT[:, :, t * P:t * P + rows], src[:, :, 0:rows], ACT.Copy).then_inc(oT_done, 1)

            def peer(layer):
                k = 2 * layer + 1
                norm(k)
                transposed(TURN[k])
                for b in range(4):
                    act.wait_ge(key_ps, 4 * layer + b + 1)
                    act.activation(keyT[:, 4 * b:4 * b + 4], ps[:, 4 + b, :].rearrange("p (c r) -> p c r", c=4),
                                   ACT.Copy).then_inc(key_done, 1)
                for n in range(2 * PH):
                    act.wait_ge(q_ps, 2 * PH * layer + n + 1)
                    act.activation(qT[:, n, 0:TP * P], ps[:, n % 2, :], ACT.Copy).then_inc(q_done, 1)
                    act.activation(qT[:, n, TP * P:NTOK], ps[:, 2 + n % 2, 0:NS], ACT.Copy).then_inc(q_done, 1)
                def scores_in(t):
                    rows = ROWS[t]
                    act.wait_ge(score_ps, TILES * layer + t + 1)
                    if t:
                        act.wait_ge(top_done, TILES * layer + t)
                    for b in range(4):
                        act.activation(score[0:rows, 4 * b:4 * b + 4],
                                       ps[0:rows, 4 + b, :].rearrange("p (c r) -> p c r", c=4), ACT.Copy)\
                           .then_inc(score_done, 1)

                def exponentials(t):
                    act.wait_ge(e_sub, TILES * layer + t + 1)
                    act.activation(topv[0:ROWS[t]], topv[0:ROWS[t]], ACT.Exp).then_inc(e_exp, 1)

                def tanh_of(t):
                    act.wait_ge(gelu_in, TILES * layer + t + 1)
                    a = acts_s2 if t == TP else acts2
                    act.activation(a, a, ACT.Tanh, scale=GELU_C).then_inc(gelu_tanh, 1)

                def diagonals(t, first, end):
                    with act.Fori(0, (end - first) // 4) as i:
                        for s in range(4):
                            act.wait_ge(v_used, 4 * i + (gather_of(layer, t) + first + s + BATCH - 4 + 1))
                            act.sem_inc(issued, 1)
                            act.activation(diag[:, s], ident[:, :], ACT.Copy,
                                           scale=wgt[:, t % 2, bass.ds(4 * i + (first + s), 1)]).then_inc(diag_done, 1)

                scores_in(0)
                exponentials(0)
                scores_in(1)
                tanh_of(0)
                for t in range(TP):
                    act.wait_ge(wgt_done, TILES * layer + t + 1)
                    diagonals(t, 0, ALONE - 8)
                    exponentials(t + 1)
                    if t < TP - 1:
                        diagonals(t, ALONE - 8, NE)
                        scores_in(t + 2)
                        tanh_of(t + 1)
                    else:
                        diagonals(t, ALONE - 8, NE - ALONE)
                        tanh_of(TP)
                        diagonals(t, NE - ALONE, NE)

            peer(0)
            ssm_act(act, norm, transposed)
            peer(1)
            norm(FINAL)

        @block.tensor
        def _(pe):
            def norm(k):
                for t, rows in enumerate(ROWS):
                    pe.wait_ge(h_done, TILES * k + t + 1)
                    for half in range(2):
                        n = 2 * t + half
                        if n >= 8:
                            pe.wait_ge(hT_done, 2 * TILES * k + n - 8 + 1)
                        for c in range(4):
                            mm = pe.transpose(ps[:, n % 8, c * P:c * P + rows],
                                              h[0:rows, t, (4 * half + c) * P:(4 * half + c + 1) * P],
                                              ident[0:rows, 0:rows])
                        mm.then_inc(hT_ps, 1)

            def block_rows(slot):
                return w[:, slot, :].rearrange("p (c n) -> p c n", c=KC)

            pe.wait_ge(consts, 4)
            pe.wait_ge(c_silu, 1)
            for c in range(KC):
                mm = pe.transpose(ps[:, 0, c * NC:(c + 1) * NC], cond[:, c * P:(c + 1) * P], ident[0:NC, 0:NC])
            mm.then_inc(cT_ps, 1)
            pe.wait_ge(cT_done, 1)
            c_transposes(pe)
            pe.wait_ge(bias_row, 2)
            pe.wait_ge(constv, 1)
            for third in range(3):
                with pe.Fori(third * ADA_BLOCKS // 6, (third + 1) * ADA_BLOCKS // 6) as i:
                    for s in range(2):
                        pe.wait_ge(w_ld[s], i * 32 + 32)
                        pe.wait_ge(mod_done, 2 * i + (s + 1))
                        for c in range(KC):
                            pe.matmul(ps[0:NC, 1 + s, :], condT[:, c, :], block_rows(s)[:, c, :],
                                      start=(c == 0), stop=False)
                        pe.matmul(ps[0:NC, 1 + s, :], ones, modp[0:1, s, 0:BW],
                                  start=False, stop=True).then_inc(w_used, 1)
                if third == 1:
                    disc_transposes(pe)
            kernel_products(pe)
            norm(0)

            with pe.Fori(0, HEADS) as head:
                pe.wait_ge(y_done, head * 2 * TILES + 1)
                for j in range(3):
                    slot = j % 2
                    pe.wait_ge(w_ld[slot], head * 64 + 32 * (W_HEADS // 2 + j // 2 + 1))
                    for t, rows in enumerate(ROWS):
                        if j:
                            pe.wait_ge(proj_done, head * 3 * TILES + ((j - 1) * TILES + t + 1))
                        elif t == 0:
                            pe.wait_ge(hT_done, 2 * TILES)
                        for c in range(KC):
                            mm = pe.matmul(ps[0:rows, t, :], hT[:, c, t * P:t * P + rows], block_rows(slot)[:, c, :],
                                           start=(c == 0), stop=(c == KC - 1))
                        mm.then_inc(proj_ps, 1)
                pe.wait_ge(rot_done, head * 2 + 2)
                pe.sem_inc(issued, 1)
                for t in range(TP):
                    if t >= 2:
                        pe.wait_ge(qk_done, head * TILES + (t - 1))
                    for c in range(4):
                        mm = pe.transpose(ps[:, 5 + t % 2, c * P:(c + 1) * P],
                                          qkr[:, t, c // 2, c % 2 * P:(c % 2 + 1) * P], ident[:, :])
                    mm.then_inc(qk_ps, 1)
                for c in range(2):
                    mm = pe.transpose(ps[:, 7, c * NS:(c + 1) * NS], qkr[0:NS, TP, 0, c * P:(c + 1) * P],
                                      ident[0:NS, 0:NS])
                mm.then_inc(qk_ps, 1)
                pe.wait_ge(qk_done, head * TILES + TILES)
                pe.wait_ge(kt_done, head + 1)
                pe.wait_ge(proj_done, head * 3 * TILES + 3 * TILES)
                for t in range(TP):
                    if t:
                        pe.wait_ge(att_done, head * TP + t)
                    for c in range(2):
                        mm = pe.matmul(ps[:, 7, 0:P], qkT[:, t, 2 + c], qkT[:, t, c], start=(c == 0), stop=(c == 1))
                    mm.then_inc(att_ps, 1)
                    if t:
                        pe.wait_ge(state_done, head * TP + t)
                        if t >= 2:
                            pe.wait_ge(cross_done, head * (TP - 1) + (t - 1))
                        for c in range(2):
                            mm = pe.matmul(ps[:, 6, :], qkT[:, t, c], state[:, c], start=(c == 0), stop=(c == 1))
                        mm.then_inc(cross_ps, 1)
                        pe.wait_ge(o_done, head * TP + t)
                    for c in range(2):
                        mm = pe.matmul(ps[:, c, :], kt[:, t, c * P:(c + 1) * P], proj[:, t, BW:2 * BW],
                                       start=True, stop=True)
                    mm.then_inc(ds_ps, 1)
                    pe.wait_ge(att_done, head * TP + (t + 1))
                    pe.matmul(ps[:, 5, :], att[:, t % 2], proj[:, t, BW:2 * BW], start=True, stop=True)\
                      .then_inc(o_ps, 1)
                pe.wait_ge(kz_done, head + 1)
                for b in range(NS):
                    for c in range(2):
                        mm = pe.matmul(ps[:, 2 + c, :], kz[:, b, c * P:(c + 1) * P], proj[0:NS, TP, BW:2 * BW],
                                       start=True, stop=True)
                    mm.then_inc(outer_ps, 1)
                    pe.wait_ge(s1_done, head * NS + (b + 1))
                    for c in range(2):
                        mm = pe.matmul(ps[0:NS, 4, :], qz[:, c, b * NS:(b + 1) * NS], sring[:, b % 2, c],
                                       start=(b == 0 and c == 0), stop=(b == NS - 1 and c == 1))
                    mm.then_inc(os_ps, 1)
                for t, rows in enumerate(ROWS):
                    pe.wait_ge(og_done, head * TILES + (t + 1))
                    if t >= 2:
                        pe.wait_ge(oT_done, head * TILES + (t - 1))
                    pe.sem_inc(issued, 1)
                    for c in range(4):
                        mm = pe.transpose(ps[:, 5 + t % 2, c * P:c * P + rows], o[0:rows, t, c * P:(c + 1) * P],
                                          ident[0:rows, 0:rows])
                    mm.then_inc(oT_ps, 1)
                pe.wait_ge(w_ld[1], head * 64 + 32 * (W_HEADS // 2 + 2))
                rows_out = w[:, 1, :].rearrange("p (k n) -> p k n", k=4)
                for t, rows in enumerate(ROWS):
                    pe.wait_ge(oT_done, head * TILES + (t + 1))
                    for half in range(2):
                        n = 2 * t + half
                        if n >= 4:
                            pe.wait_ge(y_done, head * 2 * TILES + (n - 4 + 1 + 1))
                        for c in range(4):
                            mm = pe.matmul(ps[0:rows, n % 4, :], oT[:, c, t * P:t * P + rows],
                                           rows_out[:, c, half * BW:(half + 1) * BW], start=(c == 0), stop=(c == 3))
                        mm.then_inc(y_ps, 1)

            def peer(layer):
                norm(TURN[2 * layer + 1])
                pe.wait_ge(key_ld, 16 * (2 * (layer + 1) + 1))
                pe.wait_ge(hT_done, 2 * TILES * (TURN[2 * layer + 1] + 1))
                for b in range(4):
                    for c in range(4):
                        mm = pe.transpose(ps[:, 4 + b, c * P:(c + 1) * P], keys[:, 4 * b + c], ident[:, :])
                    mm.then_inc(key_ps, 1)
                for n in range(2 * PH):
                    g = W_PEER[layer] + n // 4
                    pe.wait_ge(w_ld[g % 2], 32 * (g // 2 + 1))
                    if n >= 2:
                        pe.wait_ge(q_done, 4 * PH * layer + 2 * (n - 1))
                    for c in range(KC):
                        wq = block_rows(g % 2)[:, c, n % 4 * P:(n % 4 + 1) * P]
                        pe.matmul(ps[:, n % 2, :], wq, hT[:, c, 0:TP * P], start=(c == 0), stop=(c == KC - 1))
                        mm = pe.matmul(ps[:, 2 + n % 2, 0:NS], wq, hT[:, c, TP * P:NTOK],
                                       start=(c == 0), stop=(c == KC - 1))
                    mm.then_inc(q_ps, 1)
                pe.wait_ge(q_done, 4 * PH * (layer + 1))
                pe.wait_ge(key_done, 4 * (layer + 1))

                def scores(t):
                    rows = ROWS[t]
                    if t:
                        pe.wait_ge(score_done, 4 * (TILES * layer + t))
                    for n in range(2 * PH):
                        mm = pe.matmul(ps[0:rows, 4 + n // 4, n % 4 * P:(n % 4 + 1) * P],
                                       qT[:, n, t * P:t * P + rows], keyT[:, n], start=True, stop=True)
                    mm.then_inc(score_ps, 1)

                def mix(t, first, end):
                    bank = 2 * (t % 2)
                    if first == 0:
                        if t >= 2:
                            pe.wait_ge(mix_free, TILES * layer + t - 1)
                        for half in range(2):
                            pe.matmul(ps[:, bank + half, :], zeros[:, :], modp[:, 0, half * BW:(half + 1) * BW],
                                      start=True, stop=False)
                    with pe.Fori(0, (end - first) // BATCH) as i:
                        for s in range(BATCH):
                            pe.wait_ge(v_ld[s % RING], i * 32 + landed(layer, t, first // RING + s // RING))
                            pe.wait_ge(diag_done, i * BATCH + ((TP * layer + t) * NE + first + s + 1))
                            for half in range(2):
                                mm = pe.matmul(ps[:, bank + half, :], diag[:, s % 4],
                                               v_ring[:, s % RING, half * BW:(half + 1) * BW], start=False, stop=False)
                            mm.then_inc(v_used, 1)
                    if end == NE:
                        for half in range(2):
                            mm = pe.matmul(ps[:, bank + half, :], zeros[:, :], modp[:, 0, half * BW:(half + 1) * BW],
                                           start=False, stop=True)
                        mm.then_inc(mix_ps, 1)

                scores(0)
                scores(1)
                for t in range(TP - 1):
                    mix(t, 0, NE)
                    scores(t + 2)
                mix(TP - 1, 0, EARLY)
                pe.wait_ge(top_done, TILES * (layer + 1))
                pe.transpose(ps[:, 6, 0:NS], place_s[0:NS], ident[0:NS, 0:NS])
                pe.transpose(ps[:, 6, NS:2 * NS], gate[0:NS, TP], ident[0:NS, 0:NS]).then_inc(es_ps, 1)
                mix(TP - 1, EARLY, NE)
                pe.wait_ge(wgt_done, TILES * (layer + 1))
                for b in range(NS):
                    pe.wait_ge(v_ld[b], landed(layer, TP, 0))
                    for half in range(2):
                        mm = pe.matmul(ps[0:NS, 4 + half, :], wgt_s[:, b * NS:(b + 1) * NS],
                                       v_ring[:, b, half * BW:(half + 1) * BW], start=(b == 0), stop=(b == NS - 1))
                    mm.then_inc(v_used, 1)

            peer(0)
            ssm_pe(pe, norm, block_rows)
            peer(1)

        @block.vector
        def _(dve):
            link = Steps(dve, steps_v)

            def norm(k, times):
                if k < FINAL:
                    dve.wait_ge(mod_ld, 48 * (k + 1))
                    dve.scalar_tensor_tensor(modp[:, 1], modp[:, 1], 1.0, gain, ALU.add, ALU.mult)
                    link.link(dve.scalar_tensor_tensor(mods[0:NS, 1], mods[0:NS, 1], 1.0, gain[0:NS], ALU.add, ALU.mult))
                else:
                    dve.wait_ge(fin_ld, 16)
                dve.wait_ge(sq_done, TILES * (k + 1))
                dve.tensor_scalar(var[:, :], sq[:, :], 1.0 / D, EPS, ALU.mult, ALU.add).then_inc(var_done, 1)
                dve.wait_ge(rstd_done, times)
                for t, rows in enumerate(ROWS):
                    factor = gain if k == FINAL else (modp if t < TP else mods)[:, 1]
                    ins = dve.scalar_tensor_tensor(h[0:rows, t], x[0:rows, t], rstd[0:rows, t:t + 1], factor[0:rows],
                                                   ALU.mult, ALU.mult)
                    if k == FINAL:
                        ins.then_inc(h_done, 1)
                if k == FINAL:
                    return
                link.link(ins)
                for t, rows in enumerate(ROWS):
                    shift = (modp if t < TP else mods)[0:rows, 0]
                    dve.tensor_tensor(h[0:rows, t], h[0:rows, t], shift, ALU.add).then_inc(h_done, 1)

            link.link(dve.memset(ones, 1.0))
            dve.memset(sq[:, :], 1.0).then_inc(constv, 1)
            dve.sem_inc(mod_done, 2)
            dve.sem_inc(y_done, 1)
            dve.sem_inc(u_used, BATCH)
            dve.sem_inc(v_used, BATCH)
            dve.wait_ge(c_tanh, 1)
            link.link(dve.scalar_tensor_tensor(cond_t, cond_t, 1.0, cond, ALU.add, ALU.mult))
            dve.tensor_scalar(cond, cond_t, 0.5, None, ALU.mult).then_inc(c_silu, 1)
            dve.wait_ge(cT_ps, 1)
            dve.tensor_copy(condT, ps[:, 0, 0:KC * NC].rearrange("p (c n) -> p c n", c=KC)).then_inc(cT_done, 1)
            parameter_chain(dve, link)
            dve.wait_ge(x_ld, 32)
            norm(0, 1)
            dve.wait_ge(tab_ld, 64)
            dve.memset(qz, 0.0).then_inc(qz_zero, 1)

            def rotate(rows, t0, t1):
                qk = proj[0:rows, t0:t1, 0:BW].rearrange("p t (s f n) -> p t s f n", s=2, f=2)
                cos, sin = rots[0:rows, t0:t1, 0], rots[0:rows, t0:t1, 1]
                first, second = qk[:, :, :, 0], qk[:, :, :, 1]
                out = qkr[0:rows, t0:t1].rearrange("p t s (f n) -> p t s f n", f=2)
                n = t1 - t0
                a1, b1 = rot1[0:rows, 0:n, 0:2], rot2[0:rows, 0:n, 0:2]
                a2, b2 = rot1[0:rows, 0:n, 2:4], rot2[0:rows, 0:n, 2:4]
                for j in range(n):
                    dve.tensor_tensor(a1[:, j], first[:, j], cos[:, j], ALU.mult)
                    dve.tensor_tensor(b1[:, j], second[:, j], sin[:, j], ALU.mult)
                    dve.tensor_tensor(a2[:, j], second[:, j], cos[:, j], ALU.mult)
                    ins = dve.tensor_tensor(b2[:, j], first[:, j], sin[:, j], ALU.mult)
                link.link(ins)
                for j in range(n):
                    dve.tensor_tensor(out[:, j, :, 0], a1[:, j], b1[:, j], ALU.subtract)
                    ins = dve.tensor_tensor(out[:, j, :, 1], a2[:, j], b2[:, j], ALU.add)
                ins.then_inc(rot_done, 1)

            with dve.Fori(0, HEADS) as head:
                link.loop(head, HEAD_LINKS)
                dve.wait_ge(y_done, head * 2 * TILES + 1)
                dve.tensor_scalar(mask.unsqueeze(1), masks[:, bass.ds(head, 1), :], 1.0, None, ALU.mult)
                link.link(dve.tensor_scalar(cols.unsqueeze(1), colss[:, bass.ds(head, 1), :], 1.0, None, ALU.mult))
                dve.wait_ge(proj_done, head * 3 * TILES + TILES)
                rotate(P, 0, TP)
                dve.wait_ge(rot_done, head * 2 + 1)
                rotate(NS, TP, TILES)
                dve.wait_ge(rot_done, head * 2 + 2)
                dve.tensor_scalar(kt, qkr[:, 0:TP, 1], cols[:, 1:2], None, ALU.mult).then_inc(kt_done, 1)
                dve.tensor_tensor(kz, spread(qkr[0:NS, TP, 1], 1, NS), spread(ident[0:NS, 0:NS], 2, DK), ALU.mult)\
                   .then_inc(kz_done, 1)
                dve.wait_ge(state_free, head + 1)
                for t in range(TP):
                    dve.wait_ge(att_ps, head * TP + (t + 1))
                    dve.tensor_tensor(att[:, t % 2], ps[:, 7, 0:P], mask, ALU.mult).then_inc(att_done, 1)
                    dve.wait_ge(ds_ps, head * TP + (t + 1))
                    if t:
                        dve.wait_ge(cross_ps, head * (TP - 1) + t)
                        for c in range(2):
                            ins = dve.scalar_tensor_tensor(state[:, c], state[:, c], cols[:, 2:3], ps[:, c, :],
                                                           ALU.mult, ALU.add)
                    else:
                        ins = dve.tensor_copy(state, ps[:, 0:2, :])
                    ins.then_inc(state_done, 1)
                    dve.wait_ge(o_ps, head * TP + (t + 1))
                    if t:
                        dve.wait_ge(cross_done, head * (TP - 1) + t)
                        dve.tensor_tensor(o[:, t], ps[:, 5, :], cross[:, t % 2], ALU.add).then_inc(o_done, 1)
                    else:
                        dve.tensor_copy(o[:, t], ps[:, 5, :]).then_inc(o_done, 1)
                    dve.wait_ge(state_done, head * TP + (t + 1))
                for b in range(NS):
                    dve.wait_ge(s0_ld[b % 2], head * (NS // 2) * 16 + 16 * (b // 2 + 1))
                    dve.wait_ge(outer_ps, head * NS + (b + 1))
                    for c in range(2):
                        ins = dve.scalar_tensor_tensor(sring[:, b % 2, c], sring[:, b % 2, c], cols[:, 3:4],
                                                       ps[:, 2 + c, :], ALU.mult, ALU.add)
                    ins.then_inc(s1_done, 1)
                dve.wait_ge(os_ps, head * NS + NS)
                link.link(dve.tensor_copy(o[0:NS, TP], ps[0:NS, 4, :]))
                dve.wait_ge(o_done, head * TP + TP)
                for t, rows in enumerate(ROWS):
                    ins = dve.bn_stats(stats[0:rows, t], o[0:rows, t])
                link.link(ins)
                dve.sem_inc(issued, 1)
                for t, rows in enumerate(ROWS):
                    ins = dve.bn_aggr(meanv[0:rows, t], stats[0:rows, t])
                link.link(ins)
                for a, b, rows in ((0, TP, P), (TP, TILES, NS)):
                    ins = dve.tensor_scalar(var[0:rows, a:b], meanv[0:rows, a:b, 1], EPS, None, ALU.add)
                ins.then_inc(var_done, 1)
                dve.wait_ge(rstd_done, head + 2)
                for t, rows in enumerate(ROWS):
                    dve.tensor_scalar(o[0:rows, t], o[0:rows, t], meanv[0:rows, t, 0:1], rstd[0:rows, t:t + 1],
                                      ALU.subtract, ALU.mult)
                    if t == 0:
                        dve.wait_ge(g_tanh, head * TILES + TILES)
                    ins = dve.scalar_tensor_tensor(sil[0:rows, t], sil[0:rows, t], 1.0, proj[0:rows, t, 2 * BW:3 * BW],
                                                   ALU.add, ALU.mult)
                link.link(ins)
                for t, rows in enumerate(ROWS):
                    dve.scalar_tensor_tensor(o[0:rows, t], sil[0:rows, t], 0.5, o[0:rows, t], ALU.mult, ALU.mult)\
                       .then_inc(og_done, 1)
                for t, rows in enumerate(ROWS):
                    mod = (modp if t < TP else mods)[0:rows, 2]
                    for half in range(2):
                        dve.wait_ge(y_ps, head * 2 * TILES + (2 * t + half + 1))
                        dve.tensor_tensor(cross[0:rows, half], ps[0:rows, (2 * t + half) % 4, :],
                                          mod[:, half * BW:(half + 1) * BW], ALU.mult).then_inc(y_done, 1)
                    dve.wait_ge(y_done, head * 2 * TILES + (2 * t + 2 + 1))
                    xt = x[0:rows, t].rearrange("p (a n) -> p a n", a=2)
                    link.link(dve.tensor_tensor(xt, xt, cross[0:rows], ALU.add))
            link.end(HEADS)
            dve.sem_inc(x_ready, 1)

            def best_of(layer, t):
                rows = slice(0, ROWS[t])
                dve.wait_ge(score_done, 4 * (TILES * layer + t + 1))

                def top(values, found, index, n):
                    for e in range(n):
                        ins = dve.max(found[:, e, 0:8], values[:, e])
                    link.link(ins)
                    for e in range(n):
                        dve.max_index(index[:, e, 0:8], found[:, e, 0:8], values[:, e])
                        ins = dve.match_replace(values[:, e], found[:, e, 0:8], values[:, e], LOWEST)
                    link.link(ins)
                    for e in range(n):
                        ins = dve.max(found[:, e, 8:16], values[:, e])
                    link.link(ins)
                    for e in range(n):
                        ins = dve.max_index(index[:, e, 8:16], found[:, e, 8:16], values[:, e])
                    link.link(ins)

                top(score[rows], best[rows], besti[rows], 2 * PH)
                dve.tensor_copy(bestf[rows], besti[rows])
                by_side = best[rows].rearrange("p (e s) k -> p e s k", s=2)
                link.link(dve.tensor_tensor(cand[rows].rearrange("p e (a b) -> p e a b", a=TOPK),
                                            spread(by_side[:, :, 0], 3, TOPK), spread(by_side[:, :, 1], 2, TOPK), ALU.add))
                top(cand[rows], topv[rows], topi[rows], PH)
                gates = gate[rows, t].rearrange("p (e k) -> p e k", e=PH)
                link.link(dve.tensor_tensor(gates, topv[rows], spread(topv[rows, :, 0], 2, TOPK), ALU.subtract))
                dve.tensor_copy(topv[rows], gates).then_inc(e_sub, 1)
                picked = topi[rows].rearrange("p e k -> p (e k)")
                n1, n2 = picks[rows, 0].bitcast(U32), picks[rows, 1].bitcast(U32)
                f1, f2 = picks[rows, 2], picks[rows, 3]
                dve.tensor_scalar(n1, picked, 4, None, ALU.logical_shift_right)
                link.link(dve.tensor_scalar(n2, picked, TOPK - 1, None, ALU.bitwise_and))
                dve.tensor_copy(f1, n1)
                link.link(dve.tensor_copy(f2, n2))
                keys_of = bestf[rows].rearrange("p (e s) k -> p e s k", s=2)
                hit = cand[rows].rearrange("p e (k a) -> p (e k) a", k=TOPK)
                hit4 = cand[rows].rearrange("p e (k a) -> p e k a", k=TOPK)
                for side, f, out in ((0, f1, side1), (1, f2, side2)):
                    link.link(dve.tensor_tensor(hit, spread(f, 2, TOPK), spread(lane[rows], 1, NE), ALU.is_equal))
                    link.link(dve.tensor_tensor(hit4, hit4, spread(keys_of[:, :, side], 2, TOPK), ALU.mult))
                    link.link(dve.tensor_reduce(out[rows], hit, AX.X, ALU.add))
                link.link(dve.tensor_scalar(side1[rows], side1[rows], float(NK), float(layer * EXPERTS), ALU.mult, ALU.add))
                if t == TP:
                    dve.tensor_tensor(place_s[rows], side1[rows], side2[rows], ALU.add)
                else:
                    link.link(dve.tensor_tensor(place[rows], side1[rows], side2[rows], ALU.add))
                    dve.tensor_copy(eidx[rows, t], place[rows])
                dve.wait_ge(e_exp, TILES * layer + t + 1)
                link.link(dve.tensor_reduce(total[rows], topv[rows], AX.X, ALU.add))
                link.link(dve.reciprocal(rtotal[rows], total[rows]))
                dve.tensor_tensor(gates, topv[rows], spread(rtotal[rows], 2, TOPK), ALU.mult).then_inc(top_done, 1)
                dve.wait_ge(top_done, TILES * layer + t + 1)

            def weights(layer, n, a, a2, gates, out):
                link.link(dve.tensor_tensor(a2, a, a, ALU.mult))
                link.link(dve.tensor_scalar(a2, a2, GELU_A, 1.0, ALU.mult, ALU.add))
                dve.tensor_tensor(a2, a2, a, ALU.mult).then_inc(gelu_in, 1)
                dve.wait_ge(gelu_tanh, n)
                link.link(dve.scalar_tensor_tensor(a2, a2, 1.0, a, ALU.add, ALU.mult))
                dve.scalar_tensor_tensor(out, a2, 0.5, gates, ALU.mult, ALU.mult).then_inc(wgt_done, 1)

            def mixed(layer, t):
                rows = ROWS[t]
                bank = 4 if t == TP else 2 * (t % 2)
                mod = (modp if t < TP else mods)[0:rows, 2]
                link.link(dve.tensor_tensor(gated[0:rows], ps[0:rows, bank:bank + 2, :],
                                            mod.rearrange("p (a n) -> p a n", a=2), ALU.mult))
                dve.sem_inc(mix_free, 1)
                xt = x[0:rows, t].rearrange("p (a n) -> p a n", a=2)
                link.link(dve.tensor_tensor(xt, xt, gated[0:rows], ALU.add))

            def peer(layer):
                k = 2 * layer + 1
                norm(k, PEER_ROOT[layer])
                if layer == 0:
                    dve.wait_ge(key_ld, 48)
                for t in range(TP):
                    best_of(layer, t)
                    if t >= 2:
                        dve.wait_ge(mix_ps, TP * layer + t - 1)
                        mixed(layer, t - 2)
                    with dve.Fori(0, NE // BATCH) as i:
                        link.loop(i, 1)
                        for s in range(BATCH):
                            dve.wait_ge(u_ld[s % RING], i * 32 + landed(layer, t, s // RING))
                            dve.tensor_tensor_reduce(u_ring[:, s % RING], u_ring[:, s % RING], h[:, t], 1.0, 0.0,
                                                     ALU.mult, ALU.add, dots[:, s:s + 1]).then_inc(u_used, 1)
                        dve.wait_ge(u_used, i * BATCH + (gather_of(layer, t) + 2 * BATCH))
                        link.link(dve.tensor_scalar(acts[:, bass.ds(i * BATCH, BATCH)], dots, 1.0, None, ALU.mult))
                    link.end(NE // BATCH)
                    if t >= 2:
                        dve.wait_ge(diag_done, (TP * layer + t - 1) * NE)
                    weights(layer, TILES * layer + t + 1, acts, acts2, gate[:, t], wgt[:, t % 2])
                best_of(layer, TP)
                dve.memset(wgt_s, 0.0).then_inc(wz_zero, 1)
                dve.wait_ge(mix_ps, TP * layer + TP - 1)
                mixed(layer, TP - 2)
                dve.wait_ge(es_ps, layer + 1)
                dve.tensor_copy(eidx_s, ps[:, 6, 0:NS]).then_inc(es_done, 1)
                dve.tensor_copy(gate_s, ps[:, 6, NS:2 * NS]).then_inc(es_done, 1)
                for b in range(NS):
                    dve.wait_ge(hb_ld[b % 2], 16 * (NS // 2 * layer + b // 2 + 1))
                    dve.wait_ge(u_ld[b], landed(layer, TP, 0))
                    dve.tensor_tensor_reduce(u_ring[:, b], u_ring[:, b], hb[:, b % 2], 1.0, 0.0, ALU.mult, ALU.add,
                                             acts_s[:, b:b + 1]).then_inc(u_used, 1)
                dve.wait_ge(es_done, 2 * (layer + 1))
                dve.wait_ge(wz_zero, layer + 1)
                dve.wait_ge(u_used, BATCH + gather_of(layer, TP) + NS)
                weights(layer, TILES * (layer + 1), acts_s, acts_s2, gate_s, wgt_s[:, ::NS + 1])
                dve.wait_ge(mix_ps, TP * (layer + 1))
                mixed(layer, TP - 1)
                dve.wait_ge(v_used, BATCH + gather_of(layer, TP) + NS)
                mixed(layer, TP)
                dve.sem_inc(x_ready, 1)

            peer(0)
            ssm_dve(dve, link, norm)
            peer(1)
            norm(FINAL, NORMS)


_INS = ['x_prompt', 'x_sample', 'c_prompt', 'c_sample', 'state_ret', 'state_ssm_re', 'state_ssm_im', 'norm_g', 'final_g',
        'w_ada', 'b_ada', 'ret_w_in', 'ret_w_out', 'ssm_w_in', 'ssm_lam_re', 'ssm_lam_im', 'ssm_log_dt', 'ssm_b_re',
        'ssm_b_im', 'ssm_c_re', 'ssm_c_im', 'ssm_d', 'ssm_w_glu', 'peer_w_q', 'peer_key1', 'peer_key2', 'peer_u', 'peer_v']
_OUTS = [((1, 512, 1024), 'float32'), ((8, 1, 1024), 'float32'), ((1, 1, 4, 256, 512), 'float32'),
         ((1, 8, 4, 256, 512), 'float32'), ((1, 1, 64, 64), 'float32'), ((1, 1, 64, 64), 'float32'),
         ((1, 8, 64, 64), 'float32'), ((1, 8, 64, 64), 'float32')]


def _tables():
    import numpy as _np
    f = _np.float32
    half = DK // 2
    inv = f(10000.0) ** (-_np.arange(half, dtype=f) / f(half))
    pos = _np.zeros((TILES, P), f)
    pos[:TP] = _np.arange(TP * P, dtype=f).reshape(TP, P)
    pos[TP] = 4096
    angle = (pos[:, :, None] * inv[None, None, :]).astype(f).astype(_np.float64)
    rot = _np.zeros((P, TILES, 2, 2, half), f)
    for n, fn in enumerate((_np.cos, _np.sin)):
        value = fn(angle).astype(f).transpose(1, 0, 2)
        rot[:, :, n, 0] = value
        rot[:, :, n, 1] = value * f(DK ** -0.5)
    lg = _np.log1p(-_np.exp2(-5.0 - _np.arange(HEADS, dtype=_np.float64)))
    i = _np.arange(P, dtype=_np.float64)
    diff = i[None, :] - i[:, None]
    decay = _np.where(diff[:, None, :] >= 0, _np.exp(lg[None, :, None] * _np.maximum(diff, 0)[:, None, :]), 0.0)
    cols = _np.zeros((P, HEADS, 4), _np.float64)
    cols[:, :, 0] = _np.exp(lg[None, :] * (i[:, None] + 1))
    cols[:, :, 1] = _np.exp(lg[None, :] * (P - 1 - i[:, None]))
    cols[:, :, 2] = _np.exp(lg * P)[None, :]
    cols[:, :, 3] = _np.exp(lg)[None, :]
    lane = _np.tile(_np.arange(TOPK, dtype=f), (P, 1))
    return {"rot_tab": rot, "decay_tab": decay.astype(f),
            "decay_cols": cols.astype(f), "lane_tab": lane}


def kernel(**inputs):
    import numpy as _np
    import concourse.bacc as _bacc
    from concourse import mybir as _mybir
    from concourse.bass_utils import run_bass_kernel_spmd as _run

    nc = _bacc.Bacc("TRN2", target_bir_lowering=False, num_devices=1)
    arrays, args = {}, []
    given = {name: _np.ascontiguousarray(inputs[name]) for name in _INS}
    given.update(_tables())
    for name, a in given.items():
        arrays[f"in_{name}_dram"] = a
        args.append(nc.dram_tensor(f"in_{name}_dram", a.shape, _mybir.dt.from_np(a.dtype), kind="ExternalInput").ap())
    for i, (shape, dtype) in enumerate(_OUTS):
        dt = _mybir.dt.from_np(_np.dtype(dtype))
        args.append(nc.dram_tensor(f"out_{i}_dram", shape, dt, kind="ExternalOutput").ap())
    build(nc, *args)
    r = _run(nc, [arrays], core_ids=[0])
    return tuple(r.results[0][f"out_{i}_dram"] for i in range(len(_OUTS)))
```
